# Optimizing a Trainium2 kernel written in Bass

```python
import jax, jax.numpy as jnp
from jax import lax
import numpy as np

D_MODEL = 1024
BATCH = 1
SEQ = 1024
DEPTH = 1
DEC_BATCH = 8
DEC_SEQ = 8
PAST_LEN = 8192
PAGE_SIZE = 128

EPS = 1e-6
MIX_WIDTH = D_MODEL
POOL_WIDTH = MIX_WIDTH // 2
POOL_WINDOWS = (2, 4, 8, 16)
POOL_GROUPS = len(POOL_WINDOWS)
POOL_GROUP = POOL_WIDTH // POOL_GROUPS
POOL_MAX_WIN = max(POOL_WINDOWS)
GLA_HEADS = 4
GLA_V_WIDTH = MIX_WIDTH - POOL_WIDTH
GLA_QK_WIDTH = GLA_V_WIDTH // 2
GLA_DK = GLA_QK_WIDTH // GLA_HEADS
GLA_DV = GLA_V_WIDTH // GLA_HEADS
GLA_LOWRANK = 16
GLA_GATE_NORM = 16.0
GLA_CHUNK = 32
IN_WIDTH = POOL_WIDTH + 2 * GLA_QK_WIDTH + 2 * GLA_V_WIDTH + GLA_LOWRANK
N_EXPERT_GROUPS = 4
EXPERTS_PER_GROUP = 4
N_EXPERTS = N_EXPERT_GROUPS * EXPERTS_PER_GROUP
EXPERT_TOP_K = 2
D_EXPERT = D_MODEL // 2

kernel_name = "hymba_pool_gla_hiermoe_step"

def rmsnorm(x, g):
    xf = x.astype(jnp.float32)
    y = xf * lax.rsqrt(jnp.mean(xf * xf, axis=-1, keepdims=True) + EPS)
    return (y * g.astype(jnp.float32)).astype(x.dtype)

def pool_mixer(u, hist, start_pos, w_pool, pool_scale):
    B, T, _ = u.shape
    L = POOL_MAX_WIN - 1
    full = jnp.concatenate([hist.astype(u.dtype), u], axis=1).astype(jnp.float32)
    cs = jnp.concatenate([jnp.zeros((B, 1, POOL_WIDTH), jnp.float32),
                          jnp.cumsum(full, axis=1)], axis=1)
    pos = start_pos + jnp.arange(T)
    end = cs[:, L + 1:]
    cur = full[:, L:]
    outs = []
    for gi, w in enumerate(POOL_WINDOWS):
        sl = slice(gi * POOL_GROUP, (gi + 1) * POOL_GROUP)
        begin = cs[:, L + 1 - w: L + 1 - w + T, sl]
        cnt = jnp.minimum(pos + 1, w).astype(jnp.float32)[None, :, None]
        outs.append((end[..., sl] - begin) / cnt - cur[..., sl])
    pooled = jnp.stack(outs, axis=2)
    mixed = jnp.einsum('btgc,gcd->btgd', pooled, w_pool.astype(jnp.float32)).reshape(B, T, POOL_WIDTH)
    out = mixed * pool_scale.astype(jnp.float32)
    return out.astype(u.dtype), full[:, -L:].astype(u.dtype)

def gla_chunked(q, k, v, logf, S0):
    B, T, H, DK = q.shape
    DV = v.shape[-1]
    C = min(GLA_CHUNK, T)
    pad = (-T) % C
    if pad:
        pw = ((0, 0), (0, pad), (0, 0), (0, 0))
        q, k, v, logf = (jnp.pad(a, pw) for a in (q, k, v, logf))
    n = (T + pad) // C

    def to_chunks(a):
        return a.reshape(B, n, C, H, a.shape[-1]).transpose(1, 0, 3, 2, 4)

    qc, kc, vc, fc = to_chunks(q), to_chunks(k), to_chunks(v), to_chunks(logf)
    bc = jnp.cumsum(fc, axis=3)
    causal = jnp.tril(jnp.ones((C, C), dtype=bool))

    def step(S, inp):
        qi, ki, vi, bi = inp
        inter = jnp.einsum('bhtk,bhkv->bhtv', qi * jnp.exp(bi), S)
        diff = bi[:, :, :, None, :] - bi[:, :, None, :, :]
        decay = jnp.exp(jnp.where(causal[:, :, None], diff, -jnp.inf))
        scores = jnp.einsum('bhtk,bhsk,bhtsk->bhts', qi, ki, decay)
        intra = jnp.einsum('bhts,bhsv->bhtv', scores, vi)
        b_last = bi[:, :, -1:, :]
        S_new = jnp.exp(b_last[:, :, 0, :])[..., None] * S + jnp.einsum(
            'bhsk,bhsv->bhkv', ki * jnp.exp(b_last - bi), vi)
        return S_new, inter + intra

    S, o = lax.scan(step, S0, (qc, kc, vc, bc))
    o = o.transpose(1, 0, 3, 2, 4).reshape(B, n * C, H, DV)[:, :T]
    return o, S

def gla_mixer(q, k, v, g, gk_lr, S0, w_gk2, b_gk, gla_norm_g):
    B, T, _ = q.shape
    f32 = jnp.float32
    qh = q.astype(f32).reshape(B, T, GLA_HEADS, GLA_DK) * (GLA_DK ** -0.5)
    kh = k.astype(f32).reshape(B, T, GLA_HEADS, GLA_DK)
    vh = v.astype(f32).reshape(B, T, GLA_HEADS, GLA_DV)
    logf = jax.nn.log_sigmoid(gk_lr.astype(f32) @ w_gk2.astype(f32) + b_gk.astype(f32)) / GLA_GATE_NORM
    logf = logf.reshape(B, T, GLA_HEADS, GLA_DK)
    o, S = gla_chunked(qh, kh, vh, logf, S0.astype(f32))
    o = o * lax.rsqrt(jnp.mean(o * o, axis=-1, keepdims=True) + EPS) * gla_norm_g.astype(f32)
    o = o * jax.nn.silu(g.astype(f32).reshape(B, T, GLA_HEADS, GLA_DV))
    return o.reshape(B, T, GLA_V_WIDTH).astype(q.dtype), S.astype(q.dtype)

def hier_moe(h, w_rg, b_rg, w_re, b_re, w_gate, w_up, w_down):
    B, T, D = h.shape
    x = h.reshape(-1, D)
    N = x.shape[0]
    gprob = jax.nn.softmax((x @ w_rg + b_rg).astype(jnp.float32), axis=-1)
    gp, gidx = lax.top_k(gprob, 1)
    elog = (x @ w_re + b_re).astype(jnp.float32).reshape(N, N_EXPERT_GROUPS, EXPERTS_PER_GROUP)
    elog_sel = jnp.take_along_axis(elog, gidx[:, :, None], axis=1)[:, 0]
    ep, eidx = lax.top_k(jax.nn.softmax(elog_sel, axis=-1), EXPERT_TOP_K)
    ep = ep / jnp.sum(ep, axis=-1, keepdims=True)
    weights = gp * ep
    expert_id = gidx * EXPERTS_PER_GROUP + eidx
    combine = jnp.sum(jax.nn.one_hot(expert_id, N_EXPERTS, dtype=jnp.float32) * weights[..., None], axis=1)

    def body(acc, params):
        wg, wu, wd, c = params
        y = (jax.nn.silu(x @ wg) * (x @ wu)) @ wd
        return acc + c[:, None] * y.astype(jnp.float32), None

    acc, _ = lax.scan(body, jnp.zeros((N, D), jnp.float32), (w_gate, w_up, w_down, combine.T))
    return acc.astype(h.dtype).reshape(B, T, D)

def trunk_layer(x, hist_pool, S0, start_pos, norm1_g, w_in, w_gk2, b_gk, w_pool, pool_scale,
                gla_norm_g, w_out, norm2_g, w_router_group, b_router_group, w_router_expert,
                b_router_expert, w_gate, w_up, w_down):
    h = rmsnorm(x, norm1_g)
    proj = h @ w_in
    cuts = np.cumsum([POOL_WIDTH, GLA_QK_WIDTH, GLA_QK_WIDTH, GLA_V_WIDTH, GLA_V_WIDTH]).tolist()
    u, q, k, v, g, gk_lr = jnp.split(proj, cuts, axis=-1)
    a, new_pool = pool_mixer(u, hist_pool, start_pos, w_pool, pool_scale)
    b, new_S = gla_mixer(q, k, v, g, gk_lr, S0, w_gk2, b_gk, gla_norm_g)
    x = x + jnp.concatenate([a, b], axis=-1) @ w_out
    x = x + hier_moe(rmsnorm(x, norm2_g), w_router_group, b_router_group, w_router_expert,
                     b_router_expert, w_gate, w_up, w_down)
    return x, new_pool, new_S

def setup_inputs(seed: int = 0) -> dict:
    key = jax.random.key(seed)
    ks = jax.random.split(key, 24)
    f32 = jnp.float32

    def nrm(k, shape, scale):
        return jax.random.normal(k, shape, f32) * scale

    return {
        "x_prompt": nrm(ks[0], (BATCH, SEQ, D_MODEL), 1.0),
        "x_sample": nrm(ks[1], (DEC_BATCH, DEC_SEQ, D_MODEL), 1.0),
        "state_pool": nrm(ks[2], (DEPTH, DEC_BATCH, POOL_MAX_WIN - 1, POOL_WIDTH), 1.0),
        "state_gla": nrm(ks[3], (DEPTH, DEC_BATCH, GLA_HEADS, GLA_DK, GLA_DV), 0.5),
        "norm1_g": 1.0 + nrm(ks[4], (DEPTH, D_MODEL), 0.05),
        "w_in": nrm(ks[5], (DEPTH, D_MODEL, IN_WIDTH), D_MODEL ** -0.5),
        "w_gk2": nrm(ks[6], (DEPTH, GLA_LOWRANK, GLA_QK_WIDTH), GLA_LOWRANK ** -0.5),
        "b_gk": nrm(ks[7], (DEPTH, GLA_QK_WIDTH), 0.1),
        "w_pool": nrm(ks[8], (DEPTH, POOL_GROUPS, POOL_GROUP, POOL_GROUP), POOL_GROUP ** -0.5),
        "pool_scale": 1.0 + nrm(ks[9], (DEPTH, POOL_WIDTH), 0.1),
        "gla_norm_g": 1.0 + nrm(ks[10], (DEPTH, GLA_DV), 0.05),
        "w_out": nrm(ks[11], (DEPTH, MIX_WIDTH, D_MODEL), MIX_WIDTH ** -0.5),
        "norm2_g": 1.0 + nrm(ks[12], (DEPTH, D_MODEL), 0.05),
        "w_router_group": nrm(ks[13], (DEPTH, D_MODEL, N_EXPERT_GROUPS), D_MODEL ** -0.5),
        "b_router_group": nrm(ks[14], (DEPTH, N_EXPERT_GROUPS), 0.01),
        "w_router_expert": nrm(ks[15], (DEPTH, D_MODEL, N_EXPERTS), D_MODEL ** -0.5),
        "b_router_expert": nrm(ks[16], (DEPTH, N_EXPERTS), 0.01),
        "w_gate": nrm(ks[17], (DEPTH, N_EXPERTS, D_MODEL, D_EXPERT), D_MODEL ** -0.5),
        "w_up": nrm(ks[18], (DEPTH, N_EXPERTS, D_MODEL, D_EXPERT), D_MODEL ** -0.5),
        "w_down": nrm(ks[19], (DEPTH, N_EXPERTS, D_EXPERT, D_MODEL), D_EXPERT ** -0.5),
        "final_g": 1.0 + nrm(ks[20], (D_MODEL,), 0.05),
    }

def reference(x_prompt, x_sample, state_pool, state_gla, norm1_g, w_in, w_gk2, b_gk, w_pool,
              pool_scale, gla_norm_g, w_out, norm2_g, w_router_group, b_router_group,
              w_router_expert, b_router_expert, w_gate, w_up, w_down, final_g):
    xp, xs = x_prompt, x_sample
    Bp = x_prompt.shape[0]
    pool_p, gla_p, pool_s, gla_s = [], [], [], []
    for l in range(DEPTH):
        weights = (norm1_g[l], w_in[l], w_gk2[l], b_gk[l], w_pool[l], pool_scale[l], gla_norm_g[l],
                   w_out[l], norm2_g[l], w_router_group[l], b_router_group[l], w_router_expert[l],
                   b_router_expert[l], w_gate[l], w_up[l], w_down[l])
        hist0 = jnp.zeros((Bp, POOL_MAX_WIN - 1, POOL_WIDTH), x_prompt.dtype)
        S0 = jnp.zeros((Bp, GLA_HEADS, GLA_DK, GLA_DV), x_prompt.dtype)
        xp, npool, ngla = trunk_layer(xp, hist0, S0, 0, *weights)
        pool_p.append(npool)
        gla_p.append(ngla)
        xs, npool_s, ngla_s = trunk_layer(xs, state_pool[l], state_gla[l], PAST_LEN, *weights)
        pool_s.append(npool_s)
        gla_s.append(ngla_s)
    y_prompt = rmsnorm(xp, final_g)
    y_sample = rmsnorm(xs, final_g)
    return (y_prompt, y_sample, jnp.stack(pool_p), jnp.stack(gla_p), jnp.stack(pool_s), jnp.stack(gla_s))


_drawn_inputs = setup_inputs


def setup_inputs(seed=0):
    import zlib

    import numpy as np

    out = dict(_drawn_inputs(seed))
    spreads = {}
    factors = {'b_router_group': 3.231, 'b_router_expert': 7.606}
    for name, (base, spread) in spreads.items():
        noise = np.random.default_rng([zlib.crc32(name.encode()), seed]).standard_normal(out[name].shape)
        drawn = base * np.exp(spread * noise) if base else spread * noise
        out[name] = __import__('jax').numpy.asarray(drawn.astype(out[name].dtype))
    for name, factor in factors.items():
        out[name] = (out[name] * factor).astype(out[name].dtype)
    return out
```

```python
from contextlib import ExitStack

import concourse.bass as bass
from concourse import mybir
from concourse.alu_op_type import AluOpType as ALU

F32 = mybir.dt.float32
F32R = mybir.dt.float32r
BF16 = mybir.dt.bfloat16
FP16 = mybir.dt.float16
I32 = mybir.dt.int32
ACT = mybir.ActivationFunctionType
AX = mybir.AxisListType

P = 128
D = 1024
KC = D // P
SEQ = 1024
DEC_B, DEC_T = 8, 8
NS = DEC_B * DEC_T
N = SEQ + NS
TT = 9
ROWS = [P] * (TT - 1) + [NS]
BLK = [(0, 384), (384, 384), (768, 320)]
PW = 512
PG = 4
WINDOWS = (2, 4, 8, 16)
HIST = 15
U_P = 16
U_S = U_P + SEQ
SEG = HIST + DEC_T
U_W = U_S + DEC_B * SEG
HEADS = 4
DK, DV = 64, 128
LR = 16
NG, NE = 4, 16
DE = 512
EPS = 1e-6
GATE = 16.0
CLAMP = 80.0 * GATE
SB = 32

W = 160
W2 = W - P
ROUNDS = -(-N // W)
WREST = 4


def program(nc, A, O):
    C_U, C_Q, C_K, C_V, C_G, C_L = 0, 512, 768, 1024, 1536, 2048
    w_in = A["w_in"].rearrange("l (k p) n -> p (l k) n", p=P)
    w_out = A["w_out"].rearrange("l (k p) n -> p (l k) n", p=P)
    x_rows = [A["x_prompt"][0, i * P:(i + 1) * P, :] for i in range(TT - 1)]
    x_rows.append(A["x_sample"].rearrange("a t d -> (a t) d"))
    h2_dram = nc.dram_tensor("h2_rows", [N, D], F32).ap()
    y_dram = nc.dram_tensor("expert_rows", [N * 2, D], F32).ap()

    with ExitStack() as whole:
        def sb(name, shape, dt=F32, ctx=whole):
            return ctx.enter_context(nc.sbuf_tensor(name, shape, dt))

        def sem(name):
            return whole.enter_context(nc.semaphore(name))

        bank = [whole.enter_context(nc.psum_tensor(f"bank{i}", [P, 512], F32)) for i in range(8)]

        ident = sb("ident", [P, P])
        onesf = sb("onesf", [P, P])
        eps_c = sb("eps_c", [P, 1])

        c12 = whole.enter_context(ExitStack())
        uT = sb("uT", [P, PG, U_W], ctx=c12)
        gT = sb("gT", [P, HEADS, N], ctx=c12)
        ring = sb("ring", [P, 4, KC, 256], ctx=c12)

        b1_all(nc, A, O, whole, c12, sb, sem, bank, ident, onesf, eps_c, uT, gT, ring, w_in, w_out, x_rows,
               (C_U, C_Q, C_K, C_V, C_G, C_L))

        w1 = sb("w1", [P, TT])
        w2 = sb("w2", [P, TT])
        rank_m = sb("rank_m", [P, NE * TT])
        token = sb("token", [P, TT, 2], FP16)
        expert = sb("expert", [P, NE])
        iota_w = sb("iota_w", [P, W])
        steps = sb("steps", [1, 1], I32)
        x1 = sb("x1", [P, TT, D])
        b2_all(nc, A, sb, sem, bank, ident, onesf, eps_c, uT, gT, ring, x1, x_rows, h2_dram,
               w1, w2, rank_m, token, expert, iota_w, steps)
        b3_all(nc, A, sb, sem, bank, ident, h2_dram, y_dram, rank_m, token, expert, iota_w, steps)
        b4_all(nc, A, O, sb, sem, bank, eps_c, x1, y_dram, w1, w2)


def b1_all(nc, A, O, whole, c12, sb, sem, bank, ident, onesf, eps_c, uT, gT, ring, w_in, w_out, x_rows, cols):
    C_U, C_Q, C_K, C_V, C_G, C_L = cols
    c1 = ExitStack()
    hT = sb("hT", [P, KC, N], ctx=c1)
    qT = sb("qT", [P, 2, N], ctx=c1)
    kT = sb("kT", [P, 2, N], ctx=c1)
    bT = sb("bT", [P, 2, N], ctx=c1)
    v = sb("v", [P, TT, 512], ctx=c1)
    lrT = sb("lrT", [LR, N], ctx=c1)
    xs = sb("xs", [P, 3, D], ctx=c1)
    xn = sb("xn", [P, 2, D], ctx=c1)
    ssq = sb("ssq", [P, TT], ctx=c1)
    rstd = sb("rstd", [P, 2 * TT], ctx=c1)
    g1b = sb("g1b", [P, D], ctx=c1)
    wlr = sb("wlr", [P, KC, LR], ctx=c1)
    wgk2 = sb("wgk2", [LR, 256], ctx=c1)
    bgk = sb("bgk", [P, 2], ctx=c1)
    pscale = sb("pscale", [P, PG], ctx=c1)
    gnorm = sb("gnorm", [P, 1], ctx=c1)
    wpool = sb("wpool", [P, PG, P], ctx=c1)
    S0 = sb("S0", [P, DEC_B, 2, DV], ctx=c1)
    Sp = sb("Sp", [P, 2, DV], ctx=c1)
    tmpa = sb("tmpa", [P, N], ctx=c1)
    T1 = sb("T1", [P, 3, 2, P], ctx=c1)
    T2 = sb("T2", [P, 2, 4, P], ctx=c1)
    khN = sb("khN", [P, 2, P], ctx=c1)
    Pm = sb("Pm", [P, HEADS, P], ctx=c1)
    o2 = sb("o2", [P, 512], ctx=c1)
    hist = o2[0:DEC_B * HIST, :]
    qz = xn[:, 0, :].rearrange("p (w h t) -> p w h t", w=2, h=HEADS)
    KM = xn[0:NS, :, :].rearrange("p a (b d) -> p (a b) d", d=256)
    rs = sb("rs", [P, 512], ctx=c1)
    rmid = sb("rmid", [P, 2, SEQ // SB], ctx=c1)
    mask_p = sb("mask_p", [P, P], ctx=c1)
    mask_s = sb("mask_s", [NS, NS], ctx=c1)
    bmask = sb("bmask", [NS, DEC_B], ctx=c1)
    resets = sb("resets", [P, NS], ctx=c1)
    onesN = sb("onesN", [P, P], ctx=c1)
    icnt = sb("icnt", [P, 16], ctx=c1)
    sdec = sb("sdec", [P, 2], ctx=c1)
    o_dec = sb("o_dec", [P, 2, DEC_B], ctx=c1)
    npS = g1b[0:NS, 0:512]
    npP = g1b[0:HIST, 512:1024]
    wsum = xs

    s_const = sem("s_const")
    s_x = [sem(f"s_x{j}") for j in range(3)]
    s_g1 = sem("s_g1")
    s_ku = sem("s_ku")
    s_ssq, s_rt, s_rstd, s_xn = sem("s_ssq"), sem("s_rt"), sem("s_rstd"), sem("s_xn")
    s_tr, s_trev = sem("s_tr"), sem("s_trev")
    s_w = [sem(f"s_w{j}") for j in range(4)]
    s_wlr = sem("s_wlr")
    s_grp = sem("s_grp")
    s_eva, s_evd = sem("s_eva"), sem("s_evd")
    s_gc = sem("s_gc")
    s_hist, s_histev = sem("s_hist"), sem("s_histev")
    s_za, s_b = sem("s_za"), sem("s_b")
    s_d = sem("s_d")
    s_args, s_exp, s_kq, s_score = sem("s_args"), sem("s_exp"), sem("s_kq"), sem("s_score")
    s_khn, s_pm, s_o, s_sq, s_ms, s_rs, s_on, s_st = [sem(x) for x in (
        "s_khn", "s_pm", "s_o", "s_sq", "s_ms", "s_rs", "s_on", "s_st")]
    s_pool, s_pmix = sem("s_pool"), sem("s_pmix")
    s_np, s_npev, s_npo = sem("s_np"), sem("s_npev"), sem("s_npo")
    s_km, s_us = sem("s_km"), sem("s_us")
    s_s0, s_silu, s_fin = sem("s_s0"), sem("s_silu"), sem("s_fin")
    s_a = sem("s_a")

    NCONST = 16
    groups = [("lr", 0, b) for b in range(3)] + [("z", p, b) for p in range(2) for b in range(3)]
    groups += [("k", p, b) for p in range(2) for b in range(3)] + [("q", p, b) for p in range(2) for b in range(3)]
    groups += [("v", 0, t) for t in range(TT)]
    ug = [("u", m, b) for m in range(4) for b in range(3)] + [("g", m, b) for m in range(4) for b in range(3)]
    groups += ug + [("mix", m, b) for m in range(4) for b in range(3)]
    index = {g: n for n, g in enumerate(groups)}
    ON_ACT = {"lr", "k", "q", "u", "mix"}
    unit = {"k": 0, "q": 1, "v": 2, "u": 4, "g": 6}

    def evacs(n, on_act):
        return sum((g[0] in ON_ACT) == on_act for g in groups[:n + 1])

    def out_sem(n):
        on_act = groups[n][0] in ON_ACT
        return (s_eva if on_act else s_evd), evacs(n, on_act)

    def acc(n):
        return bank[5 + n % 3]

    def pooled(m):
        return wsum[:, :, :].rearrange("p a b -> p (a b)")[:, (m % 2) * 1536:(m % 2) * 1536 + N]

    block = ExitStack()
    blk = block.enter_context(nc.Block())

    @blk.gpsimd
    def _(pool):
        nc.gpsimd.memset(ident[:], 0.0).then_inc(s_gc, 1)
        nc.gpsimd.memset(mask_p[:], 1.0).then_inc(s_gc, 1)
        nc.gpsimd.memset(mask_s[:], 1.0).then_inc(s_gc, 1)
        nc.gpsimd.memset(bmask[:], 1.0).then_inc(s_gc, 1)
        nc.gpsimd.memset(resets[:], 1.0).then_inc(s_gc, 1)
        nc.gpsimd.memset(onesf[:], 1.0).then_inc(s_gc, 1)
        nc.gpsimd.memset(onesN[:], 1.0 / DV).then_inc(s_gc, 1)
        nc.gpsimd.memset(eps_c[:], EPS).then_inc(s_gc, 1)
        nc.gpsimd.memset(Pm[:], 0.0).then_inc(s_gc, 1)
        nc.gpsimd.memset(uT[:, :, 0:U_P], 0.0).then_inc(s_gc, 1)
        nc.gpsimd.iota(icnt[:], [[1, 16]], base=1, channel_multiplier=0,
                       allow_small_or_imprecise_dtypes=True).then_inc(s_gc, 1)
        pool.wait_ge(s_gc, 11)
        nc.gpsimd.affine_select(out=ident[:], in_=ident[:], pattern=[[-1, P]], compare_op=ALU.not_equal, fill=1.0,
                                base=0, channel_multiplier=1).then_inc(s_gc, 1)
        nc.gpsimd.affine_select(out=mask_p[:], in_=mask_p[:], pattern=[[1, P]], compare_op=ALU.is_ge, fill=0.0,
                                base=0, channel_multiplier=-1).then_inc(s_gc, 1)
        nc.gpsimd.affine_select(out=mask_s[:], in_=mask_s[:], pattern=[[1, NS]], compare_op=ALU.is_ge, fill=0.0,
                                base=0, channel_multiplier=-1).then_inc(s_gc, 1)
        nc.gpsimd.affine_select(out=bmask[:], in_=bmask[:], pattern=[[-DEC_T, DEC_B]], compare_op=ALU.is_ge,
                                fill=0.0, base=0, channel_multiplier=1).then_inc(s_gc, 1)
        nc.gpsimd.memset(resets[:].rearrange("p (b t) -> p b t", t=DEC_T)[:, :, 0:1], 0.0).then_inc(s_gc, 1)
        pool.wait_ge(s_gc, 16)
        nc.gpsimd.affine_select(out=bmask[:], in_=bmask[:], pattern=[[DEC_T, DEC_B]], compare_op=ALU.is_ge,
                                fill=0.0, base=DEC_T - 1, channel_multiplier=-1).then_inc(s_gc, 1)
        nc.gpsimd.affine_select(out=mask_s[:].rearrange("s (b t) -> s b t", t=DEC_T),
                                in_=mask_s[:].rearrange("s (b t) -> s b t", t=DEC_T),
                                pattern=[[-DEC_T, DEC_B], [0, DEC_T]], compare_op=ALU.is_ge, fill=0.0, base=0,
                                channel_multiplier=1).then_inc(s_gc, 1)
    GC = 18

    @blk.sync
    def _(sp):
        def load_x(i):
            if i >= 3:
                sp.wait_ge(s_xn, i - 2)
            sp.dma_start(xs[0:ROWS[i], i % 3, :], x_rows[i]).then_inc(s_x[i % 3], 16)

        def load_unit(n, src):
            sp.dma_start(ring[:, n % 4, :, :], src).then_inc(s_w[n % 4], 16)

        load_x(0)
        sp.dma_start(g1b[:], A["norm1_g"].broadcast_to([P, D])).then_inc(s_g1, 16)
        load_x(1)
        load_x(2)
        with nc.allow_non_contiguous_dma(reason="small vectors, one value a partition"):
            sp.dma_start(bgk[:], A["b_gk"].rearrange("l (a p) -> p (l a)", p=P)).then_inc(s_const, 16)
            sp.dma_start(pscale[:], A["pool_scale"].rearrange("l (a p) -> p (l a)", p=P)).then_inc(s_const, 16)
            sp.dma_start(gnorm[:], A["gla_norm_g"].rearrange("l p -> p l")).then_inc(s_const, 16)
        sp.dma_start(wgk2[:], A["w_gk2"][0]).then_inc(s_const, 16)
        sp.dma_start(wpool[:], A["w_pool"][0].rearrange("g c d -> c g d")).then_inc(s_const, 16)
        sp.dma_start(hist, A["state_pool"][0].rearrange("b t c -> (b t) c")).then_inc(s_const, 16)
        sp.dma_start(wlr[:], w_in[:, :, C_L:C_L + LR]).then_inc(s_wlr, 16)
        for a in range(2):
            sp.dma_start(S0[64 * a:64 * a + 64, :, :, :],
                         A["state_gla"][0].rearrange("b (p a) k v -> a k b p v", a=2)[a]).then_inc(s_const, 16)
        units = [C_K, C_Q, C_V, C_V + 256, C_U, C_U + 256, C_G, C_G + 256]
        load_unit(0, w_in[:, :, units[0]:units[0] + 256])
        for i in range(3, TT):
            load_x(i)
            if i < 6:
                load_unit(i - 2, w_in[:, :, units[i - 2]:units[i - 2] + 256])
        for b in range(DEC_B):
            sp.dma_start(O[4][0, b, 0:HIST - DEC_T, :], A["state_pool"][0, b, DEC_T:HIST, :]).then_inc(s_npo, 16)
        last = [index[("k", 1, 2)], index[("q", 1, 2)], index[("v", 0, 8)], index[("v", 0, 8)],
                index[("u", 1, 2)], index[("u", 3, 2)], index[("g", 1, 2)], index[("g", 3, 2)]]
        for n in range(4, 12):
            sp.wait_ge(s_grp, last[n - 4] + 1)
            if n < 8:
                load_unit(n, w_in[:, :, units[n]:units[n] + 256])
            else:
                load_unit(n, w_out[:, :, (n - 8) * 256:(n - 7) * 256])
        sp.wait_ge(s_npev, 1)
        sp.dma_start(O[2][0, 0], npP).then_inc(s_npo, 16)
        for b in range(DEC_B):
            sp.dma_start(O[4][0, b, HIST - DEC_T:HIST, :], npS[b * DEC_T:(b + 1) * DEC_T, :]).then_inc(s_npo, 16)
        sp.wait_ge(s_st, TT - 1)
        sp.wait_ge(s_us, DEC_B)
        for a in range(2):
            sp.dma_start(O[3][0, 0].rearrange("(p a) k v -> a k p v", a=2)[a],
                         Sp[64 * a:64 * a + 64, :, :]).then_inc(s_npo, 16)
            sp.dma_start(O[5][0].rearrange("b (p a) k v -> a k b p v", a=2)[a],
                         S0[64 * a:64 * a + 64, :, :, :]).then_inc(s_npo, 16)
        sp.wait_ge(s_npo, 16 * (2 * DEC_B + 1 + 4))

    @blk.tensor
    def _(pe):
        pe.wait_ge(s_gc, GC)
        for i in range(TT):
            r = ROWS[i]
            pe.wait_ge(s_xn, i + 1)
            for h in range(2):
                if i >= 2:
                    pe.wait_ge(s_trev, 2 * (i - 2) + h + 1)
                for k in range(4):
                    t = nc.tensor.transpose(bank[2 * (i % 2) + h][:, k * P:k * P + r],
                                            xn[0:r, i % 2, (4 * h + k) * P:(4 * h + k + 1) * P], ident[0:r, 0:r])
                t.then_inc(s_tr, 1)

        def group(kind, m, b):
            n = index[(kind, m, b)]
            if n >= 3:
                s, c = out_sem(n - 3)
                pe.wait_ge(s, c)
            if kind in unit:
                u = unit[kind] + (0 if kind in "kqv" else m // 2)
                pe.wait_ge(s_w[u % 4], 16 * (u // 4 + 1))
                if kind == "v":
                    pe.wait_ge(s_w[3], 16)
            if kind == "lr":
                t0, tn = BLK[b]
                for k in range(KC):
                    mm = nc.tensor.matmul(acc(n)[0:LR, 0:tn], wlr[:, k, :], hT[:, k, t0:t0 + tn],
                                          start=k == 0, stop=k == KC - 1)
            elif kind == "z":
                t0, tn = BLK[b]
                mm = nc.tensor.matmul(acc(n)[:, 0:tn], wgk2[:, m * P:(m + 1) * P], lrT[:, t0:t0 + tn],
                                      start=True, stop=True)
            elif kind == "mix":
                t0, tn = BLK[b]
                mm = nc.tensor.matmul(acc(n)[:, 0:tn], wpool[:, m, :], pooled(m)[:, t0:t0 + tn],
                                      start=True, stop=True)
            elif kind == "v":
                r = ROWS[b]
                for k in range(KC):
                    mm = nc.tensor.matmul(acc(n)[0:r, :], hT[:, k, b * P:b * P + r], ring[:, 2:4, k, :],
                                          start=k == 0, stop=k == KC - 1)
            else:
                t0, tn = BLK[b]
                c0 = (m % 2) * P
                for k in range(KC):
                    mm = nc.tensor.matmul(acc(n)[:, 0:tn], ring[:, u % 4, k, c0:c0 + P], hT[:, k, t0:t0 + tn],
                                          start=k == 0, stop=k == KC - 1)
            mm.then_inc(s_grp, 1)

        pe.wait_ge(s_trev, 2 * TT)
        pe.wait_ge(s_wlr, 16)
        for b in range(3):
            group("lr", 0, b)
        pe.wait_ge(s_const, 16 * 8)
        for m in range(PG):
            t = nc.tensor.transpose(bank[0][:, m * P:m * P + DEC_B * HIST], hist[:, m * P:(m + 1) * P],
                                    ident[0:DEC_B * HIST, 0:DEC_B * HIST])
        t.then_inc(s_hist, 1)
        pe.wait_ge(s_eva, 3)
        for m in range(2):
            for b in range(3):
                group("z", m, b)
        for kind in "kq":
            for m in range(2):
                for b in range(3):
                    group(kind, m, b)
        for t in range(TT):
            group("v", 0, t)

        def attend_scores(c):
            n = ROWS[c]
            if c >= 1:
                pe.wait_ge(s_pm, c)
                pe.wait_ge(s_khn, c)
            else:
                pe.wait_ge(s_histev, 1)
            pe.wait_ge(s_kq, c + 1)
            for h in range(HEADS):
                p = h // 2
                if c < TT - 1:
                    for i in range(4):
                        m = SB * (i + 1)
                        nc.tensor.matmul(bank[0][0:m, h * P + SB * i:h * P + SB * (i + 1)], T2[:, p, i, 0:m],
                                         qz[:, 0, h, SB * i:SB * (i + 1)], start=True, stop=True)
                else:
                    nc.tensor.matmul(bank[0][0:n, h * P:h * P + n], T2[:, p, 0, 0:n], qz[:, 0, h, 0:n],
                                     start=True, stop=True)
            for p in range(2):
                t = nc.tensor.transpose(bank[1][0:n, p * P:(p + 1) * P], T1[:, 2, p, 0:n], ident[:])
            t.then_inc(s_score, 1)

        def attend_out(c):
            n = ROWS[c]
            pe.wait_ge(s_pm, c + 1)
            pe.wait_ge(s_khn, c + 1)
            if c >= 1:
                pe.wait_ge(s_st, c)
                pe.wait_ge(s_on, c)
            for h in range(HEADS):
                p = h // 2
                o = nc.tensor.matmul(bank[2][:, h * P:h * P + n], v[0:n, c, h * DV:(h + 1) * DV], Pm[0:n, h, 0:n],
                                     start=True, stop=c == 0, skip_group_check=c == TT - 1)
                if c < TT - 1:
                    if c > 0:
                        o = nc.tensor.matmul(bank[2][:, h * P:h * P + n], Sp[:, p, :], qz[:, 1, h, 0:n],
                                             start=False, stop=True)
                else:
                    for b in range(DEC_B):
                        t0 = b * DEC_T
                        o = nc.tensor.matmul(bank[2][:, h * P + t0:h * P + t0 + DEC_T], S0[:, b, p, :],
                                             qz[:, 1, h, t0:t0 + DEC_T], start=False, stop=True,
                                             skip_group_check=True)
            if c < TT - 1:
                for p in range(2):
                    o = nc.tensor.matmul(bank[3][:, p * 256:(p + 1) * 256], khN[:, p, :],
                                         v[:, c, p * 256:(p + 1) * 256], start=True, stop=True)
            o.then_inc(s_o, 1)

        def attend_norm(c):
            n = ROWS[c]
            pe.wait_ge(s_sq, c + 1)
            if c >= 1:
                pe.wait_ge(s_rs, c)
            nc.tensor.matmul(bank[4][:, :], onesN[:], o2[:], start=True,
                             stop=True).then_inc(s_ms, 1)

        for c in range(TT - 1):
            group(*ug[3 * c])
            attend_scores(c)
            group(*ug[3 * c + 1])
            attend_out(c)
            group(*ug[3 * c + 2])
            attend_norm(c)
        pe.wait_ge(s_eva, evacs(index[("u", 3, 2)], True))
        pe.wait_ge(s_pm, TT - 1)
        pe.wait_ge(s_khn, TT - 1)
        for m in range(PG):
            nc.tensor.transpose(bank[0][0:HIST, m * P:(m + 1) * P], uT[:, m, U_S - HIST:U_S], ident[:])
            t = nc.tensor.transpose(bank[1][0:NS, m * P:(m + 1) * P], tmpa[:, m * NS:(m + 1) * NS], ident[:])
        t.then_inc(s_np, 1)
        for m in range(PG):
            pe.wait_ge(s_pool, m + 1)
            for b in range(3):
                group("mix", m, b)
        pe.wait_ge(s_npev, 1)
        attend_scores(TT - 1)
        attend_out(TT - 1)
        attend_norm(TT - 1)
        pe.wait_ge(s_km, 1)
        for b in range(DEC_B):
            if b >= 2:
                pe.wait_ge(s_us, b - 1)
            for p in range(2):
                t = nc.tensor.matmul(bank[[0, 3][b % 2]][:, p * 256:(p + 1) * 256], KM[:, b, p * P:(p + 1) * P],
                                     v[0:NS, TT - 1, p * 256:(p + 1) * 256], start=True, stop=True)
            t.then_inc(s_ku, 1)

    @blk.scalar
    def _(act):
        act.wait_ge(s_gc, GC)
        for i in range(TT):
            r = ROWS[i]
            act.wait_ge(s_x[i % 3], 16 * (i // 3 + 1))
            if i >= 2:
                act.wait_ge(s_tr, 2 * (i - 1))
            nc.scalar.activation(xn[0:r, i % 2, :], xs[0:r, i % 3, :], ACT.Square, scale=D ** -0.5,
                                 accum_out=ssq[0:r, i:i + 1]).then_inc(s_ssq, 1)
            act.wait_ge(s_ssq, i + 1)
            nc.scalar.activation(rstd[0:r, TT + i:TT + i + 1], ssq[0:r, i:i + 1], ACT.Sqrt,
                                 bias=eps_c[0:r, :]).then_inc(s_rt, 1)
            if i >= 1:
                j = i - 1
                act.wait_ge(s_tr, 2 * j + 1)
                nc.scalar.copy(hT[:, 0:4, j * P:(j + 1) * P],
                               bank[2 * (j % 2)][:, :].rearrange("p (k t) -> p k t", t=P)).then_inc(s_trev, 1)
                act.wait_ge(s_tr, 2 * j + 2)
                nc.scalar.copy(hT[:, 4:8, j * P:(j + 1) * P],
                               bank[2 * (j % 2) + 1][:, :].rearrange("p (k t) -> p k t", t=P)).then_inc(s_trev, 1)
        j = TT - 1
        for h in range(2):
            act.wait_ge(s_tr, 2 * j + 1 + h)
            nc.scalar.copy(hT[:, 4 * h:4 * h + 4, j * P:j * P + NS],
                           bank[2 * (j % 2) + h][:, :].rearrange("p (k t) -> p k t", t=P)[:, :, 0:NS]).then_inc(s_trev, 1)

        def evac(kind, m, b):
            n = index[(kind, m, b)]
            act.wait_ge(s_grp, n + 1)
            t0, tn = BLK[b]
            a = acc(n)
            if kind == "lr":
                nc.scalar.copy(lrT[:, t0:t0 + tn], a[0:LR, 0:tn]).then_inc(s_eva, 1)
            elif kind == "k":
                nc.scalar.copy(kT[:, m, t0:t0 + tn], a[:, 0:tn]).then_inc(s_eva, 1)
            elif kind == "q":
                nc.scalar.mul(qT[:, m, t0:t0 + tn], a[:, 0:tn], DK ** -0.5).then_inc(s_eva, 1)
            elif kind == "u":
                pn = min(tn, SEQ - t0)
                if pn == tn:
                    nc.scalar.copy(uT[:, m, U_P + t0:U_P + t0 + tn], a[:, 0:tn]).then_inc(s_eva, 1)
                else:
                    nc.scalar.copy(uT[:, m, U_P + t0:U_P + t0 + pn], a[:, 0:pn])
                    nc.scalar.copy(tmpa[:, m * NS:(m + 1) * NS], a[:, pn:tn])
                    nc.scalar.copy(uT[:, m, U_S:].rearrange("p (b t) -> p b t", t=SEG)[:, :, HIST:],
                                   a[:, pn:tn].rearrange("p (b t) -> p b t", t=DEC_T)).then_inc(s_eva, 1)
            elif kind == "mix":
                nc.scalar.activation(uT[:, m, t0:t0 + tn], a[:, 0:tn], ACT.Copy,
                                     scale=pscale[:, m:m + 1]).then_inc(s_eva, 1)

        for b in range(3):
            evac("lr", 0, b)
        act.wait_ge(s_hist, 1)
        nc.scalar.copy(uT[:, :, U_S:].rearrange("p m (b t) -> p m b t", t=SEG)[:, 0:2, :, 0:HIST],
                       bank[0][:, :].rearrange("p (m x) -> p m x", m=PG)[:, 0:2, 0:DEC_B * HIST].rearrange(
                           "p m (b t) -> p m b t", t=HIST))
        nc.scalar.copy(uT[:, :, U_S:].rearrange("p m (b t) -> p m b t", t=SEG)[:, 2:4, :, 0:HIST],
                       bank[0][:, :].rearrange("p (m x) -> p m x", m=PG)[:, 2:4, 0:DEC_B * HIST].rearrange(
                           "p m (b t) -> p m b t", t=HIST)).then_inc(s_histev, 1)
        for m in range(2):
            act.wait_ge(s_evd, 3 * m + 3)
            if m:
                act.wait_ge(s_b, m)
            nc.scalar.activation(tmpa[:], bT[:, m, :], ACT.Abs).then_inc(s_a, 1)
            act.wait_ge(s_a, 2 * m + 1)
            nc.scalar.activation(tmpa[:], tmpa[:], ACT.Exp, scale=-1.0).then_inc(s_a, 1)
            act.wait_ge(s_a, 2 * m + 2)
            nc.scalar.activation(tmpa[:], tmpa[:], ACT.Ln, bias=1.0).then_inc(s_za, 1)
        for kind in "kq":
            for m in range(2):
                for b in range(3):
                    evac(kind, m, b)

        def exps(c):
            n = ROWS[c]
            act.wait_ge(s_args, c + 1)
            if c < TT - 1:
                nc.scalar.activation(T1[:, :, :, :].rearrange("p a b t -> p (a b t)"),
                                     T1[:, :, :, :].rearrange("p a b t -> p (a b t)"), ACT.Exp, scale=1.0 / GATE)
                nc.scalar.activation(T2[:, :, :, :].rearrange("p a b t -> p (a b t)"),
                                     T2[:, :, :, :].rearrange("p a b t -> p (a b t)"), ACT.Exp,
                                     scale=1.0 / GATE).then_inc(s_exp, 1)
            else:
                nc.scalar.activation(T1[:, :, :, 0:n].rearrange("p a b t -> p (a b) t"),
                                     T1[:, :, :, 0:n].rearrange("p a b t -> p (a b) t"), ACT.Exp, scale=1.0 / GATE)
                nc.scalar.activation(T2[:, :, 0, 0:n], T2[:, :, 0, 0:n], ACT.Exp, scale=1.0 / GATE).then_inc(s_exp, 1)

        def keys_rows(c):
            n = ROWS[c]
            act.wait_ge(s_score, c + 1)
            nc.scalar.copy(khN[0:n, :, :], bank[1][0:n, 0:256].rearrange("p (a d) -> p a d", a=2)).then_inc(s_khn, 1)

        def squares(c):
            act.wait_ge(s_o, c + 1)
            nc.scalar.activation(o2[:] if ROWS[c] == P else o2[:].rearrange("p (h t) -> p h t", h=HEADS)[:, :, 0:NS],
                                 bank[2][:, :] if ROWS[c] == P else
                                 bank[2][:, :].rearrange("p (h t) -> p h t", h=HEADS)[:, :, 0:NS],
                                 ACT.Square).then_inc(s_sq, 1)

        def inv_root(c):
            act.wait_ge(s_ms, c + 1)
            if c >= 1:
                act.wait_ge(s_on, c)
            nc.scalar.activation(rs[:], bank[4][:, :], ACT.Ln, bias=eps_c[:]).then_inc(s_a, 1)
            act.wait_ge(s_a, 5 + c)
            nc.scalar.activation(rs[:], rs[:], ACT.Exp, scale=-0.5).then_inc(s_rs, 1)

        exps(0)
        for c in range(TT - 1):
            if ug[3 * c][0] == "u":
                evac(*ug[3 * c])
            keys_rows(c)
            if ug[3 * c + 1][0] == "u":
                evac(*ug[3 * c + 1])
            squares(c)
            if c + 1 < TT - 1:
                exps(c + 1)
            if ug[3 * c + 2][0] == "u":
                evac(*ug[3 * c + 2])
            inv_root(c)
        exps(TT - 1)
        act.wait_ge(s_np, 1)
        nc.scalar.copy(npP, bank[0][0:HIST, :])
        nc.scalar.copy(npS, bank[1][0:NS, :]).then_inc(s_npev, 1)
        for m in range(4):
            for b in range(3):
                evac("mix", m, b)
        keys_rows(TT - 1)
        squares(TT - 1)
        inv_root(TT - 1)
        act.wait_ge(s_evd, evacs(len(groups) - 1, False))
        for m in range(4):
            nc.scalar.activation(gT[:, m, :], gT[:, m, :], ACT.Silu).then_inc(s_silu, 1)

    @blk.vector
    def _(dve):
        chain = [0]

        def link(ins):
            chain[0] += 1
            ins.then_inc(s_d, 1)
            dve.wait_ge(s_d, chain[0])

        dve.wait_ge(s_g1, 16)
        dve.wait_ge(s_gc, GC)
        link(nc.vector.reciprocal(icnt[:], icnt[:]))
        for i in range(TT):
            r = ROWS[i]
            dve.wait_ge(s_rt, i + 1)
            link(nc.vector.reciprocal(rstd[0:r, i:i + 1], rstd[0:r, TT + i:TT + i + 1]))
            if i == 0:
                dve.wait_ge(s_const, 16 * 8)
            nc.vector.scalar_tensor_tensor(out=xn[0:r, i % 2, :], in0=xs[0:r, i % 3, :], scalar=rstd[0:r, i:i + 1],
                                           in1=g1b[0:r, :], op0=ALU.mult, op1=ALU.mult).then_inc(s_xn, 1)

        def evac(kind, m, b):
            n = index[(kind, m, b)]
            dve.wait_ge(s_grp, n + 1)
            a = acc(n)
            if kind == "v":
                nc.vector.tensor_copy(v[0:ROWS[b], b, :], a[0:ROWS[b], :]).then_inc(s_evd, 1)
                return
            t0, tn = BLK[b]
            if kind == "z":
                nc.vector.tensor_scalar(bT[:, m, t0:t0 + tn], a[:, 0:tn], bgk[:, m:m + 1], None,
                                        ALU.add).then_inc(s_evd, 1)
            else:
                nc.vector.tensor_copy(gT[:, m, t0:t0 + tn], a[:, 0:tn]).then_inc(s_evd, 1)

        for m in range(2):
            for b in range(3):
                evac("z", m, b)
        for m in range(2):
            dve.wait_ge(s_za, m + 1)
            nc.vector.scalar_tensor_tensor(out=bT[:, m, :], in0=bT[:, m, :], scalar=0.0, in1=tmpa[:], op0=ALU.min,
                                           op1=ALU.subtract).then_inc(s_b, 1)
            dve.wait_ge(s_b, m + 1)
        for c in range(TT):
            for m in range(2):
                n = ROWS[c]
                sl = bT[:, m, c * P:c * P + n]
                ch = nc.vector.tensor_tensor_scan(sl, onesf[:, 0:n] if n == P else resets[:], sl, 0.0,
                                                  ALU.mult, ALU.add)
        link(ch)
        link(nc.vector.tensor_copy(rmid[:, :, :],
                                   bT[:, :, 0:SEQ].rearrange("p a (i t) -> p a i t", t=SB)[:, :, :, SB // 2 - 1]))

        for t in range(TT):
            evac("v", 0, t)

        def args(c):
            n = ROWS[c]
            B = bT[:, :, c * P:c * P + n]
            if c >= 1:
                dve.wait_ge(s_o, c)
            if c < TT - 1:
                r = rmid[:, :, 4 * c:4 * c + 4]
                nc.vector.tensor_tensor(T1[:, 0, :, :].rearrange("p a (i t) -> p a i t", t=SB),
                                        B.rearrange("p a (i t) -> p a i t", t=SB),
                                        r.unsqueeze(3).broadcast_to([P, 2, 4, SB]), ALU.subtract)
                nc.vector.tensor_copy(T1[:, 1, :, :], B)
                nc.vector.tensor_tensor(T1[:, 2, :, :], B[:, :, P - 1:P].broadcast_to([P, 2, P]), B, ALU.subtract)
                for p in range(2):
                    link(nc.vector.tensor_tensor(T2[:, p, :, :], r[:, p, :].unsqueeze(2).broadcast_to([P, 4, P]),
                                                 B[:, p, :].unsqueeze(1).broadcast_to([P, 4, P]), ALU.subtract))
                nc.vector.tensor_scalar(T1[:, 0, :, :], T1[:, 0, :, :], CLAMP, -CLAMP, ALU.min, ALU.max)
                nc.vector.tensor_scalar(T2[:, :, :, :], T2[:, :, :, :], CLAMP, -CLAMP, ALU.min,
                                        ALU.max).then_inc(s_args, 1)
            else:
                nc.vector.tensor_scalar(T1[:, 0, :, 0:n], B, CLAMP, -CLAMP, ALU.min, ALU.max)
                nc.vector.tensor_copy(T1[:, 1, :, 0:n], B)
                for p in range(2):
                    bl = B[:, p, :].rearrange("p (b t) -> p b t", t=DEC_T)
                    nc.vector.tensor_tensor(T1[:, 2, p, 0:n].rearrange("p (b t) -> p b t", t=DEC_T),
                                            bl[:, :, DEC_T - 1:DEC_T].broadcast_to([P, DEC_B, DEC_T]), bl,
                                            ALU.subtract)
                nc.vector.tensor_scalar(T2[:, :, 0, 0:n], B, -1.0, CLAMP, ALU.mult, ALU.min).then_inc(s_args, 1)

        def decayed(c):
            n = ROWS[c]
            dve.wait_ge(s_exp, c + 1)
            if c == 0:
                dve.wait_ge(s_eva, evacs(index[("q", 1, 2)], True))
            q, k = qT[:, :, c * P:c * P + n], kT[:, :, c * P:c * P + n]
            if c < TT - 1:
                nc.vector.tensor_copy(sdec[:], T1[:, 1, :, P - 1])
            else:
                nc.vector.tensor_copy(o_dec[:], T1[:, 1, :, 0:n].rearrange("p a (b t) -> p a b t", t=DEC_T)[:, :, :, DEC_T - 1])
            dve.wait_ge(s_exp, c + 1)
            chain[0] += 1
            nc.vector.tensor_tensor(T1[:, 2, :, 0:n], T1[:, 2, :, 0:n], k, ALU.mult).then_inc(s_d, 1)
            dve.wait_ge(s_d, chain[0])
            for a in range(2):
                rows = slice(64 * a, 64 * a + 64)
                nc.vector.tensor_tensor(qz[rows, :, :, 0:n].rearrange("p w (b a) t -> p w b a t", a=2)[:, :, :, a, :],
                                        T1[rows, 0:2, :, 0:n], q[rows, :, :].unsqueeze(1).broadcast_to([64, 2, 2, n]),
                                        ALU.mult)
            if c < TT - 1:
                for p in range(2):
                    x = nc.vector.tensor_tensor(T2[:, p, :, :], T2[:, p, :, :],
                                                k[:, p, :].unsqueeze(1).broadcast_to([P, 4, P]), ALU.mult)
            else:
                x = nc.vector.tensor_tensor(T2[:, :, 0, 0:n], T2[:, :, 0, 0:n], k, ALU.mult)
            x.then_inc(s_kq, 1)

        def mask_scores(c):
            n = ROWS[c]
            dve.wait_ge(s_score, c + 1)
            S = bank[0][:, :].rearrange("p (h t) -> p h t", h=HEADS)
            if c < TT - 1:
                for i in range(4):
                    m = SB * (i + 1)
                    t = slice(SB * i, SB * (i + 1))
                    x = nc.vector.tensor_tensor(Pm[0:m, :, t], S[0:m, :, t],
                                                mask_p[0:m, t].unsqueeze(1).broadcast_to([m, HEADS, SB]), ALU.mult)
            else:
                x = nc.vector.tensor_tensor(Pm[0:n, :, 0:n], S[0:n, :, 0:n],
                                            mask_s[:].unsqueeze(1).broadcast_to([n, HEADS, n]), ALU.mult)
            x.then_inc(s_pm, 1)

        def state(c):
            dve.wait_ge(s_o, c + 1)
            for h in range(HEADS):
                p, a = h // 2, 64 * (h % 2)
                add = bank[3][a:a + 64, p * 256 + 2 * a:p * 256 + 2 * a + DV]
                if c == 0:
                    x = nc.vector.tensor_copy(Sp[a:a + 64, p, :], add)
                else:
                    x = nc.vector.scalar_tensor_tensor(out=Sp[a:a + 64, p, :], in0=Sp[a:a + 64, p, :],
                                                       scalar=sdec[a:a + 64, p:p + 1], in1=add, op0=ALU.mult,
                                                       op1=ALU.add)
            x.then_inc(s_st, 1)

        def out_norm(c):
            n = ROWS[c]
            dve.wait_ge(s_rs, c + 1)
            O_, R_ = bank[2][:, :], rs[:]
            dst = v[:, c, 0:HEADS * n].rearrange("p (h t) -> p h t", h=HEADS)
            nc.vector.scalar_tensor_tensor(out=dst, in0=O_.rearrange("p (h t) -> p h t", h=HEADS)[:, :, 0:n],
                                           scalar=gnorm[:], in1=R_.rearrange("p (h t) -> p h t", h=HEADS)[:, :, 0:n],
                                           op0=ALU.mult, op1=ALU.mult).then_inc(s_on, 1)

        def pool_group(m):
            w = WINDOWS[m]
            full = wsum[:, :, :].rearrange("p a b -> p (a b)")[:, (m % 2) * 1536:(m % 2) * 1536 + U_W - U_P]
            dve.wait_ge(s_eva, evacs(index[("u", m, 2)], True))
            if m == 0:
                dve.wait_ge(s_histev, 1)
            if m >= 2:
                dve.wait_ge(s_grp, index[("mix", m - 2, 2)] + 1)
            link(nc.vector.tensor_tensor_scan(full, uT[:, m, U_P:U_W], uT[:, m, U_P - w:U_W - w], 0.0,
                                              ALU.add, ALU.subtract))
            cur = uT[:, m, U_P:U_P + 16]
            link(nc.vector.tensor_tensor(rs[:, 0:w], full[:, 0:w], icnt[:, 0:w], ALU.mult))
            link(nc.vector.scalar_tensor_tensor(out=rs[:, 32:32 + NS].rearrange("p (b t) -> p b t", t=DEC_T),
                                           in0=full[:, SEQ:].rearrange("p (b t) -> p b t", t=SEG)[:, :, HIST:],
                                           scalar=1.0 / w,
                                           in1=uT[:, m, U_S:].rearrange("p (b t) -> p b t", t=SEG)[:, :, HIST:],
                                           op0=ALU.mult, op1=ALU.subtract))
            nc.vector.scalar_tensor_tensor(out=full[:, w:SEQ], in0=full[:, w:SEQ], scalar=1.0 / w,
                                           in1=uT[:, m, U_P + w:U_S], op0=ALU.mult, op1=ALU.subtract)
            nc.vector.tensor_tensor(full[:, 0:w], rs[:, 0:w], cur[:, 0:w], ALU.subtract)
            nc.vector.tensor_copy(full[:, SEQ:SEQ + NS], rs[:, 32:32 + NS]).then_inc(s_pool, 1)

        dve.wait_ge(s_tr, 2 * TT)
        link(nc.vector.memset(qz[:, :, :, :], 0.0))
        args(0)
        decayed(0)
        for c in range(TT - 1):
            if ug[3 * c][0] == "g":
                evac(*ug[3 * c])
            mask_scores(c)
            if ug[3 * c + 1][0] == "g":
                evac(*ug[3 * c + 1])
            state(c)
            if c + 1 < TT - 1:
                args(c + 1)
                decayed(c + 1)
            if ug[3 * c + 2][0] == "g":
                evac(*ug[3 * c + 2])
            out_norm(c)
        args(TT - 1)
        dve.wait_ge(s_on, TT - 1)
        for m in range(PG):
            pool_group(m)
        decayed(TT - 1)
        mask_scores(TT - 1)
        dve.wait_ge(s_o, TT)
        dve.wait_ge(s_khn, TT)
        nc.vector.tensor_tensor(KM, khN[0:NS, :, :].rearrange("p a d -> p (a d)").unsqueeze(1).broadcast_to(
            [NS, DEC_B, 256]), bmask[:].unsqueeze(2).broadcast_to([NS, DEC_B, 256]), ALU.mult).then_inc(s_km, 1)
        dve.wait_ge(s_o, TT)
        for p in range(2):
            link(nc.vector.tensor_tensor(S0[:, :, p, :], S0[:, :, p, :],
                                         o_dec[:, p, :].unsqueeze(2).broadcast_to([P, DEC_B, DV]), ALU.mult))
        for b in range(DEC_B):
            dve.wait_ge(s_ku, b + 1)
            for a in range(2):
                src = bank[[0, 3][b % 2]][64 * a:64 * a + 64, :].rearrange("p (q x) -> p q x", q=2)[
                    :, :, a * DV:(a + 1) * DV]
                x = nc.vector.tensor_tensor(S0[64 * a:64 * a + 64, b, :, :], S0[64 * a:64 * a + 64, b, :, :], src,
                                            ALU.add)
            x.then_inc(s_us, 1)
        out_norm(TT - 1)
        for m in range(4):
            dve.wait_ge(s_silu, m + 1)
            dve.wait_ge(s_on, TT)
            nc.vector.tensor_tensor(gT[:, m, 0:SEQ].rearrange("p (c t) -> p c t", t=P),
                                    gT[:, m, 0:SEQ].rearrange("p (c t) -> p c t", t=P),
                                    v[:, 0:TT - 1, m * P:(m + 1) * P], ALU.mult)
            nc.vector.tensor_tensor(gT[:, m, SEQ:N], gT[:, m, SEQ:N], v[:, TT - 1, m * NS:(m + 1) * NS], ALU.mult)

    block.close()
    c1.close()


def b2_all(nc, A, sb, sem, bank, ident, onesf, eps_c, uT, gT, ring, x1, x_rows, h2_dram,
           w1, w2, rank_m, token, expert, iota_w, steps):
    c2 = ExitStack()
    h2 = sb("h2", [P, 2, D], ctx=c2)
    h2T = sb("h2T", [P, 2, KC, P], ctx=c2)
    g2b = sb("g2b", [P, D], ctx=c2)
    wr = sb("wr", [P, KC, NG + NE], ctx=c2)
    rb = sb("rb", [P, NG + NE], ctx=c2)
    ssq = sb("ssq2", [P, TT], ctx=c2)
    root = sb("root2", [P, TT], ctx=c2)
    rstd = sb("rstd2", [P, TT], ctx=c2)
    L = sb("L", [P, TT, NG + NE], ctx=c2)
    before = sb("before", [P, P], BF16, ctx=c2)
    onesb = sb("onesb", [P, P], BF16, ctx=c2)
    first = sb("first", [P, 4], ctx=c2)
    M = sb("M", [P, TT, NE], ctx=c2)
    M1 = sb("M1", [P, TT, NE], ctx=c2)
    M2 = sb("M2", [P, TT, NE], ctx=c2)
    Mb = sb("Mb", [P, TT, NE], BF16, ctx=c2)
    Mp = sb("Mp", [P, TT + 1, NE], BF16, ctx=c2)
    rank = sb("rank", [P, TT, NE], ctx=c2)
    t4 = sb("t4", [P, TT, NG], ctx=c2)
    ohg = sb("ohg", [P, TT, NG], ctx=c2)
    oh1 = sb("oh1", [P, TT, 4], ctx=c2)
    oh2 = sb("oh2", [P, TT, 4], ctx=c2)
    es = sb("es", [P, TT, 4], ctx=c2)
    pr = sb("pr", [P, TT, 4, 4], ctx=c2)
    s1 = sb("s1", [P, TT], ctx=c2)
    s2 = sb("s2", [P, TT], ctx=c2)
    gp = sb("gp", [P, TT], ctx=c2)
    mx = sb("mx", [P, TT], ctx=c2)
    full = sb("full", [P, NE], ctx=c2)
    mxc = sb("mxc", [P, 2], ctx=c2)
    rlim = sb("rlim", [P, 8], ctx=c2)

    r_c, r_w = sem("r_c"), sem("r_w")
    r_x = sem("r_x")
    r_y, r_x1, r_ssq, r_root, r_h2, r_tr, r_trev, r_lg, r_lgev = [sem(x) for x in (
        "r_y", "r_x1", "r_ssq", "r_root", "r_h2", "r_tr", "r_trev", "r_lg", "r_lgev")]
    r_hout = [sem(f"r_hout{j}") for j in range(2)]
    r_gc, r_d, r_ex, r_exd, r_m, r_rk, r_hf = [sem(x) for x in ("r_gc", "r_d", "r_ex", "r_exd", "r_m", "r_rk", "r_hf")]
    r_xt = [sem(f"r_xt{i}") for i in range(TT)]
    block = ExitStack()
    blk = block.enter_context(nc.Block())
    GC = 11

    @blk.gpsimd
    def _(pool):
        nc.gpsimd.memset(before[:], 1.0).then_inc(r_gc, 1)
        nc.gpsimd.memset(onesb[:], 1.0).then_inc(r_gc, 1)
        nc.gpsimd.memset(L[:], 0.0).then_inc(r_gc, 1)
        nc.gpsimd.memset(rlim[:], 0.0).then_inc(r_gc, 1)
        nc.gpsimd.iota(first[:], [[-1, 4]], base=4, channel_multiplier=0,
                       allow_small_or_imprecise_dtypes=True).then_inc(r_gc, 1)
        nc.gpsimd.iota(expert[:], [[1, NE]], base=1, channel_multiplier=0,
                       allow_small_or_imprecise_dtypes=True).then_inc(r_gc, 1)
        nc.gpsimd.iota(iota_w[:], [[1, W]], base=0, channel_multiplier=0,
                       allow_small_or_imprecise_dtypes=True).then_inc(r_gc, 1)
        nc.gpsimd.iota(token[:, :, 0], [[P, TT]], base=0, channel_multiplier=1,
                       allow_small_or_imprecise_dtypes=True).then_inc(r_gc, 1)
        nc.gpsimd.memset(Mp[:], 0.0).then_inc(r_gc, 1)
        pool.wait_ge(r_gc, 9)
        nc.gpsimd.affine_select(out=before[:], in_=before[:], pattern=[[1, P]], compare_op=ALU.is_gt, fill=0.0,
                                base=0, channel_multiplier=-1).then_inc(r_gc, 1)
        nc.gpsimd.iota(rlim[:, 0:ROUNDS], [[W, ROUNDS]], base=0, channel_multiplier=0,
                       allow_small_or_imprecise_dtypes=True).then_inc(r_gc, 1)

    @blk.sync
    def _(sp):
        sp.dma_start(g2b[:], A["norm2_g"].broadcast_to([P, D])).then_inc(r_c, 16)
        with nc.allow_non_contiguous_dma(reason="router weights, 16 and 64 bytes a row"):
            sp.dma_start(wr[:, :, 0:NG], A["w_router_group"][0].rearrange("(k p) n -> p k n", p=P)).then_inc(r_c, 16)
            sp.dma_start(wr[:, :, NG:], A["w_router_expert"][0].rearrange("(k p) n -> p k n", p=P)).then_inc(r_c, 16)
        sp.dma_start(rb[:, 0:NG], A["b_router_group"].broadcast_to([P, NG])).then_inc(r_c, 16)
        sp.dma_start(rb[:, NG:], A["b_router_expert"].broadcast_to([P, NE])).then_inc(r_c, 16)
        for i in range(TT):
            sp.dma_start(x1[0:ROWS[i], i, :], x_rows[i]).then_inc(r_xt[i], 16)
        for i in range(TT):
            sp.wait_ge(r_h2, i + 1)
            sp.dma_start(h2_dram[i * P:i * P + ROWS[i], :], h2[0:ROWS[i], i % 2, :]).then_inc(r_hout[i % 2], 16)
        for j in range(2):
            sp.wait_ge(r_hout[j], 16 * len(range(j, TT, 2)))

    @blk.tensor
    def _(pe):
        def router(i):
            r = ROWS[i]
            pe.wait_ge(r_h2, i + 1)
            if i >= 1:
                pe.wait_ge(r_trev, 2 * i)
            for h in range(2):
                for k in range(4):
                    t = nc.tensor.transpose(bank[4 + h][:, k * P:k * P + r],
                                            h2[0:r, i % 2, (4 * h + k) * P:(4 * h + k + 1) * P], ident[0:r, 0:r])
                t.then_inc(r_tr, 1)
            if i == 0:
                return
            logits(i - 1)

        def logits(i):
            r = ROWS[i]
            pe.wait_ge(r_trev, 2 * (i + 1))
            if i >= 1:
                pe.wait_ge(r_lgev, i)
            for k in range(KC):
                m = nc.tensor.matmul(bank[6][0:r, 0:NG + NE], h2T[:, i % 2, k, 0:r], wr[:, k, :],
                                     start=k == 0, stop=k == KC - 1)
            m.then_inc(r_lg, 1)

        pe.wait_ge(r_c, 16 * 5)
        for i in range(TT):
            r = ROWS[i]
            for h in range(2):
                if i >= 2:
                    pe.wait_ge(r_x1, 2 * (i - 2) + h + 1)
                for k in range(KC):
                    a = uT[:, k, i * P:i * P + r] if k < 4 else gT[:, k - 4, i * P:i * P + r]
                    m = nc.tensor.matmul(bank[2 * (i % 2) + h][0:r, :], a, ring[:, 2 * h:2 * h + 2, k, :],
                                         start=k == 0, stop=k == KC - 1)
                m.then_inc(r_y, 1)
            if i >= 1:
                router(i - 1)
        router(TT - 1)
        logits(TT - 1)
        pe.wait_ge(r_m, 1)
        nc.tensor.matmul(bank[7][:, 0:TT * NE], onesb[:], Mp[:, 0:TT, :].rearrange("p t e -> p (t e)"),
                         start=True, stop=False)
        nc.tensor.matmul(bank[7][:, 0:TT * NE], before[:], Mb[:].rearrange("p t e -> p (t e)"), start=False, stop=True)
        nc.tensor.matmul(bank[6][:, 0:NE], onesb[:], Mp[:, TT, :], start=True, stop=True).then_inc(r_rk, 1)

    @blk.scalar
    def _(act):
        def transposed(i):
            r = ROWS[i]
            if i >= 2:
                act.wait_ge(r_lg, i - 1)
            for h in range(2):
                act.wait_ge(r_tr, 2 * i + h + 1)
                nc.scalar.copy(h2T[:, i % 2, 4 * h:4 * h + 4, 0:r],
                               bank[4 + h][:, :].rearrange("p (k t) -> p k t", t=P)[:, :, 0:r]).then_inc(r_trev, 1)

        for i in range(TT):
            r = ROWS[i]
            act.wait_ge(r_x1, 2 * i + 2)
            if i >= 2:
                act.wait_ge(r_tr, 2 * (i - 1))
                act.wait_ge(r_hout[i % 2], 16 * (i // 2))
            nc.scalar.activation(h2[0:r, i % 2, :], x1[0:r, i, :], ACT.Square, scale=D ** -0.5,
                                 accum_out=ssq[0:r, i:i + 1]).then_inc(r_ssq, 1)
            act.wait_ge(r_ssq, i + 1)
            nc.scalar.activation(root[0:r, i:i + 1], ssq[0:r, i:i + 1], ACT.Sqrt,
                                 bias=eps_c[0:r, :]).then_inc(r_root, 1)
            if i >= 1:
                transposed(i - 1)
        transposed(TT - 1)
        act.wait_ge(r_exd, 1)
        nc.scalar.activation(t4[:], t4[:], ACT.Exp).then_inc(r_ex, 1)
        act.wait_ge(r_exd, 2)
        nc.scalar.activation(s2[:], s2[:], ACT.Exp).then_inc(r_ex, 1)

    @blk.vector
    def _(dve):
        chain = [0]

        def link(ins):
            chain[0] += 1
            ins.then_inc(r_d, 1)
            dve.wait_ge(r_d, chain[0])

        def logit_out(i):
            r = ROWS[i]
            dve.wait_ge(r_lg, i + 1)
            nc.vector.tensor_tensor(L[0:r, i, :], bank[6][0:r, 0:NG + NE], rb[0:r, :], ALU.add).then_inc(r_lgev, 1)

        dve.wait_ge(r_c, 16 * 5)
        dve.wait_ge(r_gc, GC)
        for i in range(TT):
            r = ROWS[i]
            dve.wait_ge(r_xt[i], 16)
            for h in range(2):
                dve.wait_ge(r_y, 2 * i + h + 1)
                nc.vector.tensor_tensor(x1[0:r, i, h * 512:(h + 1) * 512], x1[0:r, i, h * 512:(h + 1) * 512],
                                        bank[2 * (i % 2) + h][0:r, :], ALU.add).then_inc(r_x1, 1)
            dve.wait_ge(r_root, i + 1)
            link(nc.vector.reciprocal(rstd[0:r, i:i + 1], root[0:r, i:i + 1]))
            nc.vector.scalar_tensor_tensor(out=h2[0:r, i % 2, :], in0=x1[0:r, i, :], scalar=rstd[0:r, i:i + 1],
                                           in1=g2b[0:r, :], op0=ALU.mult, op1=ALU.mult).then_inc(r_h2, 1)
            if i >= 2:
                logit_out(i - 2)
        logit_out(TT - 2)
        logit_out(TT - 1)
        dve.wait_ge(r_lgev, TT)

        def b(ap, shape):
            return ap.unsqueeze(2).broadcast_to(shape)

        def pick(oh, vals, top):
            link(nc.vector.tensor_reduce(top[:], vals, axis=AX.X, op=ALU.max))
            link(nc.vector.tensor_tensor(oh[:], vals, b(top[:], [P, TT, 4]), ALU.is_equal))
            link(nc.vector.tensor_tensor(oh[:], oh[:], first[:].unsqueeze(1).broadcast_to([P, TT, 4]), ALU.mult))
            link(nc.vector.tensor_reduce(mx[:], oh[:], axis=AX.X, op=ALU.max))
            link(nc.vector.tensor_tensor(oh[:], oh[:], b(mx[:], [P, TT, 4]), ALU.is_equal))

        gl, el = L[:, :, 0:NG], L[:, :, NG:]
        pick(ohg, gl, s1)
        nc.vector.tensor_tensor(t4[:], gl, b(s1[:], [P, TT, NG]), ALU.subtract).then_inc(r_exd, 1)
        link(nc.vector.tensor_tensor(pr[:], el.rearrange("p t (g j) -> p t g j", g=NG),
                                     ohg[:].unsqueeze(3).broadcast_to([P, TT, NG, 4]), ALU.mult))
        link(nc.vector.tensor_reduce(es[:], pr[:].rearrange("p t g j -> p t j g"), axis=AX.X, op=ALU.add))
        pick(oh1, es[:], s1)
        link(nc.vector.scalar_tensor_tensor(out=es[:], in0=oh1[:], scalar=-3e38, in1=es[:], op0=ALU.mult, op1=ALU.add))
        pick(oh2, es[:], s2)
        nc.vector.tensor_tensor(s2[:], s2[:], s1[:], ALU.subtract).then_inc(r_exd, 1)
        for oh, m in ((oh1, M1), (oh2, M2)):
            link(nc.vector.tensor_tensor(m[:].rearrange("p t (g j) -> p t g j", g=NG),
                                         ohg[:].unsqueeze(3).broadcast_to([P, TT, NG, 4]),
                                         oh[:].unsqueeze(2).broadcast_to([P, TT, NG, 4]), ALU.mult))
        link(nc.vector.memset(M1[NS:P, TT - 1, :], 0.0))
        link(nc.vector.memset(M2[NS:P, TT - 1, :], 0.0))
        link(nc.vector.tensor_tensor(M[:], M1[:], M2[:], ALU.add))
        link(nc.vector.tensor_copy(Mb[:], M[:]))
        for t in range(TT):
            x = nc.vector.tensor_tensor(Mp[:, t + 1, :], Mp[:, t, :], Mb[:, t, :], ALU.add)
            if t < TT - 1:
                link(x)
        x.then_inc(r_m, 1)
        dve.wait_ge(r_ex, 2)
        link(nc.vector.tensor_reduce(gp[:], t4[:], axis=AX.X, op=ALU.add))
        link(nc.vector.tensor_scalar(s1[:], s2[:], 1.0, None, ALU.add))
        link(nc.vector.tensor_tensor(s1[:], s1[:], gp[:], ALU.mult))
        link(nc.vector.reciprocal(w1[:], s1[:]))
        link(nc.vector.tensor_tensor(w2[:], w1[:], s2[:], ALU.mult))
        dve.wait_ge(r_rk, 1)
        link(nc.vector.tensor_copy(rank[:].rearrange("p t e -> p (t e)"), bank[7][:, 0:TT * NE]))
        link(nc.vector.tensor_tensor(M2[:], M2[:], expert[:].unsqueeze(1).broadcast_to([P, TT, NE]), ALU.mult))
        link(nc.vector.tensor_reduce(mx[:], M2[:], axis=AX.X, op=ALU.add))
        link(nc.vector.tensor_copy(token[:, :, 1], mx[:]))
        link(nc.vector.scalar_tensor_tensor(out=rank[:], in0=rank[:], scalar=1.0, in1=M[:], op0=ALU.add, op1=ALU.mult))
        link(nc.vector.tensor_scalar(rank_m[:].rearrange("p (e t) -> p t e", e=NE), rank[:], -1.0, None, ALU.add))
        link(nc.vector.tensor_reduce(mxc[:, 0:1], bank[6][:, 0:NE], axis=AX.X, op=ALU.max))
        link(nc.vector.tensor_scalar(rlim[:, 0:ROUNDS], rlim[:, 0:ROUNDS], mxc[:, 0:1], float(NE), ALU.is_lt, ALU.mult))
        link(nc.vector.tensor_reduce(mxc[:, 1:2], rlim[:, 0:ROUNDS], axis=AX.X, op=ALU.add))
        link(nc.vector.tensor_copy(steps[0:1, 0:1], mxc[0:1, 1:2]))

    block.close()
    c2.close()


def b3_all(nc, A, sb, sem, bank, ident, h2_dram, y_dram, rank_m, token, expert, iota_w, steps):
    c3 = ExitStack()
    wt = sb("wt", [P, 6, 2048], ctx=c3)
    xg = sb("xg", [P, 2, D], ctx=c3)
    xT = sb("xT", [P, KC, W], ctx=c3)
    oh = sb("oh", [P, TT, W], FP16, ctx=c3)
    idx = sb("idx", [P, 2], I32, ctx=c3)
    far = sb("far", [P, 2], ctx=c3)
    dest = sb("dest", [P, 2], I32, ctx=c3)
    dest_now = sb("dest_now", [P, 2], I32, ctx=c3)
    sg = sb("sg", [P, 2, W], ctx=c3)
    hold_at = sb("hold_at", [P, 1], ctx=c3)
    hid = sb("hid", [P, 4, W], ctx=c3)
    yT = sb("yT", [P, KC, W], ctx=c3)
    yr = sb("yr", [P, 2, D], ctx=c3)
    wg = A["w_gate"].rearrange("l e (k p) n -> (l e) p k n", p=P)
    wu = A["w_up"].rearrange("l e (k p) n -> (l e) p k n", p=P)
    wd = A["w_down"].rearrange("l e (k p) n -> (l e) p k n", p=P)

    e_w = [sem(f"e_w{u}") for u in range(6)]
    e_oh, e_ix, e_idx = sem("e_oh"), sem("e_ix"), sem("e_idx")
    e_far, e_now = sem("e_far"), sem("e_now")
    e_hold = sem("e_hold")
    e_rk = sem("e_rk")
    e_xg, e_xt, e_xe = sem("e_xg"), sem("e_xt"), sem("e_xe")
    e_gu, e_si, e_h = sem("e_gu"), sem("e_si"), sem("e_h")
    e_yt, e_ya, e_yd = sem("e_yt"), sem("e_ya"), sem("e_yd")
    e_yr, e_re, e_out = sem("e_yr"), sem("e_re"), sem("e_out")
    block = ExitStack()
    blk = block.enter_context(nc.Block())

    def count(eng):
        return eng.value_load(steps[0:1, 0:1], min_val=NE, max_val=NE * ROUNDS)

    @blk.sync
    def _(sp):
        def unit(u, e):
            if u < 4:
                src = (wg, wu)[u % 2][e, :, :, (u // 2) * 256:(u // 2 + 1) * 256]
                return wt[:, u, :].rearrange("p (k n) -> p k n", k=KC), src
            return (wt[:, u, :].rearrange("p (k n) -> p k n", k=4),
                    wd[e, :, :, (u - 4) * 512:(u - 3) * 512])

        n = count(sp)
        for u in range(6):
            dst, src = unit(u, 0)
            sp.dma_start(dst, src).then_inc(e_w[u], 16)
        with sp.Fori(0, n - 1) as i:
            e = (i + 1) % NE
            for u in range(6):
                sp.wait_ge(e_gu if u < 4 else e_yt, i * 4 + (2 if u in (0, 1, 4) else 4))
                dst, src = unit(u, bass.ds(e, 1))
                sp.dma_start(dst, src.rearrange("o p k n -> p (o k) n")).then_inc(e_w[u], 16)

    @blk.gpsimd
    def _(pool):
        def gather():
            nc.gpsimd.indirect_dma_start(out=xg[:, 0, :], out_offset=None, in_=h2_dram,
                                         in_offset=bass.IndirectOffsetOnAxis(ap=idx[:, 0:1], axis=0)
                                         ).then_inc(e_xg, 16)
            nc.gpsimd.indirect_dma_start(out=xg[0:W2, 1, :], out_offset=None, in_=h2_dram,
                                         in_offset=bass.IndirectOffsetOnAxis(ap=idx[0:W2, 1:2], axis=0)
                                         ).then_inc(e_xg, 16)

        def scatter():
            for c, m in ((0, P), (1, W2)):
                nc.gpsimd.indirect_dma_start(out=y_dram, in_=yr[0:m, c, :], in_offset=None, bounds_check=2 * N - 1,
                                             out_offset=bass.IndirectOffsetOnAxis(ap=dest_now[0:m, c:c + 1], axis=0),
                                             oob_is_err=False).then_inc(e_out, 16)

        def hold():
            nc.gpsimd.tensor_tensor(hold_at[:], ident[:, 0:1], ident[:, 1:2], ALU.add).then_inc(e_hold, 1)

        n = count(pool)
        pool.wait_ge(e_idx, 1)
        gather()
        with pool.Fori(0, n) as i:
            pool.wait_ge(e_hold, i * 2)
            pool.wait_ge(e_idx, i + 2)
            pool.wait_ge(e_xt, i * 3 + 3)
            hold()
            gather()
            pool.wait_ge(e_hold, i * 2 + 1)
            pool.wait_ge(e_re, i * 4 + 4)
            hold()
            scatter()
        pool.wait_ge(e_out, n * 32)
        pool.wait_ge(e_xg, n * 32 + 32)

    @blk.tensor
    def _(pe):
        def indices():
            for c, m in ((0, P), (1, W2)):
                for t in range(TT):
                    x = nc.tensor.matmul(bank[7][0:m, 2 * c:2 * c + 2], oh[:, t, c * P:c * P + m], token[:, t, :],
                                         start=t == 0, stop=t == TT - 1)
            x.then_inc(e_ix, 1)

        def rows_in():
            for h in range(2):
                for k in range(4):
                    x = nc.tensor.transpose(bank[4 + h][:, k * P:(k + 1) * P],
                                            xg[:, 0, (4 * h + k) * P:(4 * h + k + 1) * P], ident[:])
                x.then_inc(e_xt, 1)
            for k in range(KC):
                x = nc.tensor.transpose(bank[6][:, k * W2:(k + 1) * W2], xg[0:W2, 1, k * P:(k + 1) * P],
                                        ident[0:W2, 0:W2])
            x.then_inc(e_xt, 1)

        def gate_up(f):
            c0 = (f % 2) * P
            for side in range(2):
                u = 2 * (f // 2) + side
                for k in range(KC):
                    x = nc.tensor.matmul(bank[f % 2][:, side * 256:side * 256 + W],
                                         wt[:, u, k * 256 + c0:k * 256 + c0 + P], xT[:, k, :],
                                         start=k == 0, stop=k == KC - 1)
            x.then_inc(e_gu, 1)

        def down(j):
            for q in range(2):
                d = 2 * j + q
                u = 4 + d // 4
                for k in range(4):
                    x = nc.tensor.matmul(bank[2 + j % 2][:, q * 256:q * 256 + W],
                                         wt[:, u, k * 512 + (d % 4) * P:k * 512 + (d % 4 + 1) * P], hid[:, k, :],
                                         start=k == 0, stop=k == 3)
            x.then_inc(e_yt, 1)

        n = count(pe)
        pe.wait_ge(e_oh, 1)
        indices()
        pe.wait_ge(e_xg, 32)
        rows_in()
        with pe.Fori(0, n) as i:
            pe.wait_ge(e_xe, i * 3 + 3)
            for f in range(4):
                pe.wait_ge(e_h, i * 4 + (0 if f < 2 else f - 1))
                if f % 2 == 0:
                    pe.wait_ge(e_w[f], i * 16 + 16)
                    pe.wait_ge(e_w[f + 1], i * 16 + 16)
                gate_up(f)
                if f == 0:
                    pe.wait_ge(e_oh, i + 2)
                    pe.wait_ge(e_re, i * 4)
                    indices()
            pe.wait_ge(e_xg, i * 32 + 64)
            rows_in()
            for j in range(4):
                pe.wait_ge(e_ya if j % 2 == 0 else e_yd, i * 2 + j // 2)
                if j % 2 == 0:
                    pe.wait_ge(e_w[4 + j // 2], i * 16 + 16)
                if j == 0:
                    pe.wait_ge(e_h, i * 4 + 4)
                down(j)
            pe.wait_ge(e_xe, i * 3 + 6)
            pe.wait_ge(e_idx, i + 2)
            for c, m in ((0, P), (1, W2)):
                for h in range(2):
                    pe.wait_ge(e_ya, i * 2 + h + 1)
                    pe.wait_ge(e_yd, i * 2 + h + 1)
                    for k in range(4):
                        x = nc.tensor.transpose(bank[4 + 2 * c + h][0:m, k * P:(k + 1) * P],
                                                yT[:, 4 * h + k, c * P:c * P + m], ident[:])
                    x.then_inc(e_yr, 1)

    @blk.scalar
    def _(act):
        n = count(act)
        with act.Fori(0, n) as i:
            for f in range(4):
                act.wait_ge(e_gu, i * 4 + f + 1)
                nc.scalar.activation(sg[:, f % 2, :], bank[f % 2][:, 0:W], ACT.Silu).then_inc(e_si, 1)
            for j in (0, 2):
                act.wait_ge(e_yt, i * 4 + j + 1)
                nc.scalar.copy(yT[:, 2 * j:2 * j + 2, :],
                               bank[2][:, :].rearrange("p (q t) -> p q t", q=2)[:, :, 0:W]).then_inc(e_ya, 1)
            act.wait_ge(e_out, i * 32)
            for c, m in ((0, P), (1, W2)):
                for h in range(2):
                    act.wait_ge(e_yr, i * 4 + 2 * c + h + 1)
                    nc.scalar.copy(yr[0:m, c, h * 512:(h + 1) * 512], bank[4 + 2 * c + h][0:m, :]).then_inc(e_re, 1)

    @blk.vector
    def _(dve):
        def onehot(e):
            nc.vector.tensor_tensor(oh[:], iota_w[:].unsqueeze(1).broadcast_to([P, TT, W]),
                                    rank_m[:, bass.ds(e * TT, TT)].unsqueeze(2).broadcast_to([P, TT, W]),
                                    ALU.is_equal).then_inc(e_oh, 1)

        def lower(e):
            nc.vector.tensor_scalar(rank_m[:, bass.ds(e * TT, TT)], rank_m[:, bass.ds(e * TT, TT)], float(-W), None,
                                    ALU.add).then_inc(e_rk, 1)

        def indices(e, s):
            tok, second = bank[7][:, 0:3:2], bank[7][:, 1:4:2]
            nc.vector.tensor_copy(idx[:], tok)
            nc.vector.tensor_scalar(far[:], second, 0.0, float(4 * N), ALU.is_equal, ALU.mult).then_inc(e_far, 1)
            dve.wait_ge(e_far, s * 2 + 1)
            nc.vector.scalar_tensor_tensor(out=far[:], in0=tok, scalar=2.0, in1=far[:], op0=ALU.mult,
                                           op1=ALU.add).then_inc(e_far, 1)
            dve.wait_ge(e_far, s * 2 + 2)
            nc.vector.scalar_tensor_tensor(out=dest[:], in0=second, scalar=expert[:, bass.ds(e, 1)], in1=far[:],
                                           op0=ALU.is_equal, op1=ALU.add).then_inc(e_idx, 1)

        n = count(dve)
        nc.vector.memset(bank[7][:, 0:4], 0.0)
        onehot(0)
        dve.wait_ge(e_ix, 1)
        lower(0)
        indices(0, 0)

        def x_out(base):
            for h in range(2):
                dve.wait_ge(e_xt, base + h + 1)
                nc.vector.tensor_copy(xT[:, 4 * h:4 * h + 4, 0:P],
                                      bank[4 + h][:, :].rearrange("p (k t) -> p k t", t=P)).then_inc(e_xe, 1)
            dve.wait_ge(e_xt, base + 3)
            nc.vector.tensor_copy(xT[:, :, P:W],
                                  bank[6][:, 0:KC * W2].rearrange("p (k t) -> p k t", t=W2)).then_inc(e_xe, 1)

        x_out(0)
        with dve.Fori(0, n) as i:
            e = (i + 1) % NE
            dve.wait_ge(e_ix, i + 1)
            dve.wait_ge(e_rk, i + 1)
            onehot(e)
            for f in range(4):
                dve.wait_ge(e_si, i * 4 + f + 1)
                nc.vector.tensor_tensor(hid[:, f, :], sg[:, f % 2, :], bank[f % 2][:, 256:256 + W],
                                        ALU.mult).then_inc(e_h, 1)
                if f == 1:
                    dve.wait_ge(e_ix, i + 2)
                    dve.wait_ge(e_xg, i * 32 + 32)
                    lower(e)
                    dve.wait_ge(e_out, i * 32)
                    dve.wait_ge(e_idx, i + 1)
                    nc.vector.tensor_copy(dest_now[:], dest[:]).then_inc(e_now, 1)
                    dve.wait_ge(e_now, i + 1)
                    indices(e, i + 1)
            x_out(i * 3 + 3)
            for j in (1, 3):
                dve.wait_ge(e_yt, i * 4 + j + 1)
                nc.vector.tensor_copy(yT[:, 2 * j:2 * j + 2, :],
                                      bank[3][:, :].rearrange("p (q t) -> p q t", q=2)[:, :, 0:W]).then_inc(e_yd, 1)

    block.close()
    c3.close()


def b4_all(nc, A, O, sb, sem, bank, eps_c, x1, y_dram, w1, w2):
    c4 = ExitStack()
    B = 3
    yc = sb("yc", [P, B, 2, D], ctx=c4)
    ot = sb("ot", [P, B, D], ctx=c4)
    gfb = sb("gfb", [P, D], ctx=c4)
    ssq = sb("ssq4", [P, TT], ctx=c4)
    root = sb("root4", [P, TT], ctx=c4)
    rstd = sb("rstd4", [P, TT], ctx=c4)
    f_g = sem("f_g")
    f_y = [sem(f"f_y{j}") for j in range(B)]
    f_s, f_x2, f_ssq, f_root, f_r, f_o = [sem(x) for x in ("f_s", "f_x2", "f_ssq", "f_root", "f_r", "f_o")]
    f_out = [sem(f"f_out{j}") for j in range(B)]
    block = ExitStack()
    blk = block.enter_context(nc.Block())

    @blk.sync
    def _(sp):
        sp.dma_start(gfb[:], A["final_g"].rearrange("(o d) -> o d", o=1).broadcast_to([P, D])).then_inc(f_g, 16)
        y_view = y_dram.rearrange("(t c) d -> t c d", c=2)

        def load(i):
            if i >= B:
                sp.wait_ge(f_x2, i - B + 1)
            sp.dma_start(yc[0:ROWS[i], i % B, :, :], y_view[i * P:i * P + ROWS[i], :, :]).then_inc(f_y[i % B], 16)

        for i in range(B):
            load(i)
        for i in range(TT):
            if i + B < TT:
                load(i + B)
            sp.wait_ge(f_o, i + 1)
            dst = O[0][0, i * P:(i + 1) * P, :] if i < TT - 1 else O[1].rearrange("a t d -> (a t) d")
            sp.dma_start(dst, ot[0:ROWS[i], i % B, :]).then_inc(f_out[i % B], 16)
        for j in range(B):
            sp.wait_ge(f_out[j], 16 * len(range(j, TT, B)))

    @blk.vector
    def _(dve):
        def finish(i):
            r = ROWS[i]
            dve.wait_ge(f_root, i + 1)
            nc.vector.reciprocal(rstd[0:r, i:i + 1], root[0:r, i:i + 1]).then_inc(f_r, 1)
            dve.wait_ge(f_r, i + 1)
            nc.vector.scalar_tensor_tensor(out=ot[0:r, i % B, :], in0=x1[0:r, i, :], scalar=rstd[0:r, i:i + 1],
                                           in1=gfb[0:r, :], op0=ALU.mult, op1=ALU.mult).then_inc(f_o, 1)

        dve.wait_ge(f_g, 16)
        for i in range(TT):
            r = ROWS[i]
            dve.wait_ge(f_y[i % B], 16 * (i // B + 1))
            nc.vector.scalar_tensor_tensor(out=x1[0:r, i, :], in0=yc[0:r, i % B, 0, :], scalar=w1[0:r, i:i + 1],
                                           in1=x1[0:r, i, :], op0=ALU.mult, op1=ALU.add).then_inc(f_s, 1)
            dve.wait_ge(f_s, i + 1)
            nc.vector.scalar_tensor_tensor(out=x1[0:r, i, :], in0=yc[0:r, i % B, 1, :], scalar=w2[0:r, i:i + 1],
                                           in1=x1[0:r, i, :], op0=ALU.mult, op1=ALU.add).then_inc(f_x2, 1)
            if i >= 1:
                finish(i - 1)
        finish(TT - 1)

    @blk.scalar
    def _(act):
        for i in range(TT):
            r = ROWS[i]
            act.wait_ge(f_x2, i + 1)
            if i >= B:
                act.wait_ge(f_out[i % B], 16 * (i // B))
            nc.scalar.activation(ot[0:r, i % B, :], x1[0:r, i, :], ACT.Square, scale=D ** -0.5,
                                 accum_out=ssq[0:r, i:i + 1]).then_inc(f_ssq, 1)
            act.wait_ge(f_ssq, i + 1)
            nc.scalar.activation(root[0:r, i:i + 1], ssq[0:r, i:i + 1], ACT.Sqrt,
                                 bias=eps_c[0:r, :]).then_inc(f_root, 1)

    block.close()
    c4.close()


_INS = ["x_prompt", "x_sample", "state_pool", "state_gla", "norm1_g", "w_in", "w_gk2", "b_gk", "w_pool", "pool_scale",
        "gla_norm_g", "w_out", "norm2_g", "w_router_group", "b_router_group", "w_router_expert", "b_router_expert",
        "w_gate", "w_up", "w_down", "final_g"]
_OUTS = [(1, SEQ, D), (DEC_B, DEC_T, D), (1, 1, HIST, PW), (1, 1, HEADS, DK, DV), (1, DEC_B, HIST, PW),
         (1, DEC_B, HEADS, DK, DV)]


def kernel(**inputs):
    import numpy as _np
    import concourse.bacc as _bacc
    from concourse import mybir as _mybir
    from concourse.bass_utils import run_bass_kernel_spmd as _run

    nc = _bacc.Bacc("TRN2", target_bir_lowering=False, num_devices=1)
    arrays, args = {}, {}
    for name in _INS:
        a = _np.ascontiguousarray(inputs[name])
        arrays[f"in_{name}"] = a
        args[name] = nc.dram_tensor(f"in_{name}", a.shape, _mybir.dt.from_np(a.dtype), kind="ExternalInput").ap()
    outs = [nc.dram_tensor(f"out_{i}", s, F32, kind="ExternalOutput").ap() for i, s in enumerate(_OUTS)]
    program(nc, args, outs)
    r = _run(nc, [arrays], core_ids=[0])
    return tuple(r.results[0][f"out_{i}"] for i in range(len(_OUTS)))
```

```python
from contextlib import ExitStack

import concourse.bass as bass
from concourse import mybir
from concourse.alu_op_type import AluOpType as ALU

F32 = mybir.dt.float32
F32R = mybir.dt.float32r
BF16 = mybir.dt.bfloat16
FP16 = mybir.dt.float16
I32 = mybir.dt.int32
ACT = mybir.ActivationFunctionType
AX = mybir.AxisListType

P = 128
D = 1024
KC = D // P
SEQ = 1024
DEC_B, DEC_T = 8, 8
NS = DEC_B * DEC_T
N = SEQ + NS
TT = 9
ROWS = [P] * (TT - 1) + [NS]
BLK = [(0, 384), (384, 384), (768, 320)]
PW = 512
PG = 4
WINDOWS = (2, 4, 8, 16)
HIST = 15
U_P = 16
U_S = U_P + SEQ
SEG = HIST + DEC_T
U_W = U_S + DEC_B * SEG
HEADS = 4
DK, DV = 64, 128
LR = 16
NG, NE = 4, 16
DE = 512
EPS = 1e-6
GATE = 16.0
CLAMP = 80.0 * GATE
SB = 32

W = 160
W2 = W - P
ROUNDS = -(-N // W)


def program(nc, A, O):
    C_U, C_Q, C_K, C_V, C_G, C_L = 0, 512, 768, 1024, 1536, 2048
    w_in = A["w_in"].rearrange("l (k p) n -> p (l k) n", p=P)
    w_out = A["w_out"].rearrange("l (k p) n -> p (l k) n", p=P)
    x_rows = [A["x_prompt"][0, i * P:(i + 1) * P, :] for i in range(TT - 1)]
    x_rows.append(A["x_sample"].rearrange("a t d -> (a t) d"))
    h2_dram = nc.dram_tensor("h2_rows", [N, D], F32).ap()
    y_dram = nc.dram_tensor("expert_rows", [N * 2, D], F32).ap()

    with ExitStack() as whole:
        def sb(name, shape, dt=F32, ctx=whole):
            return ctx.enter_context(nc.sbuf_tensor(name, shape, dt))

        def sem(name):
            return whole.enter_context(nc.semaphore(name))

        bank = [whole.enter_context(nc.psum_tensor(f"bank{i}", [P, 512], F32)) for i in range(8)]

        ident = sb("ident", [P, P])
        onesf = sb("onesf", [P, P])
        eps_c = sb("eps_c", [P, 1])

        w1 = sb("w1", [P, TT])
        w2 = sb("w2", [P, TT])
        rank_m = sb("rank_m", [P, NE * TT])
        token = sb("token", [P, TT, 2], FP16)
        expert = sb("expert", [P, NE])
        iota_w = sb("iota_w", [P, W])
        steps = sb("steps", [1, 1], I32)
        x1 = sb("x1", [P, TT, D])

        uT = sb("uT", [P, PG, U_W])
        gT = sb("gT", [P, HEADS, N])
        ring = sb("ring", [P, 4, KC, 256])

        S0 = sb("S0", [P, DEC_B, 2, DV])
        Sp = sb("Sp", [P, 2, DV])
        s_w = [sem(f"s_w{j}") for j in range(4)]

        b1_all(nc, A, O, S0, Sp, s_w, sb, sem, bank, ident, onesf, eps_c, uT, gT, ring, x1, w_in, w_out, x_rows,
               (C_U, C_Q, C_K, C_V, C_G, C_L))

        wdn = sb("wdn", [P, 2, 2048])
        e_w = [sem(f"e_w{u}") for u in range(6)]

        b2_all(nc, A, O, S0, Sp, s_w, sb, sem, e_w, wdn, bank, ident, onesf, eps_c, uT, gT, ring, x1, x_rows, h2_dram,
               w1, w2, rank_m, token, expert, iota_w, steps)
        b3_all(nc, A, sb, sem, e_w, ring, wdn, bank, ident, h2_dram, y_dram, rank_m, token, expert, iota_w, steps)
        b4_all(nc, A, O, sb, sem, bank, eps_c, x1, y_dram, w1, w2)


def b1_all(nc, A, O, S0, Sp, s_w, sb, sem, bank, ident, onesf, eps_c, uT, gT, ring, x1, w_in, w_out, x_rows, cols):
    C_U, C_Q, C_K, C_V, C_G, C_L = cols
    c1 = ExitStack()
    POOL_AT = U_W - U_P
    scratch = x1[:, :, :].rearrange("p a b -> p (a b)")
    hT = sb("hT", [P, KC, N], ctx=c1)
    qT = sb("qT", [P, 2, N], ctx=c1)
    kT = sb("kT", [P, 2, N], ctx=c1)
    bT = scratch[:, 5120:5120 + 2 * N].rearrange("p (a t) -> p a t", a=2)
    v = sb("v", [P, TT, 512], ctx=c1)
    lr_or_decay = sb("lr_or_decay", [P, N], ctx=c1)
    lrT = lr_or_decay[0:LR, :]
    X_AT = (0, 1, 2, 5, 6)
    xn = x1[:, 3:5, :]
    ssq = sb("ssq", [P, TT], ctx=c1)
    rstd = sb("rstd", [P, 2 * TT], ctx=c1)
    g1b = sb("g1b", [P, D], ctx=c1)
    wlr = sb("wlr", [P, KC, LR], ctx=c1)
    wgk2 = sb("wgk2", [LR, 256], ctx=c1)
    bgk = sb("bgk", [P, 2], ctx=c1)
    pscale = sb("pscale", [P, PG], ctx=c1)
    gnorm = sb("gnorm", [P, 1], ctx=c1)
    wpool = sb("wpool", [P, PG, P], ctx=c1)
    tmpa = sb("tmpa", [P, N], ctx=c1)
    T1even = sb("T1", [P, 3, 2, P], ctx=c1)
    T1s = [T1even[:, :, :, :], lr_or_decay[:, 0:768].rearrange("p (w a t) -> p w a t", w=3, a=2)]
    T2s = [t.rearrange("p (a i t) -> p a i t", a=2, i=4) for t in (xn[:, 1, :], g1b[:, :])]
    Pm = scratch[:, 8320:8832].rearrange("p (h t) -> p h t", h=HEADS)
    khN = scratch[:, 8832:9088].rearrange("p (a d) -> p a d", a=2)
    o2 = scratch[:, 7296:7808]
    hist = o2[0:DEC_B * HIST, :]
    qz = xn[:, 0, :].rearrange("p (w h t) -> p w h t", w=2, h=HEADS)
    KM = xn[0:NS, :, :].rearrange("p a (b d) -> p (a b) d", d=256)
    rs = scratch[:, 7808:8320]
    rmid = sb("rmid", [P, 2, SEQ // SB], ctx=c1)
    mask_p = sb("mask_p", [P, P], ctx=c1)
    mask_s = sb("mask_s", [NS, NS], ctx=c1)
    bmask = sb("bmask", [NS, DEC_B], ctx=c1)
    resets = sb("resets", [P, NS], ctx=c1)
    onesN = sb("onesN", [P, P], ctx=c1)
    icnt = sb("icnt", [P, 16], ctx=c1)
    sdecs = sb("sdec", [P, 2, 2], ctx=c1)
    o_dec = sb("o_dec", [P, 2, DEC_B], ctx=c1)
    npS = tmpa[0:NS, 256:768]
    npP = scratch[0:HIST, 2 * POOL_AT:2 * POOL_AT + 512]
    wsum = [scratch[:, POOL_AT * j:POOL_AT * (j + 1)] for j in range(2)]
    edge = scratch[:, 9088:9088 + 96]

    s_const = sem("s_const")
    s_x = [sem(f"s_x{j}") for j in range(5)]
    s_g1 = sem("s_g1")
    s_ku = sem("s_ku")
    s_ssq, s_rt, s_rstd, s_xn = sem("s_ssq"), sem("s_rt"), sem("s_rstd"), sem("s_xn")
    s_tr = sem("s_tr")
    s_tra, s_trd = sem("s_tra"), sem("s_trd")
    s_wlr = sem("s_wlr")
    s_grp = sem("s_grp")
    s_eva, s_evd = sem("s_eva"), sem("s_evd")
    s_gc = sem("s_gc")
    s_hist, s_histev = sem("s_hist"), sem("s_histev")
    s_za, s_b = sem("s_za"), sem("s_b")
    s_d = sem("s_d")
    s_args, s_exp, s_kq, s_score = sem("s_args"), sem("s_exp"), sem("s_kq"), sem("s_score")
    s_khn, s_pm, s_o, s_sq, s_ms, s_rs, s_on, s_st = [sem(x) for x in (
        "s_khn", "s_pm", "s_o", "s_sq", "s_ms", "s_rs", "s_on", "s_st")]
    s_pool, s_pmix = sem("s_pool"), sem("s_pmix")
    s_np, s_npev, s_npo = sem("s_np"), sem("s_npev"), sem("s_npo")
    s_km, s_us = sem("s_km"), sem("s_us")
    s_s0, s_silu, s_fin = sem("s_s0"), sem("s_silu"), sem("s_fin")
    s_a = sem("s_a")

    groups = [(kind, m, b) for b in range(3) for kind, m in (("lr", 0), ("k", 0), ("k", 1))]
    groups += [("z", p, b) for p in range(2) for b in range(3)] + [("q", p, b) for p in range(2) for b in range(3)]
    groups += [("v", 0, t) for t in range(TT)]
    g_list = [("g", m, b) for m in range(4) for b in range(3)]
    between = [[[("u", c, b)] for b in range(3)] for c in range(4)]
    between += [[[g_list[2 * c]], [g_list[2 * c + 1]], [("mix", c, b) for b in range(3)]] for c in range(4)]
    between += [[[g_list[8]], [g_list[9]], g_list[10:12]]]
    groups += [g for chunk in between for part in chunk for g in part]
    index = {g: n for n, g in enumerate(groups)}
    ON_ACT = {"lr", "k", "q", "u", "mix"}
    unit = {"k": 0, "q": 1, "v": 2, "u": 4, "g": 6}

    def evacs(n, on_act):
        return sum((g[0] in ON_ACT) == on_act for g in groups[:n + 1])

    def out_sem(n):
        on_act = groups[n][0] in ON_ACT
        return (s_eva if on_act else s_evd), evacs(n, on_act)

    def acc(n):
        return bank[5 + n % 3]

    def pooled(m):
        return wsum[m % 2][:, 0:N]

    block = ExitStack()
    blk = block.enter_context(nc.Block())

    @blk.gpsimd
    def _(pool):
        nc.gpsimd.memset(ident[:], 0.0).then_inc(s_gc, 1)
        nc.gpsimd.memset(mask_p[:], 1.0).then_inc(s_gc, 1)
        nc.gpsimd.memset(mask_s[:], 1.0).then_inc(s_gc, 1)
        nc.gpsimd.memset(bmask[:], 1.0).then_inc(s_gc, 1)
        nc.gpsimd.memset(resets[:], 1.0).then_inc(s_gc, 1)
        nc.gpsimd.memset(onesf[:], 1.0).then_inc(s_gc, 1)
        nc.gpsimd.memset(onesN[:], 1.0 / DV).then_inc(s_gc, 1)
        nc.gpsimd.memset(eps_c[:], EPS).then_inc(s_gc, 1)
        nc.gpsimd.memset(Pm, 0.0).then_inc(s_gc, 1)
        nc.gpsimd.memset(uT[:, :, 0:U_P], 0.0).then_inc(s_gc, 1)
        nc.gpsimd.iota(icnt[:], [[1, 16]], base=1, channel_multiplier=0,
                       allow_small_or_imprecise_dtypes=True).then_inc(s_gc, 1)
        pool.wait_ge(s_gc, 11)
        nc.gpsimd.affine_select(out=ident[:], in_=ident[:], pattern=[[-1, P]], compare_op=ALU.not_equal, fill=1.0,
                                base=0, channel_multiplier=1).then_inc(s_gc, 1)
        nc.gpsimd.affine_select(out=mask_p[:], in_=mask_p[:], pattern=[[1, P]], compare_op=ALU.is_ge, fill=0.0,
                                base=0, channel_multiplier=-1).then_inc(s_gc, 1)
        nc.gpsimd.affine_select(out=mask_s[:], in_=mask_s[:], pattern=[[1, NS]], compare_op=ALU.is_ge, fill=0.0,
                                base=0, channel_multiplier=-1).then_inc(s_gc, 1)
        nc.gpsimd.affine_select(out=bmask[:], in_=bmask[:], pattern=[[-DEC_T, DEC_B]], compare_op=ALU.is_ge,
                                fill=0.0, base=0, channel_multiplier=1).then_inc(s_gc, 1)
        nc.gpsimd.memset(resets[:].rearrange("p (b t) -> p b t", t=DEC_T)[:, :, 0:1], 0.0).then_inc(s_gc, 1)
        pool.wait_ge(s_gc, 16)
        nc.gpsimd.affine_select(out=bmask[:], in_=bmask[:], pattern=[[DEC_T, DEC_B]], compare_op=ALU.is_ge,
                                fill=0.0, base=DEC_T - 1, channel_multiplier=-1).then_inc(s_gc, 1)
        nc.gpsimd.affine_select(out=mask_s[:].rearrange("s (b t) -> s b t", t=DEC_T),
                                in_=mask_s[:].rearrange("s (b t) -> s b t", t=DEC_T),
                                pattern=[[-DEC_T, DEC_B], [0, DEC_T]], compare_op=ALU.is_ge, fill=0.0, base=0,
                                channel_multiplier=1).then_inc(s_gc, 1)
    GC = 18

    @blk.sync
    def _(sp):
        def load_x(i):
            if i >= 5:
                sp.wait_ge(s_xn, i - 4)
            sp.dma_start(x1[0:ROWS[i], X_AT[i % 5], :], x_rows[i]).then_inc(s_x[i % 5], 16)

        def load_unit(n, src):
            sp.dma_start(ring[:, n % 4, :, :], src).then_inc(s_w[n % 4], 16)

        units = [C_K, C_Q, C_V, C_V + 256, C_U, C_U + 256, C_G, C_G + 256]
        load_x(0)
        sp.dma_start(g1b[:], A["norm1_g"].broadcast_to([P, D])).then_inc(s_g1, 16)
        load_x(1)
        load_x(2)
        sp.dma_start(wlr[:], w_in[:, :, C_L:C_L + LR]).then_inc(s_wlr, 16)
        load_unit(0, w_in[:, :, units[0]:units[0] + 256])
        for i in range(3, TT):
            load_x(i)
        with nc.allow_non_contiguous_dma(reason="small vectors, one value a partition"):
            sp.dma_start(bgk[:], A["b_gk"].rearrange("l (a p) -> p (l a)", p=P)).then_inc(s_const, 16)
            sp.dma_start(pscale[:], A["pool_scale"].rearrange("l (a p) -> p (l a)", p=P)).then_inc(s_const, 16)
            sp.dma_start(gnorm[:], A["gla_norm_g"].rearrange("l p -> p l")).then_inc(s_const, 16)
        sp.dma_start(wgk2[:], A["w_gk2"][0]).then_inc(s_const, 16)
        sp.dma_start(wpool[:], A["w_pool"][0].rearrange("g c d -> c g d")).then_inc(s_const, 16)
        sp.dma_start(hist, A["state_pool"][0].rearrange("b t c -> (b t) c")).then_inc(s_const, 16)
        for u in range(1, 4):
            load_unit(u, w_in[:, :, units[u]:units[u] + 256])
        for a in range(2):
            sp.dma_start(S0[64 * a:64 * a + 64, :, :, :],
                         A["state_gla"][0].rearrange("b (p a) k v -> a k b p v", a=2)[a]).then_inc(s_s0, 16)
        for b in range(DEC_B):
            sp.dma_start(O[4][0, b, 0:HIST - DEC_T, :], A["state_pool"][0, b, DEC_T:HIST, :]).then_inc(s_npo, 16)
        last = [index[("k", 1, 2)], index[("q", 1, 2)], index[("v", 0, 8)], index[("v", 0, 8)],
                index[("u", 1, 2)], index[("u", 3, 2)], index[("g", 1, 2)], index[("g", 3, 2)]]
        for n in range(4, 12):
            sp.wait_ge(s_grp, last[n - 4] + 1)
            if n < 8:
                load_unit(n, w_in[:, :, units[n]:units[n] + 256])
            else:
                load_unit(n, w_out[:, :, (n - 8) * 256:(n - 7) * 256])
        sp.wait_ge(s_npev, 1)
        sp.dma_start(O[2][0, 0], npP).then_inc(s_npo, 16)
        for b in range(DEC_B):
            sp.dma_start(O[4][0, b, HIST - DEC_T:HIST, :], npS[b * DEC_T:(b + 1) * DEC_T, :]).then_inc(s_npo, 16)
        sp.wait_ge(s_npo, 16 * (2 * DEC_B + 1))

    @blk.tensor
    def _(pe):
        def turn(i):
            r = ROWS[i]
            pe.wait_ge(s_xn, i + 1)
            for h in range(2):
                if i >= 2:
                    pe.wait_ge(s_trd if h else s_tra, i - 1)
                for k in range(4):
                    t = nc.tensor.transpose(bank[2 * (i % 2) + h][:, k * P:k * P + r],
                                            xn[0:r, i % 2, (4 * h + k) * P:(4 * h + k + 1) * P], ident[0:r, 0:r])
                t.then_inc(s_tr, 1)

        def group(kind, m, b):
            n = index[(kind, m, b)]
            if n >= 3:
                s, c = out_sem(n - 3)
                pe.wait_ge(s, c)
            if kind in unit:
                u = unit[kind] + (0 if kind in "kqv" else m // 2)
                pe.wait_ge(s_w[u % 4], 16 * (u // 4 + 1))
                if kind == "v":
                    pe.wait_ge(s_w[3], 16)
            if kind == "lr":
                t0, tn = BLK[b]
                for k in range(KC):
                    mm = nc.tensor.matmul(acc(n)[0:LR, 0:tn], wlr[:, k, :], hT[:, k, t0:t0 + tn],
                                          start=k == 0, stop=k == KC - 1)
            elif kind == "z":
                t0, tn = BLK[b]
                mm = nc.tensor.matmul(acc(n)[:, 0:tn], wgk2[:, m * P:(m + 1) * P], lrT[:, t0:t0 + tn],
                                      start=True, stop=True)
            elif kind == "mix":
                t0, tn = BLK[b]
                mm = nc.tensor.matmul(acc(n)[:, 0:tn], wpool[:, m, :], pooled(m)[:, t0:t0 + tn],
                                      start=True, stop=True)
            elif kind == "v":
                r = ROWS[b]
                for k in range(KC):
                    mm = nc.tensor.matmul(acc(n)[0:r, :], hT[:, k, b * P:b * P + r], ring[:, 2:4, k, :],
                                          start=k == 0, stop=k == KC - 1)
            else:
                t0, tn = BLK[b]
                c0 = (m % 2) * P
                for k in range(KC):
                    mm = nc.tensor.matmul(acc(n)[:, 0:tn], ring[:, u % 4, k, c0:c0 + P], hT[:, k, t0:t0 + tn],
                                          start=k == 0, stop=k == KC - 1)
            mm.then_inc(s_grp, 1)

        pe.wait_ge(s_gc, GC)
        for i in range(3):
            turn(i)
        for b in range(3):
            if b < 2:
                turn(3 * b + 3)
            pe.wait_ge(s_tra, 3 * b + 3)
            pe.wait_ge(s_trd, 3 * b + 3)
            if b == 0:
                pe.wait_ge(s_wlr, 16)
            group("lr", 0, b)
            if b < 2:
                turn(3 * b + 4)
            group("k", 0, b)
            if b < 2:
                turn(3 * b + 5)
            group("k", 1, b)
        pe.wait_ge(s_const, 16 * 6)
        for m in range(PG):
            t = nc.tensor.transpose(bank[0][:, m * P:m * P + DEC_B * HIST], hist[:, m * P:(m + 1) * P],
                                    ident[0:DEC_B * HIST, 0:DEC_B * HIST])
        t.then_inc(s_hist, 1)
        pe.wait_ge(s_eva, evacs(index[("lr", 0, 2)], True))
        for m in range(2):
            for b in range(3):
                group("z", m, b)
        for m in range(2):
            for b in range(3):
                group("q", m, b)
        for t in range(TT):
            group("v", 0, t)

        def attend_scores(c):
            T1, T2 = T1s[c % 2], T2s[c % 2]
            n = ROWS[c]
            if c >= 1:
                pe.wait_ge(s_pm, c)
                pe.wait_ge(s_khn, c)
            else:
                pe.wait_ge(s_histev, 1)
            pe.wait_ge(s_kq, c + 1)
            for h in range(HEADS):
                p = h // 2
                if c < TT - 1:
                    for i in range(4):
                        m = SB * (i + 1)
                        nc.tensor.matmul(bank[0][0:m, h * P + SB * i:h * P + SB * (i + 1)], T2[:, p, i, 0:m],
                                         qz[:, 0, h, SB * i:SB * (i + 1)], start=True, stop=True)
                else:
                    nc.tensor.matmul(bank[0][0:n, h * P:h * P + n], T2[:, p, 0, 0:n], qz[:, 0, h, 0:n],
                                     start=True, stop=True)
            for p in range(2):
                t = nc.tensor.transpose(bank[1][0:n, p * P:(p + 1) * P], T1[:, 2, p, 0:n], ident[:])
            t.then_inc(s_score, 1)

        def attend_out(c):
            n = ROWS[c]
            if c == TT - 1:
                pe.wait_ge(s_s0, 32)
            pe.wait_ge(s_pm, c + 1)
            pe.wait_ge(s_khn, c + 1)
            if c >= 1:
                pe.wait_ge(s_st, c)
                pe.wait_ge(s_on, c)
            for h in range(HEADS):
                p = h // 2
                o = nc.tensor.matmul(bank[2][:, h * P:h * P + n], v[0:n, c, h * DV:(h + 1) * DV], Pm[0:n, h, 0:n],
                                     start=h == 0 or c < TT - 1, stop=c == 0, skip_group_check=c == TT - 1)
                if c < TT - 1:
                    if c > 0:
                        o = nc.tensor.matmul(bank[2][:, h * P:h * P + n], Sp[:, p, :], qz[:, 1, h, 0:n],
                                             start=False, stop=True)
            if c == TT - 1:
                for b in range(DEC_B):
                    t0 = b * DEC_T
                    for p in range(2):
                        o = nc.tensor.matmul(
                            bank[2][:, 2 * p * P:2 * (p + 1) * P].rearrange("v (a t) -> v a t", a=2)[:, :, t0:t0 + DEC_T],
                            S0[:, b, p, :], qz[:, 1, 2 * p:2 * p + 2, t0:t0 + DEC_T], start=False, stop=True,
                            skip_group_check=True)
            if c < TT - 1:
                for p in range(2):
                    o = nc.tensor.matmul(bank[3][:, p * 256:(p + 1) * 256], khN[:, p, :],
                                         v[:, c, p * 256:(p + 1) * 256], start=True, stop=True)
            o.then_inc(s_o, 1)

        def attend_norm(c):
            n = ROWS[c]
            pe.wait_ge(s_sq, c + 1)
            if c >= 1:
                pe.wait_ge(s_rs, c)
            nc.tensor.matmul(bank[4][:, :], onesN[:], o2, start=True,
                             stop=True).then_inc(s_ms, 1)

        def rows_of_state():
            pe.wait_ge(s_eva, evacs(index[("u", 3, 2)], True))
            pe.wait_ge(s_pm, 4)
            pe.wait_ge(s_khn, 4)
            for m in range(PG):
                nc.tensor.transpose(bank[0][0:HIST, m * P:(m + 1) * P], uT[:, m, U_S - HIST:U_S], ident[:])
                t = nc.tensor.transpose(bank[1][0:NS, m * P:(m + 1) * P], tmpa[:, m * NS:(m + 1) * NS], ident[:])
            t.then_inc(s_np, 1)

        def fill(c, part):
            for kind, m, b in between[c][part]:
                if kind == "mix" and b == 0:
                    pe.wait_ge(s_pool, m + 1)
                group(kind, m, b)

        for c in range(TT):
            if c == 4:
                rows_of_state()
            fill(c, 0)
            if c == 4:
                pe.wait_ge(s_npev, 1)
            attend_scores(c)
            fill(c, 1)
            attend_out(c)
            fill(c, 2)
            attend_norm(c)
        pe.wait_ge(s_km, 1)
        for b in range(DEC_B):
            if b >= 2:
                pe.wait_ge(s_us, b - 1)
            for p in range(2):
                t = nc.tensor.matmul(bank[[0, 3][b % 2]][:, p * 256:(p + 1) * 256], KM[:, b, p * P:(p + 1) * P],
                                     v[0:NS, TT - 1, p * 256:(p + 1) * 256], start=True, stop=True)
            t.then_inc(s_ku, 1)

    @blk.scalar
    def _(act):
        def square(i):
            r = ROWS[i]
            act.wait_ge(s_x[i % 5], 16 * (i // 5 + 1))
            nc.scalar.activation(tmpa[0:r, 0:D], x1[0:r, X_AT[i % 5], :], ACT.Square, scale=D ** -0.5,
                                 accum_out=ssq[0:r, i:i + 1]).then_inc(s_ssq, 1)
            act.wait_ge(s_ssq, i + 1)
            nc.scalar.activation(rstd[0:r, TT + i:TT + i + 1], ssq[0:r, i:i + 1], ACT.Sqrt,
                                 bias=eps_c[0:r, :]).then_inc(s_rt, 1)

        def turned(i):
            act.wait_ge(s_tr, 2 * i + 1)
            nc.scalar.copy(hT[:, 0:4, i * P:i * P + ROWS[i]],
                           bank[2 * (i % 2)][:, :].rearrange("p (k t) -> p k t", t=P)[:, :, 0:ROWS[i]]).then_inc(s_tra, 1)

        def evac(kind, m, b):
            n = index[(kind, m, b)]
            act.wait_ge(s_grp, n + 1)
            t0, tn = BLK[b]
            a = acc(n)
            if kind == "lr":
                nc.scalar.copy(lrT[:, t0:t0 + tn], a[0:LR, 0:tn]).then_inc(s_eva, 1)
            elif kind == "k":
                nc.scalar.copy(kT[:, m, t0:t0 + tn], a[:, 0:tn]).then_inc(s_eva, 1)
            elif kind == "q":
                nc.scalar.mul(qT[:, m, t0:t0 + tn], a[:, 0:tn], DK ** -0.5).then_inc(s_eva, 1)
            elif kind == "u":
                pn = min(tn, SEQ - t0)
                if pn == tn:
                    nc.scalar.copy(uT[:, m, U_P + t0:U_P + t0 + tn], a[:, 0:tn]).then_inc(s_eva, 1)
                else:
                    nc.scalar.copy(uT[:, m, U_P + t0:U_P + t0 + pn], a[:, 0:pn])
                    nc.scalar.copy(tmpa[:, m * NS:(m + 1) * NS], a[:, pn:tn])
                    nc.scalar.copy(uT[:, m, U_S:].rearrange("p (b t) -> p b t", t=SEG)[:, :, HIST:],
                                   a[:, pn:tn].rearrange("p (b t) -> p b t", t=DEC_T)).then_inc(s_eva, 1)
            elif kind == "mix":
                nc.scalar.activation(uT[:, m, t0:t0 + tn], a[:, 0:tn], ACT.Copy,
                                     scale=pscale[:, m:m + 1]).then_inc(s_eva, 1)

        act.wait_ge(s_gc, GC)
        for i in range(TT):
            square(i)
            if i >= 1:
                turned(i - 1)
            if i in (5, 8):
                for kind, m in (("lr", 0), ("k", 0), ("k", 1)):
                    evac(kind, m, i // 3 - 1)
        turned(TT - 1)
        for kind, m in (("lr", 0), ("k", 0), ("k", 1)):
            evac(kind, m, 2)
        act.wait_ge(s_hist, 1)
        nc.scalar.copy(uT[:, :, U_S:].rearrange("p m (b t) -> p m b t", t=SEG)[:, 0:2, :, 0:HIST],
                       bank[0][:, :].rearrange("p (m x) -> p m x", m=PG)[:, 0:2, 0:DEC_B * HIST].rearrange(
                           "p m (b t) -> p m b t", t=HIST))
        nc.scalar.copy(uT[:, :, U_S:].rearrange("p m (b t) -> p m b t", t=SEG)[:, 2:4, :, 0:HIST],
                       bank[0][:, :].rearrange("p (m x) -> p m x", m=PG)[:, 2:4, 0:DEC_B * HIST].rearrange(
                           "p m (b t) -> p m b t", t=HIST)).then_inc(s_histev, 1)
        for m in range(2):
            act.wait_ge(s_evd, 3 * m + 3)
            if m:
                act.wait_ge(s_b, m)
            nc.scalar.activation(tmpa[:], bT[:, m, :], ACT.Abs).then_inc(s_a, 1)
            act.wait_ge(s_a, 2 * m + 1)
            nc.scalar.activation(tmpa[:], tmpa[:], ACT.Exp, scale=-1.0).then_inc(s_a, 1)
            act.wait_ge(s_a, 2 * m + 2)
            nc.scalar.activation(tmpa[:], tmpa[:], ACT.Ln, bias=1.0).then_inc(s_za, 1)
        for m in range(2):
            for b in range(3):
                evac("q", m, b)

        def exps(c):
            n = ROWS[c]
            T1, T2 = T1s[c % 2], T2s[c % 2]
            act.wait_ge(s_args, c + 1)
            if c < TT - 1:
                nc.scalar.activation(T1.rearrange("p a b t -> p (a b t)"),
                                     T1.rearrange("p a b t -> p (a b t)"), ACT.Exp, scale=1.0 / GATE)
                nc.scalar.activation(T2.rearrange("p a b t -> p (a b t)"),
                                     T2.rearrange("p a b t -> p (a b t)"), ACT.Exp,
                                     scale=1.0 / GATE).then_inc(s_exp, 1)
            else:
                nc.scalar.activation(T1[:, :, :, 0:n].rearrange("p a b t -> p (a b) t"),
                                     T1[:, :, :, 0:n].rearrange("p a b t -> p (a b) t"), ACT.Exp, scale=1.0 / GATE)
                nc.scalar.activation(T2[:, :, 0, 0:n], T2[:, :, 0, 0:n], ACT.Exp, scale=1.0 / GATE).then_inc(s_exp, 1)

        def keys_rows(c):
            n = ROWS[c]
            act.wait_ge(s_score, c + 1)
            nc.scalar.copy(khN[0:n, :, :], bank[1][0:n, 0:256].rearrange("p (a d) -> p a d", a=2)).then_inc(s_khn, 1)

        def squares(c):
            act.wait_ge(s_o, c + 1)
            nc.scalar.activation(o2 if ROWS[c] == P else o2.rearrange("p (h t) -> p h t", h=HEADS)[:, :, 0:NS],
                                 bank[2][:, :] if ROWS[c] == P else
                                 bank[2][:, :].rearrange("p (h t) -> p h t", h=HEADS)[:, :, 0:NS],
                                 ACT.Square).then_inc(s_sq, 1)

        def inv_root(c):
            act.wait_ge(s_ms, c + 1)
            if c >= 1:
                act.wait_ge(s_on, c)
            nc.scalar.activation(rs, bank[4][:, :], ACT.Ln, bias=eps_c[:]).then_inc(s_a, 1)
            act.wait_ge(s_a, 5 + c)
            nc.scalar.activation(rs, rs, ACT.Exp, scale=-0.5).then_inc(s_rs, 1)

        def fill(c, part):
            for g in between[c][part]:
                if g[0] in ON_ACT:
                    evac(*g)

        def silu(m):
            nc.scalar.activation(gT[:, m, :], gT[:, m, :], ACT.Silu).then_inc(s_silu, 1)

        exps(0)
        exps(1)
        for c in range(TT):
            if c == 4:
                act.wait_ge(s_np, 1)
                nc.scalar.copy(npP, bank[0][0:HIST, :])
                nc.scalar.copy(npS, bank[1][0:NS, :]).then_inc(s_npev, 1)
            fill(c, 0)
            keys_rows(c)
            if c == TT - 1:
                act.wait_ge(s_evd, out_sem(index[("g", 2, 2)])[1])
                for m in range(3):
                    silu(m)
            fill(c, 1)
            squares(c)
            fill(c, 2)
            inv_root(c)
            if c + 2 < TT:
                exps(c + 2)
        act.wait_ge(s_evd, evacs(len(groups) - 1, False))
        silu(3)

    @blk.vector
    def _(dve):
        chain = [0]

        def link(ins):
            chain[0] += 1
            ins.then_inc(s_d, 1)
            dve.wait_ge(s_d, chain[0])

        dve.wait_ge(s_gc, GC)
        link(nc.vector.reciprocal(icnt[:], icnt[:]))

        def turned(i):
            dve.wait_ge(s_tr, 2 * i + 2)
            nc.vector.tensor_copy(hT[:, 4:8, i * P:i * P + ROWS[i]],
                                  bank[2 * (i % 2) + 1][:, :].rearrange("p (k t) -> p k t", t=P)[:, :, 0:ROWS[i]]
                                  ).then_inc(s_trd, 1)

        for i in range(TT):
            r = ROWS[i]
            dve.wait_ge(s_rt, i + 1)
            link(nc.vector.reciprocal(rstd[0:r, i:i + 1], rstd[0:r, TT + i:TT + i + 1]))
            if i == 0:
                dve.wait_ge(s_g1, 16)
            if i >= 2:
                dve.wait_ge(s_tr, 2 * (i - 1))
            nc.vector.scalar_tensor_tensor(out=xn[0:r, i % 2, :], in0=x1[0:r, X_AT[i % 5], :],
                                           scalar=rstd[0:r, i:i + 1], in1=g1b[0:r, :], op0=ALU.mult,
                                           op1=ALU.mult).then_inc(s_xn, 1)
            if i >= 1:
                turned(i - 1)
        turned(TT - 1)
        dve.wait_ge(s_const, 16 * 6)

        def evac(kind, m, b):
            n = index[(kind, m, b)]
            dve.wait_ge(s_grp, n + 1)
            a = acc(n)
            if kind == "v":
                nc.vector.tensor_copy(v[0:ROWS[b], b, :], a[0:ROWS[b], :]).then_inc(s_evd, 1)
                return
            t0, tn = BLK[b]
            if kind == "z":
                nc.vector.tensor_scalar(bT[:, m, t0:t0 + tn], a[:, 0:tn], bgk[:, m:m + 1], None,
                                        ALU.add).then_inc(s_evd, 1)
            else:
                nc.vector.tensor_copy(gT[:, m, t0:t0 + tn], a[:, 0:tn]).then_inc(s_evd, 1)

        for m in range(2):
            for b in range(3):
                evac("z", m, b)
        for m in range(2):
            dve.wait_ge(s_za, m + 1)
            nc.vector.scalar_tensor_tensor(out=bT[:, m, :], in0=bT[:, m, :], scalar=0.0, in1=tmpa[:], op0=ALU.min,
                                           op1=ALU.subtract).then_inc(s_b, 1)
            dve.wait_ge(s_b, m + 1)
        for c in range(TT):
            for m in range(2):
                n = ROWS[c]
                sl = bT[:, m, c * P:c * P + n]
                ch = nc.vector.tensor_tensor_scan(sl, onesf[:, 0:n] if n == P else resets[:], sl, 0.0,
                                                  ALU.mult, ALU.add)
        link(ch)
        link(nc.vector.tensor_copy(rmid[:, :, :],
                                   bT[:, :, 0:SEQ].rearrange("p a (i t) -> p a i t", t=SB)[:, :, :, SB // 2 - 1]))

        def args(c):
            n = ROWS[c]
            B = bT[:, :, c * P:c * P + n]
            T1, T2 = T1s[c % 2], T2s[c % 2]
            if c >= 2:
                dve.wait_ge(s_score, c - 1)
            if c < TT - 1:
                r = rmid[:, :, 4 * c:4 * c + 4]
                nc.vector.tensor_tensor(T1[:, 0, :, :].rearrange("p a (i t) -> p a i t", t=SB),
                                        B.rearrange("p a (i t) -> p a i t", t=SB),
                                        r.unsqueeze(3).broadcast_to([P, 2, 4, SB]), ALU.subtract)
                nc.vector.tensor_copy(T1[:, 1, :, :], B)
                nc.vector.tensor_tensor(T1[:, 2, :, :], B[:, :, P - 1:P].broadcast_to([P, 2, P]), B, ALU.subtract)
                for p in range(2):
                    link(nc.vector.tensor_tensor(T2[:, p, :, :], r[:, p, :].unsqueeze(2).broadcast_to([P, 4, P]),
                                                 B[:, p, :].unsqueeze(1).broadcast_to([P, 4, P]), ALU.subtract))
                nc.vector.tensor_scalar(T1[:, 0, :, :], T1[:, 0, :, :], CLAMP, -CLAMP, ALU.min, ALU.max)
                nc.vector.tensor_scalar(T2, T2, CLAMP, -CLAMP, ALU.min,
                                        ALU.max).then_inc(s_args, 1)
            else:
                nc.vector.tensor_scalar(T1[:, 0, :, 0:n], B, CLAMP, -CLAMP, ALU.min, ALU.max)
                nc.vector.tensor_copy(T1[:, 1, :, 0:n], B)
                for p in range(2):
                    bl = B[:, p, :].rearrange("p (b t) -> p b t", t=DEC_T)
                    nc.vector.tensor_tensor(T1[:, 2, p, 0:n].rearrange("p (b t) -> p b t", t=DEC_T),
                                            bl[:, :, DEC_T - 1:DEC_T].broadcast_to([P, DEC_B, DEC_T]), bl,
                                            ALU.subtract)
                nc.vector.tensor_scalar(T2[:, :, 0, 0:n], B, -1.0, CLAMP, ALU.mult, ALU.min).then_inc(s_args, 1)

        def decayed_k(c):
            n = ROWS[c]
            T1, T2 = T1s[c % 2], T2s[c % 2]
            dve.wait_ge(s_exp, c + 1)
            if c == 0:
                dve.wait_ge(s_eva, evacs(index[("q", 1, 2)], True))
            k = kT[:, :, c * P:c * P + n]
            if c < TT - 1:
                nc.vector.tensor_copy(sdecs[:, c % 2, :], T1[:, 1, :, P - 1])
            else:
                nc.vector.tensor_copy(o_dec[:], T1[:, 1, :, 0:n].rearrange("p a (b t) -> p a b t",
                                                                           t=DEC_T)[:, :, :, DEC_T - 1])
            nc.vector.tensor_tensor(T1[:, 2, :, 0:n], T1[:, 2, :, 0:n], k, ALU.mult)
            if c < TT - 1:
                for p in range(2):
                    nc.vector.tensor_tensor(T2[:, p, :, :], T2[:, p, :, :],
                                            k[:, p, :].unsqueeze(1).broadcast_to([P, 4, P]), ALU.mult)
            else:
                nc.vector.tensor_tensor(T2[:, :, 0, 0:n], T2[:, :, 0, 0:n], k, ALU.mult)

        def decayed_q(c):
            n = ROWS[c]
            T1 = T1s[c % 2]
            q = qT[:, :, c * P:c * P + n]
            if c >= 1:
                dve.wait_ge(s_o, c)
            for a in range(2):
                rows = slice(64 * a, 64 * a + 64)
                x = nc.vector.tensor_tensor(qz[rows, :, :, 0:n].rearrange("p w (b a) t -> p w b a t", a=2)[:, :, :, a, :],
                                            T1[rows, 0:2, :, 0:n],
                                            q[rows, :, :].unsqueeze(1).broadcast_to([64, 2, 2, n]), ALU.mult)
            x.then_inc(s_kq, 1)

        def mask_scores(c):
            n = ROWS[c]
            dve.wait_ge(s_score, c + 1)
            S = bank[0][:, :].rearrange("p (h t) -> p h t", h=HEADS)
            if c < TT - 1:
                for i in range(4):
                    m = SB * (i + 1)
                    t = slice(SB * i, SB * (i + 1))
                    x = nc.vector.tensor_tensor(Pm[0:m, :, t], S[0:m, :, t],
                                                mask_p[0:m, t].unsqueeze(1).broadcast_to([m, HEADS, SB]), ALU.mult)
            else:
                x = nc.vector.tensor_tensor(Pm[0:n, :, 0:n], S[0:n, :, 0:n],
                                            mask_s[:].unsqueeze(1).broadcast_to([n, HEADS, n]), ALU.mult)
            x.then_inc(s_pm, 1)

        def state(c):
            dve.wait_ge(s_o, c + 1)
            for h in range(HEADS):
                p, a = h // 2, 64 * (h % 2)
                add = bank[3][a:a + 64, p * 256 + 2 * a:p * 256 + 2 * a + DV]
                if c == 0:
                    x = nc.vector.tensor_copy(Sp[a:a + 64, p, :], add)
                else:
                    x = nc.vector.scalar_tensor_tensor(out=Sp[a:a + 64, p, :], in0=Sp[a:a + 64, p, :],
                                                       scalar=sdecs[a:a + 64, c % 2, p:p + 1], in1=add, op0=ALU.mult,
                                                       op1=ALU.add)
            x.then_inc(s_st, 1)

        def out_norm(c):
            n = ROWS[c]
            dve.wait_ge(s_rs, c + 1)
            O_, R_ = bank[2][:, :], rs
            dst = v[:, c, :] if c < TT - 1 else R_
            dst = dst.rearrange("p (h t) -> p h t", h=HEADS)[:, :, 0:n]
            nc.vector.scalar_tensor_tensor(out=dst, in0=O_.rearrange("p (h t) -> p h t", h=HEADS)[:, :, 0:n],
                                           scalar=gnorm[:], in1=R_.rearrange("p (h t) -> p h t", h=HEADS)[:, :, 0:n],
                                           op0=ALU.mult, op1=ALU.mult).then_inc(s_on, 1)

        def pool_group(m):
            w = WINDOWS[m]
            full = wsum[m % 2]
            dve.wait_ge(s_eva, evacs(index[("u", m, 2)], True))
            if m == 0:
                dve.wait_ge(s_histev, 1)
            if m >= 2:
                dve.wait_ge(s_grp, index[("mix", m - 2, 2)] + 1)
            link(nc.vector.tensor_tensor_scan(full, uT[:, m, U_P:U_W], uT[:, m, U_P - w:U_W - w], 0.0,
                                              ALU.add, ALU.subtract))
            cur = uT[:, m, U_P:U_P + 16]
            link(nc.vector.tensor_tensor(edge[:, 0:w], full[:, 0:w], icnt[:, 0:w], ALU.mult))
            link(nc.vector.scalar_tensor_tensor(out=edge[:, 32:32 + NS].rearrange("p (b t) -> p b t", t=DEC_T),
                                           in0=full[:, SEQ:].rearrange("p (b t) -> p b t", t=SEG)[:, :, HIST:],
                                           scalar=1.0 / w,
                                           in1=uT[:, m, U_S:].rearrange("p (b t) -> p b t", t=SEG)[:, :, HIST:],
                                           op0=ALU.mult, op1=ALU.subtract))
            nc.vector.scalar_tensor_tensor(out=full[:, w:SEQ], in0=full[:, w:SEQ], scalar=1.0 / w,
                                           in1=uT[:, m, U_P + w:U_S], op0=ALU.mult, op1=ALU.subtract)
            nc.vector.tensor_tensor(full[:, 0:w], edge[:, 0:w], cur[:, 0:w], ALU.subtract)
            nc.vector.tensor_copy(full[:, SEQ:SEQ + NS], edge[:, 32:32 + NS]).then_inc(s_pool, 1)

        def fill(c, part):
            for g in between[c][part]:
                if g[0] not in ON_ACT:
                    evac(*g)

        dve.wait_ge(s_tr, 2 * TT)
        link(nc.vector.memset(qz[:, :, :, :], 0.0))
        args(0)
        args(1)
        for t in range(3):
            evac("v", 0, t)
        decayed_k(0)
        decayed_q(0)
        for t in range(3, TT):
            evac("v", 0, t)
        for c in range(TT - 1):
            fill(c, 0)
            mask_scores(c)
            decayed_k(c + 1)
            fill(c, 1)
            decayed_q(c + 1)
            state(c)
            fill(c, 2)
            if c + 2 < TT:
                args(c + 2)
            out_norm(c)
            if 3 <= c < 7:
                pool_group(c - 3)
        def gate(m):
            dve.wait_ge(s_silu, m + 1)
            nc.vector.tensor_tensor(gT[:, m, 0:SEQ].rearrange("p (c t) -> p c t", t=P),
                                    gT[:, m, 0:SEQ].rearrange("p (c t) -> p c t", t=P),
                                    v[:, 0:TT - 1, m * P:(m + 1) * P], ALU.mult)

        def state_add(b):
            dve.wait_ge(s_ku, b + 1)
            for a in range(2):
                src = bank[[0, 3][b % 2]][64 * a:64 * a + 64, :].rearrange("p (q x) -> p q x", q=2)[
                    :, :, a * DV:(a + 1) * DV]
                x = nc.vector.tensor_tensor(S0[64 * a:64 * a + 64, b, :, :], S0[64 * a:64 * a + 64, b, :, :], src,
                                            ALU.add)
            x.then_inc(s_us, 1)

        c = TT - 1
        fill(c, 0)
        mask_scores(c)
        dve.wait_ge(s_on, c)
        for m in range(3):
            gate(m)
        fill(c, 1)
        dve.wait_ge(s_o, TT)
        dve.wait_ge(s_khn, TT)
        nc.vector.tensor_tensor(KM, khN[0:NS, :, :].rearrange("p a d -> p (a d)").unsqueeze(1).broadcast_to(
            [NS, DEC_B, 256]), bmask[:].unsqueeze(2).broadcast_to([NS, DEC_B, 256]), ALU.mult).then_inc(s_km, 1)
        for p in range(2):
            link(nc.vector.tensor_tensor(S0[:, :, p, :], S0[:, :, p, :],
                                         o_dec[:, p, :].unsqueeze(2).broadcast_to([P, DEC_B, DV]), ALU.mult))
        fill(c, 2)
        for b in range(4):
            state_add(b)
        out_norm(c)
        gate(3)
        dve.wait_ge(s_on, TT)
        nc.vector.tensor_tensor(gT[:, :, SEQ:N], gT[:, :, SEQ:N], rs.rearrange("p (h t) -> p h t", t=P)[:, :, 0:NS],
                                ALU.mult)
        for b in range(4, DEC_B):
            state_add(b)

    block.close()
    c1.close()


def b2_all(nc, A, O, S0, Sp, s_w, sb, sem, e_w, wdn, bank, ident, onesf, eps_c, uT, gT, ring, x1, x_rows, h2_dram,
           w1, w2, rank_m, token, expert, iota_w, steps):
    c2 = ExitStack()
    whi = sb("whi", [P, KC, 512], F32R, ctx=c2)
    wlo = sb("wlo", [P, KC, 512], F32R, ctx=c2)
    ahi = sb("ahi", [P, 2, KC, P], F32R, ctx=c2)
    alo = sb("alo", [P, 2, KC, P], F32R, ctx=c2)
    h2 = sb("h2", [P, 2, D], ctx=c2)
    h2T = sb("h2T", [P, 2, KC, P], ctx=c2)
    g2b = sb("g2b", [P, D], ctx=c2)
    wr = sb("wr", [P, KC, NG + NE], ctx=c2)
    rb = sb("rb", [P, NG + NE], ctx=c2)
    ssq = sb("ssq2", [P, TT], ctx=c2)
    root = sb("root2", [P, TT], ctx=c2)
    rstd = sb("rstd2", [P, TT], ctx=c2)
    L = sb("L", [P, TT, NG + NE], ctx=c2)
    before = sb("before", [P, P], BF16, ctx=c2)
    onesb = sb("onesb", [P, P], BF16, ctx=c2)
    first = sb("first", [P, 4], ctx=c2)
    M = sb("M", [P, TT, NE], ctx=c2)
    M1 = sb("M1", [P, TT, NE], ctx=c2)
    M2 = sb("M2", [P, TT, NE], ctx=c2)
    Mb = sb("Mb", [P, TT, NE], BF16, ctx=c2)
    Mp = sb("Mp", [P, TT + 1, NE], BF16, ctx=c2)
    rank = sb("rank", [P, TT, NE], ctx=c2)
    t4 = sb("t4", [P, TT, NG], ctx=c2)
    ohg = sb("ohg", [P, TT, NG], ctx=c2)
    oh1 = sb("oh1", [P, TT, 4], ctx=c2)
    oh2 = sb("oh2", [P, TT, 4], ctx=c2)
    es = sb("es", [P, TT, 4], ctx=c2)
    pr = sb("pr", [P, TT, 4, 4], ctx=c2)
    s1 = sb("s1", [P, TT], ctx=c2)
    s2 = sb("s2", [P, TT], ctx=c2)
    gp = sb("gp", [P, TT], ctx=c2)
    mx = sb("mx", [P, TT], ctx=c2)
    full = sb("full", [P, NE], ctx=c2)
    mxc = sb("mxc", [P, 2], ctx=c2)
    rlim = sb("rlim", [P, 8], ctx=c2)

    r_c = sem("r_c")
    s_states = sem("s_states")
    r_x = sem("r_x")
    r_y, r_x1, r_ssq, r_root, r_h2, r_tr, r_trev, r_lg, r_lgev = [sem(x) for x in (
        "r_y", "r_x1", "r_ssq", "r_root", "r_h2", "r_tr", "r_trev", "r_lg", "r_lgev")]
    r_hout = [sem(f"r_hout{j}") for j in range(2)]
    r_wh, r_wl, r_wu = sem("r_wh"), sem("r_wl"), sem("r_wu")
    r_ah, r_al = sem("r_ah"), sem("r_al")
    r_gc, r_d, r_ex, r_exd, r_m, r_rk, r_hf = [sem(x) for x in ("r_gc", "r_d", "r_ex", "r_exd", "r_m", "r_rk", "r_hf")]
    r_xt = [sem(f"r_xt{i}") for i in range(TT)]
    block = ExitStack()
    blk = block.enter_context(nc.Block())
    GC = 11

    @blk.gpsimd
    def _(pool):
        nc.gpsimd.memset(before[:], 1.0).then_inc(r_gc, 1)
        nc.gpsimd.memset(onesb[:], 1.0).then_inc(r_gc, 1)
        nc.gpsimd.memset(L[:], 0.0).then_inc(r_gc, 1)
        nc.gpsimd.memset(rlim[:], 0.0).then_inc(r_gc, 1)
        nc.gpsimd.iota(first[:], [[-1, 4]], base=4, channel_multiplier=0,
                       allow_small_or_imprecise_dtypes=True).then_inc(r_gc, 1)
        nc.gpsimd.iota(expert[:], [[1, NE]], base=1, channel_multiplier=0,
                       allow_small_or_imprecise_dtypes=True).then_inc(r_gc, 1)
        nc.gpsimd.iota(iota_w[:], [[1, W]], base=0, channel_multiplier=0,
                       allow_small_or_imprecise_dtypes=True).then_inc(r_gc, 1)
        nc.gpsimd.iota(token[:, :, 0], [[P, TT]], base=0, channel_multiplier=1,
                       allow_small_or_imprecise_dtypes=True).then_inc(r_gc, 1)
        nc.gpsimd.memset(Mp[:], 0.0).then_inc(r_gc, 1)
        pool.wait_ge(r_gc, 9)
        nc.gpsimd.affine_select(out=before[:], in_=before[:], pattern=[[1, P]], compare_op=ALU.is_gt, fill=0.0,
                                base=0, channel_multiplier=-1).then_inc(r_gc, 1)
        nc.gpsimd.iota(rlim[:, 0:ROUNDS], [[W, ROUNDS]], base=0, channel_multiplier=0,
                       allow_small_or_imprecise_dtypes=True).then_inc(r_gc, 1)

    @blk.sync
    def _(sp):
        sp.dma_start(g2b[:], A["norm2_g"].broadcast_to([P, D])).then_inc(r_c, 16)
        with nc.allow_non_contiguous_dma(reason="router weights, 16 and 64 bytes a row"):
            sp.dma_start(wr[:, :, 0:NG], A["w_router_group"][0].rearrange("(k p) n -> p k n", p=P)).then_inc(r_c, 16)
            sp.dma_start(wr[:, :, NG:], A["w_router_expert"][0].rearrange("(k p) n -> p k n", p=P)).then_inc(r_c, 16)
        sp.dma_start(rb[:, 0:NG], A["b_router_group"].broadcast_to([P, NG])).then_inc(r_c, 16)
        sp.dma_start(rb[:, NG:], A["b_router_expert"].broadcast_to([P, NE])).then_inc(r_c, 16)
        for i in range(TT):
            sp.dma_start(x1[0:ROWS[i], i, :], x_rows[i]).then_inc(r_xt[i], 16)
        for a in range(2):
            sp.dma_start(O[3][0, 0].rearrange("(p a) k v -> a k p v", a=2)[a],
                         Sp[64 * a:64 * a + 64, :, :]).then_inc(s_states, 16)
            sp.dma_start(O[5][0].rearrange("b (p a) k v -> a k b p v", a=2)[a],
                         S0[64 * a:64 * a + 64, :, :, :]).then_inc(s_states, 16)
        for u in (4, 5):
            dst, src = expert_unit(A, ring, wdn, u, 0)
            sp.dma_start(dst, src).then_inc(e_w[u], 16)
        sp.wait_ge(r_wl, 2 * KC)
        for u in range(4):
            dst, src = expert_unit(A, ring, wdn, u, 0)
            sp.dma_start(dst, src).then_inc(e_w[u], 16)
        for i in range(TT):
            sp.wait_ge(r_h2, i + 1)
            sp.dma_start(h2_dram[i * P:i * P + ROWS[i], :], h2[0:ROWS[i], i % 2, :]).then_inc(r_hout[i % 2], 16)
        for j in range(2):
            sp.wait_ge(r_hout[j], 16 * len(range(j, TT, 2)))
        sp.wait_ge(s_states, 16 * 4)

    @blk.tensor
    def _(pe):
        def router(i):
            r = ROWS[i]
            pe.wait_ge(r_h2, i + 1)
            if i >= 1:
                pe.wait_ge(r_trev, 2 * i)
            for h in range(2):
                for k in range(4):
                    t = nc.tensor.transpose(bank[4 + h][:, k * P:k * P + r],
                                            h2[0:r, i % 2, (4 * h + k) * P:(4 * h + k + 1) * P], ident[0:r, 0:r])
                t.then_inc(r_tr, 1)
            if i == 0:
                return
            logits(i - 1)

        def logits(i):
            r = ROWS[i]
            pe.wait_ge(r_trev, 2 * (i + 1))
            if i >= 1:
                pe.wait_ge(r_lgev, i)
            else:
                pe.wait_ge(r_c, 16 * 5)
            for k in range(KC):
                m = nc.tensor.matmul(bank[6][0:r, 0:NG + NE], h2T[:, i % 2, k, 0:r], wr[:, k, :],
                                     start=k == 0, stop=k == KC - 1)
            m.then_inc(r_lg, 1)

        for n in range(2 * TT):
            h, i = n // TT, n % TT
            r, s = ROWS[i], n % 2
            if n >= 4:
                pe.wait_ge(r_x1, n - 3)
            pe.wait_ge(r_al, n + 1)
            out = bank[n % 4][0:r, :]
            for k in range(KC):
                if i == 0:
                    pe.wait_ge(r_wl, KC * h + k + 1)
                nc.tensor.matmul(out, ahi[:, s, k, 0:r], whi[:, k, :], start=k == 0, stop=False)
                nc.tensor.matmul(out, ahi[:, s, k, 0:r], wlo[:, k, :], start=False, stop=False)
                m = nc.tensor.matmul(out, alo[:, s, k, 0:r], whi[:, k, :], start=False, stop=k == KC - 1)
                if i == TT - 1 and k < KC - 1:
                    m.then_inc(r_wu, 1)
            m.then_inc(r_y, 1)
            if h == 1 and i >= 1:
                router(i - 1)
        router(TT - 1)
        logits(TT - 1)
        pe.wait_ge(r_m, 1)
        nc.tensor.matmul(bank[7][:, 0:TT * NE], onesb[:], Mp[:, 0:TT, :].rearrange("p t e -> p (t e)"),
                         start=True, stop=False)
        nc.tensor.matmul(bank[7][:, 0:TT * NE], before[:], Mb[:].rearrange("p t e -> p (t e)"), start=False, stop=True)
        nc.tensor.matmul(bank[6][:, 0:NE], onesb[:], Mp[:, TT, :], start=True, stop=True).then_inc(r_rk, 1)

    @blk.scalar
    def _(act):
        def transposed(i):
            r = ROWS[i]
            if i >= 2:
                act.wait_ge(r_lg, i - 1)
            for h in range(2):
                act.wait_ge(r_tr, 2 * i + h + 1)
                nc.scalar.copy(h2T[:, i % 2, 4 * h:4 * h + 4, 0:r],
                               bank[4 + h][:, :].rearrange("p (k t) -> p k t", t=P)[:, :, 0:r]).then_inc(r_trev, 1)

        def tile_hi(n):
            r, t0 = ROWS[n % TT], n % TT * P
            if n >= 2:
                act.wait_ge(r_y, n - 1)
            nc.scalar.copy(ahi[:, n % 2, 0:4, 0:r], uT[:, :, t0:t0 + r])
            nc.scalar.copy(ahi[:, n % 2, 4:8, 0:r], gT[:, :, t0:t0 + r]).then_inc(r_ah, 1)

        def weights_hi(h):
            for j in (2 * h, 2 * h + 1):
                act.wait_ge(s_w[j], 48)
            for k in range(KC):
                if h == 1 and k < KC - 1:
                    act.wait_ge(r_wu, k + 1)
                elif h == 1:
                    act.wait_ge(r_y, TT)
                nc.scalar.copy(whi[:, k, :].rearrange("p (u n) -> p u n", u=2),
                               ring[:, 2 * h:2 * h + 2, k, :]).then_inc(r_wh, 1)

        tile_hi(0)
        weights_hi(0)
        for n in range(1, TT + 1):
            tile_hi(n)
        weights_hi(1)
        for i in range(TT):
            r = ROWS[i]
            if i < TT - 1:
                tile_hi(TT + i + 1)
            act.wait_ge(r_x1, TT + i + 1)
            if i >= 2:
                act.wait_ge(r_tr, 2 * (i - 1))
                act.wait_ge(r_hout[i % 2], 16 * (i // 2))
            nc.scalar.activation(h2[0:r, i % 2, :], x1[0:r, i, :], ACT.Square, scale=D ** -0.5,
                                 accum_out=ssq[0:r, i:i + 1]).then_inc(r_ssq, 1)
            act.wait_ge(r_ssq, i + 1)
            nc.scalar.activation(root[0:r, i:i + 1], ssq[0:r, i:i + 1], ACT.Sqrt,
                                 bias=eps_c[0:r, :]).then_inc(r_root, 1)
            if i >= 1:
                transposed(i - 1)
        transposed(TT - 1)
        act.wait_ge(r_exd, 1)
        nc.scalar.activation(t4[:], t4[:], ACT.Exp).then_inc(r_ex, 1)
        act.wait_ge(r_exd, 2)
        nc.scalar.activation(s2[:], s2[:], ACT.Exp).then_inc(r_ex, 1)

    @blk.vector
    def _(dve):
        chain = [0]

        def link(ins):
            chain[0] += 1
            ins.then_inc(r_d, 1)
            dve.wait_ge(r_d, chain[0])

        def logit_out(i):
            r = ROWS[i]
            dve.wait_ge(r_lg, i + 1)
            nc.vector.tensor_tensor(L[0:r, i, :], bank[6][0:r, 0:NG + NE], rb[0:r, :], ALU.add).then_inc(r_lgev, 1)

        dve.wait_ge(r_gc, GC)
        def tile_lo(n):
            r, t0 = ROWS[n % TT], n % TT * P
            dve.wait_ge(r_ah, n + 1)
            nc.vector.tensor_tensor(alo[:, n % 2, 0:4, 0:r], uT[:, :, t0:t0 + r],
                                    ahi[:, n % 2, 0:4, 0:r].bitcast(F32), ALU.subtract)
            nc.vector.tensor_tensor(alo[:, n % 2, 4:8, 0:r], gT[:, :, t0:t0 + r],
                                    ahi[:, n % 2, 4:8, 0:r].bitcast(F32), ALU.subtract).then_inc(r_al, 1)

        def weights_lo(h):
            for k in range(KC):
                dve.wait_ge(r_wh, KC * h + k + 1)
                nc.vector.tensor_tensor(wlo[:, k, :].rearrange("p (u n) -> p u n", u=2),
                                        ring[:, 2 * h:2 * h + 2, k, :],
                                        whi[:, k, :].bitcast(F32).rearrange("p (u n) -> p u n", u=2),
                                        ALU.subtract).then_inc(r_wl, 1)

        def residual(n):
            h, i = n // TT, n % TT
            r = ROWS[i]
            dve.wait_ge(r_xt[i], 16)
            dve.wait_ge(r_y, n + 1)
            nc.vector.tensor_tensor(x1[0:r, i, h * 512:(h + 1) * 512], x1[0:r, i, h * 512:(h + 1) * 512],
                                    bank[n % 4][0:r, :], ALU.add).then_inc(r_x1, 1)

        tile_lo(0)
        weights_lo(0)
        for n in range(1, TT + 1):
            tile_lo(n)
            if n < TT:
                residual(n - 1)
        weights_lo(1)
        residual(TT - 1)
        for i in range(TT):
            r = ROWS[i]
            if i < TT - 1:
                tile_lo(TT + i + 1)
            residual(TT + i)
            dve.wait_ge(r_root, i + 1)
            link(nc.vector.reciprocal(rstd[0:r, i:i + 1], root[0:r, i:i + 1]))
            if i == 0:
                dve.wait_ge(r_c, 16 * 5)
            nc.vector.scalar_tensor_tensor(out=h2[0:r, i % 2, :], in0=x1[0:r, i, :], scalar=rstd[0:r, i:i + 1],
                                           in1=g2b[0:r, :], op0=ALU.mult, op1=ALU.mult).then_inc(r_h2, 1)
            if i >= 2:
                logit_out(i - 2)
        logit_out(TT - 2)
        logit_out(TT - 1)
        dve.wait_ge(r_lgev, TT)

        def b(ap, shape):
            return ap.unsqueeze(2).broadcast_to(shape)

        def pick(oh, vals, top):
            link(nc.vector.tensor_reduce(top[:], vals, axis=AX.X, op=ALU.max))
            link(nc.vector.tensor_tensor(oh[:], vals, b(top[:], [P, TT, 4]), ALU.is_equal))
            link(nc.vector.tensor_tensor(oh[:], oh[:], first[:].unsqueeze(1).broadcast_to([P, TT, 4]), ALU.mult))
            link(nc.vector.tensor_reduce(mx[:], oh[:], axis=AX.X, op=ALU.max))
            link(nc.vector.tensor_tensor(oh[:], oh[:], b(mx[:], [P, TT, 4]), ALU.is_equal))

        gl, el = L[:, :, 0:NG], L[:, :, NG:]
        pick(ohg, gl, s1)
        nc.vector.tensor_tensor(t4[:], gl, b(s1[:], [P, TT, NG]), ALU.subtract).then_inc(r_exd, 1)
        link(nc.vector.tensor_tensor(pr[:], el.rearrange("p t (g j) -> p t g j", g=NG),
                                     ohg[:].unsqueeze(3).broadcast_to([P, TT, NG, 4]), ALU.mult))
        link(nc.vector.tensor_reduce(es[:], pr[:].rearrange("p t g j -> p t j g"), axis=AX.X, op=ALU.add))
        pick(oh1, es[:], s1)
        link(nc.vector.scalar_tensor_tensor(out=es[:], in0=oh1[:], scalar=-3e38, in1=es[:], op0=ALU.mult, op1=ALU.add))
        pick(oh2, es[:], s2)
        nc.vector.tensor_tensor(s2[:], s2[:], s1[:], ALU.subtract).then_inc(r_exd, 1)
        for oh, m in ((oh1, M1), (oh2, M2)):
            link(nc.vector.tensor_tensor(m[:].rearrange("p t (g j) -> p t g j", g=NG),
                                         ohg[:].unsqueeze(3).broadcast_to([P, TT, NG, 4]),
                                         oh[:].unsqueeze(2).broadcast_to([P, TT, NG, 4]), ALU.mult))
        link(nc.vector.memset(M1[NS:P, TT - 1, :], 0.0))
        link(nc.vector.memset(M2[NS:P, TT - 1, :], 0.0))
        link(nc.vector.tensor_tensor(M[:], M1[:], M2[:], ALU.add))
        link(nc.vector.tensor_copy(Mb[:], M[:]))
        for t in range(TT):
            x = nc.vector.tensor_tensor(Mp[:, t + 1, :], Mp[:, t, :], Mb[:, t, :], ALU.add)
            if t < TT - 1:
                link(x)
        x.then_inc(r_m, 1)
        dve.wait_ge(r_ex, 2)
        link(nc.vector.tensor_reduce(gp[:], t4[:], axis=AX.X, op=ALU.add))
        link(nc.vector.tensor_scalar(s1[:], s2[:], 1.0, None, ALU.add))
        link(nc.vector.tensor_tensor(s1[:], s1[:], gp[:], ALU.mult))
        link(nc.vector.reciprocal(w1[:], s1[:]))
        link(nc.vector.tensor_tensor(w2[:], w1[:], s2[:], ALU.mult))
        dve.wait_ge(r_rk, 1)
        link(nc.vector.tensor_copy(rank[:].rearrange("p t e -> p (t e)"), bank[7][:, 0:TT * NE]))
        link(nc.vector.tensor_tensor(M2[:], M2[:], expert[:].unsqueeze(1).broadcast_to([P, TT, NE]), ALU.mult))
        link(nc.vector.tensor_reduce(mx[:], M2[:], axis=AX.X, op=ALU.add))
        link(nc.vector.tensor_copy(token[:, :, 1], mx[:]))
        link(nc.vector.scalar_tensor_tensor(out=rank[:], in0=rank[:], scalar=1.0, in1=M[:], op0=ALU.add, op1=ALU.mult))
        link(nc.vector.tensor_scalar(rank_m[:].rearrange("p (e t) -> p t e", e=NE), rank[:], -1.0, None, ALU.add))
        link(nc.vector.tensor_reduce(mxc[:, 0:1], bank[6][:, 0:NE], axis=AX.X, op=ALU.max))
        link(nc.vector.tensor_scalar(rlim[:, 0:ROUNDS], rlim[:, 0:ROUNDS], mxc[:, 0:1], float(NE), ALU.is_lt, ALU.mult))
        link(nc.vector.tensor_reduce(mxc[:, 1:2], rlim[:, 0:ROUNDS], axis=AX.X, op=ALU.add))
        link(nc.vector.tensor_copy(steps[0:1, 0:1], mxc[0:1, 1:2]))

    block.close()
    c2.close()


def expert_unit(A, ring, wdn, u, e):
    if u < 4:
        w = (A["w_gate"], A["w_up"])[u % 2].rearrange("l e (k p) n -> (l e) p k n", p=P)
        return ring[:, u, :, :], w[e, :, :, (u // 2) * 256:(u // 2 + 1) * 256]
    w = A["w_down"].rearrange("l e (k p) n -> (l e) p k n", p=P)
    return wdn[:, u - 4, :].rearrange("p (k n) -> p k n", k=4), w[e, :, :, (u - 4) * 512:(u - 3) * 512]


def b3_all(nc, A, sb, sem, e_w, ring, wdn, bank, ident, h2_dram, y_dram, rank_m, token, expert, iota_w, steps):
    c3 = ExitStack()
    xg = sb("xg", [P, 2, D], ctx=c3)
    xT = sb("xT", [P, KC, W], ctx=c3)
    oh = sb("oh", [P, TT, W], FP16, ctx=c3)
    idx = sb("idx", [P, 2], I32, ctx=c3)
    far = sb("far", [P, 2], ctx=c3)
    dest = sb("dest", [P, 2], I32, ctx=c3)
    dest_now = sb("dest_now", [P, 2], I32, ctx=c3)
    sg = sb("sg", [P, 2, W], ctx=c3)
    hold_at = sb("hold_at", [P, 1], ctx=c3)
    hid = sb("hid", [P, 4, W], ctx=c3)
    yT = sb("yT", [P, KC, W], ctx=c3)
    yr = sb("yr", [P, 2, D], ctx=c3)

    e_oh, e_ix, e_idx = sem("e_oh"), sem("e_ix"), sem("e_idx")
    e_free = sem("e_free")
    e_far, e_now = sem("e_far"), sem("e_now")
    e_hold = sem("e_hold")
    e_rk = sem("e_rk")
    e_xg, e_xt, e_xe = sem("e_xg"), sem("e_xt"), sem("e_xe")
    e_gu, e_si, e_h = sem("e_gu"), sem("e_si"), sem("e_h")
    e_yt, e_ya, e_yd = sem("e_yt"), sem("e_ya"), sem("e_yd")
    e_yr, e_re, e_out = sem("e_yr"), sem("e_re"), sem("e_out")
    block = ExitStack()
    blk = block.enter_context(nc.Block())

    def count(eng):
        return eng.value_load(steps[0:1, 0:1], min_val=NE, max_val=NE * ROUNDS)

    @blk.sync
    def _(sp):
        n = count(sp)
        with sp.Fori(0, n - 1) as i:
            e = (i + 1) % NE
            for u in range(6):
                sp.wait_ge(e_gu if u < 4 else e_yt, i * 4 + (2 if u in (0, 1, 4) else 4))
                dst, src = expert_unit(A, ring, wdn, u, bass.ds(e, 1))
                sp.dma_start(dst, src.rearrange("o p k n -> p (o k) n")).then_inc(e_w[u], 16)

    @blk.gpsimd
    def _(pool):
        def gather():
            nc.gpsimd.indirect_dma_start(out=xg[:, 0, :], out_offset=None, in_=h2_dram,
                                         in_offset=bass.IndirectOffsetOnAxis(ap=idx[:, 0:1], axis=0)
                                         ).then_inc(e_xg, 16)
            nc.gpsimd.indirect_dma_start(out=xg[0:W2, 1, :], out_offset=None, in_=h2_dram,
                                         in_offset=bass.IndirectOffsetOnAxis(ap=idx[0:W2, 1:2], axis=0)
                                         ).then_inc(e_xg, 16)

        def scatter():
            for c, m in ((0, P), (1, W2)):
                nc.gpsimd.indirect_dma_start(out=y_dram, in_=yr[0:m, c, :], in_offset=None, bounds_check=2 * N - 1,
                                             out_offset=bass.IndirectOffsetOnAxis(ap=dest_now[0:m, c:c + 1], axis=0),
                                             oob_is_err=False).then_inc(e_out, 16)

        def hold():
            nc.gpsimd.tensor_tensor(hold_at[:], ident[:, 0:1], ident[:, 1:2], ALU.add).then_inc(e_hold, 1)

        n = count(pool)
        pool.sem_inc(e_free, 1)
        pool.sem_inc(e_hold, 1)
        pool.wait_ge(e_idx, 1)
        gather()
        with pool.Fori(0, n) as i:
            pool.wait_ge(e_hold, i * 2 + 1)
            pool.wait_ge(e_idx, i + 2)
            pool.wait_ge(e_xt, i * 3 + 3)
            hold()
            gather()
            pool.wait_ge(e_hold, i * 2 + 2)
            pool.wait_ge(e_re, i * 4 + 5)
            hold()
            scatter()
            pool.wait_ge(e_out, i * 32 + 32)
            pool.sem_inc(e_free, 1)
        pool.wait_ge(e_xg, n * 32 + 32)

    @blk.tensor
    def _(pe):
        def indices():
            for c, m in ((0, P), (1, W2)):
                for t in range(TT):
                    x = nc.tensor.matmul(bank[7][0:m, 2 * c:2 * c + 2], oh[:, t, c * P:c * P + m], token[:, t, :],
                                         start=t == 0, stop=t == TT - 1)
            x.then_inc(e_ix, 1)

        def rows_in():
            for h in range(2):
                for k in range(4):
                    x = nc.tensor.transpose(bank[4 + h][:, k * P:(k + 1) * P],
                                            xg[:, 0, (4 * h + k) * P:(4 * h + k + 1) * P], ident[:])
                x.then_inc(e_xt, 1)
            for k in range(KC):
                x = nc.tensor.transpose(bank[6][:, k * W2:(k + 1) * W2], xg[0:W2, 1, k * P:(k + 1) * P],
                                        ident[0:W2, 0:W2])
            x.then_inc(e_xt, 1)

        def gate_up(f):
            c0 = (f % 2) * P
            for side in range(2):
                u = 2 * (f // 2) + side
                for k in range(KC):
                    x = nc.tensor.matmul(bank[f % 2][:, side * 256:side * 256 + W],
                                         ring[:, u, k, c0:c0 + P], xT[:, k, :],
                                         start=k == 0, stop=k == KC - 1)
            x.then_inc(e_gu, 1)

        def down(j, i):
            for q in range(2):
                d = 2 * j + q
                for k in range(4):
                    if j == 0 and q == 0 and k >= 2:
                        pe.wait_ge(e_h, i * 4 + k + 2)
                    x = nc.tensor.matmul(bank[2 + j % 2][:, q * 256:q * 256 + W],
                                         wdn[:, d // 4, k * 512 + (d % 4) * P:k * 512 + (d % 4 + 1) * P],
                                         hid[:, k, :], start=k == 0, stop=k == 3)
            x.then_inc(e_yt, 1)

        def rows_back(h):
            for c, m in ((0, P), (1, W2)):
                for k in range(4):
                    x = nc.tensor.transpose(bank[6 if c else 4 + h][0:m, k * P:(k + 1) * P],
                                            yT[:, 4 * h + k, c * P:c * P + m], ident[:])
                x.then_inc(e_yr, 1)

        n = count(pe)
        pe.wait_ge(e_oh, 1)
        indices()
        pe.wait_ge(e_oh, 2)
        pe.wait_ge(e_idx, 1)
        indices()
        pe.wait_ge(e_xg, 32)
        rows_in()
        with pe.Fori(0, n) as i:
            pe.wait_ge(e_xe, i * 3 + 3)
            for f in range(4):
                pe.wait_ge(e_h, i * 4 + (1 if f < 2 else f))
                if f % 2 == 0:
                    pe.wait_ge(e_w[f], i * 16 + 16)
                    pe.wait_ge(e_w[f + 1], i * 16 + 16)
                gate_up(f)
            for j in range(4):
                pe.wait_ge(e_ya if j % 2 == 0 else e_yd, i * 2 + j // 2 + 1)
                if j % 2 == 0:
                    pe.wait_ge(e_w[4 + j // 2], i * 16 + 16)
                down(j, i)
                if j == 1:
                    pe.wait_ge(e_xg, i * 32 + 64)
                    pe.wait_ge(e_re, i * 4 + 1)
                    rows_in()
                elif j == 2:
                    pe.wait_ge(e_xe, i * 3 + 6)
                    pe.wait_ge(e_ya, i * 2 + 2)
                    pe.wait_ge(e_yd, i * 2 + 2)
                    rows_back(0)
            pe.wait_ge(e_oh, i + 3)
            pe.wait_ge(e_idx, i + 2)
            indices()
            pe.wait_ge(e_ya, i * 2 + 3)
            pe.wait_ge(e_yd, i * 2 + 3)
            pe.wait_ge(e_re, i * 4 + 3)
            rows_back(1)

    @blk.scalar
    def _(act):
        n = count(act)
        act.sem_inc(e_ya, 1)
        act.sem_inc(e_re, 1)
        with act.Fori(0, n) as i:
            for f in range(4):
                act.wait_ge(e_gu, i * 4 + f + 1)
                nc.scalar.activation(sg[:, f % 2, :], bank[f % 2][:, 0:W], ACT.Silu).then_inc(e_si, 1)
            for j in (0, 2):
                act.wait_ge(e_yt, i * 4 + j + 1)
                nc.scalar.copy(yT[:, 2 * j:2 * j + 2, :],
                               bank[2][:, :].rearrange("p (q t) -> p q t", q=2)[:, :, 0:W]).then_inc(e_ya, 1)
            act.wait_ge(e_free, i + 1)
            for h in range(2):
                for c, m in ((0, P), (1, W2)):
                    act.wait_ge(e_yr, i * 4 + 2 * h + c + 1)
                    nc.scalar.copy(yr[0:m, c, h * 512:(h + 1) * 512],
                                   bank[6 if c else 4 + h][0:m, :]).then_inc(e_re, 1)

    @blk.vector
    def _(dve):
        def onehot(e):
            nc.vector.tensor_tensor(oh[:], iota_w[:].unsqueeze(1).broadcast_to([P, TT, W]),
                                    rank_m[:, bass.ds(e * TT, TT)].unsqueeze(2).broadcast_to([P, TT, W]),
                                    ALU.is_equal).then_inc(e_oh, 1)

        def lower(e):
            nc.vector.tensor_scalar(rank_m[:, bass.ds(e * TT, TT)], rank_m[:, bass.ds(e * TT, TT)], float(-W), None,
                                    ALU.add).then_inc(e_rk, 1)

        def indices(e, s):
            tok, second = bank[7][:, 0:3:2], bank[7][:, 1:4:2]
            nc.vector.tensor_copy(idx[:], tok)
            nc.vector.tensor_scalar(far[:], second, 0.0, float(4 * N), ALU.is_equal, ALU.mult).then_inc(e_far, 1)
            dve.wait_ge(e_far, s * 2 + 1)
            nc.vector.scalar_tensor_tensor(out=far[:], in0=tok, scalar=2.0, in1=far[:], op0=ALU.mult,
                                           op1=ALU.add).then_inc(e_far, 1)
            dve.wait_ge(e_far, s * 2 + 2)
            nc.vector.scalar_tensor_tensor(out=dest[:], in0=second, scalar=expert[:, bass.ds(e, 1)], in1=far[:],
                                           op0=ALU.is_equal, op1=ALU.add).then_inc(e_idx, 1)

        n = count(dve)
        dve.sem_inc(e_h, 1)
        dve.sem_inc(e_yd, 1)
        nc.vector.memset(bank[7][:, 0:4], 0.0)
        onehot(0)
        dve.wait_ge(e_oh, 1)
        lower(0)
        dve.wait_ge(e_ix, 1)
        indices(0, 0)
        onehot(1)
        dve.wait_ge(e_oh, 2)
        lower(1)

        def x_out(base):
            for h in range(2):
                dve.wait_ge(e_xt, base + h + 1)
                nc.vector.tensor_copy(xT[:, 4 * h:4 * h + 4, 0:P],
                                      bank[4 + h][:, :].rearrange("p (k t) -> p k t", t=P)).then_inc(e_xe, 1)
            dve.wait_ge(e_xt, base + 3)
            nc.vector.tensor_copy(xT[:, :, P:W],
                                  bank[6][:, 0:KC * W2].rearrange("p (k t) -> p k t", t=W2)).then_inc(e_xe, 1)

        x_out(0)
        with dve.Fori(0, n) as i:
            dve.wait_ge(e_ix, i + 2)
            dve.wait_ge(e_rk, i + 2)
            onehot((i + 2) % NE)
            for f in range(4):
                dve.wait_ge(e_si, i * 4 + f + 1)
                nc.vector.tensor_tensor(hid[:, f, :], sg[:, f % 2, :], bank[f % 2][:, 256:256 + W],
                                        ALU.mult).then_inc(e_h, 1)
                if f == 0:
                    dve.wait_ge(e_xg, i * 32 + 32)
                    dve.wait_ge(e_free, i + 1)
                    dve.wait_ge(e_idx, i + 1)
                    nc.vector.tensor_copy(dest_now[:], dest[:]).then_inc(e_now, 1)
                    dve.wait_ge(e_now, i + 1)
                    indices((i + 1) % NE, i + 1)
                    dve.wait_ge(e_oh, i + 3)
                    lower((i + 2) % NE)
            for j in (1, 3):
                dve.wait_ge(e_yt, i * 4 + j + 1)
                nc.vector.tensor_copy(yT[:, 2 * j:2 * j + 2, :],
                                      bank[3][:, :].rearrange("p (q t) -> p q t", q=2)[:, :, 0:W]).then_inc(e_yd, 1)
                if j == 1:
                    x_out(i * 3 + 3)

    block.close()
    c3.close()


def b4_all(nc, A, O, sb, sem, bank, eps_c, x1, y_dram, w1, w2):
    c4 = ExitStack()
    B = 3
    yc = sb("yc", [P, B, 2, D], ctx=c4)
    ot = sb("ot", [P, B, D], ctx=c4)
    gfb = sb("gfb", [P, D], ctx=c4)
    ssq = sb("ssq4", [P, TT], ctx=c4)
    root = sb("root4", [P, TT], ctx=c4)
    rstd = sb("rstd4", [P, TT], ctx=c4)
    f_g = sem("f_g")
    f_y = [sem(f"f_y{j}") for j in range(B)]
    f_s, f_x2, f_ssq, f_root, f_r, f_o = [sem(x) for x in ("f_s", "f_x2", "f_ssq", "f_root", "f_r", "f_o")]
    f_out = [sem(f"f_out{j}") for j in range(B)]
    block = ExitStack()
    blk = block.enter_context(nc.Block())

    @blk.sync
    def _(sp):
        sp.dma_start(gfb[:], A["final_g"].rearrange("(o d) -> o d", o=1).broadcast_to([P, D])).then_inc(f_g, 16)
        y_view = y_dram.rearrange("(t c) d -> t c d", c=2)

        def load(i):
            if i >= B:
                sp.wait_ge(f_x2, i - B + 1)
            sp.dma_start(yc[0:ROWS[i], i % B, :, :], y_view[i * P:i * P + ROWS[i], :, :]).then_inc(f_y[i % B], 16)

        for i in range(B):
            load(i)
        for i in range(TT):
            if i + B < TT:
                load(i + B)
            sp.wait_ge(f_o, i + 1)
            dst = O[0][0, i * P:(i + 1) * P, :] if i < TT - 1 else O[1].rearrange("a t d -> (a t) d")
            sp.dma_start(dst, ot[0:ROWS[i], i % B, :]).then_inc(f_out[i % B], 16)
        for j in range(B):
            sp.wait_ge(f_out[j], 16 * len(range(j, TT, B)))

    @blk.vector
    def _(dve):
        def finish(i):
            r = ROWS[i]
            dve.wait_ge(f_root, i + 1)
            nc.vector.reciprocal(rstd[0:r, i:i + 1], root[0:r, i:i + 1]).then_inc(f_r, 1)
            dve.wait_ge(f_r, i + 1)
            nc.vector.scalar_tensor_tensor(out=ot[0:r, i % B, :], in0=x1[0:r, i, :], scalar=rstd[0:r, i:i + 1],
                                           in1=gfb[0:r, :], op0=ALU.mult, op1=ALU.mult).then_inc(f_o, 1)

        dve.wait_ge(f_g, 16)
        for i in range(TT):
            r = ROWS[i]
            dve.wait_ge(f_y[i % B], 16 * (i // B + 1))
            nc.vector.scalar_tensor_tensor(out=x1[0:r, i, :], in0=yc[0:r, i % B, 0, :], scalar=w1[0:r, i:i + 1],
                                           in1=x1[0:r, i, :], op0=ALU.mult, op1=ALU.add).then_inc(f_s, 1)
            dve.wait_ge(f_s, i + 1)
            nc.vector.scalar_tensor_tensor(out=x1[0:r, i, :], in0=yc[0:r, i % B, 1, :], scalar=w2[0:r, i:i + 1],
                                           in1=x1[0:r, i, :], op0=ALU.mult, op1=ALU.add).then_inc(f_x2, 1)
            if i >= 1:
                finish(i - 1)
        finish(TT - 1)

    @blk.scalar
    def _(act):
        for i in range(TT):
            r = ROWS[i]
            act.wait_ge(f_x2, i + 1)
            if i >= B:
                act.wait_ge(f_out[i % B], 16 * (i // B))
            nc.scalar.activation(ot[0:r, i % B, :], x1[0:r, i, :], ACT.Square, scale=D ** -0.5,
                                 accum_out=ssq[0:r, i:i + 1]).then_inc(f_ssq, 1)
            act.wait_ge(f_ssq, i + 1)
            nc.scalar.activation(root[0:r, i:i + 1], ssq[0:r, i:i + 1], ACT.Sqrt,
                                 bias=eps_c[0:r, :]).then_inc(f_root, 1)

    block.close()
    c4.close()


_INS = ["x_prompt", "x_sample", "state_pool", "state_gla", "norm1_g", "w_in", "w_gk2", "b_gk", "w_pool", "pool_scale",
        "gla_norm_g", "w_out", "norm2_g", "w_router_group", "b_router_group", "w_router_expert", "b_router_expert",
        "w_gate", "w_up", "w_down", "final_g"]
_OUTS = [(1, SEQ, D), (DEC_B, DEC_T, D), (1, 1, HIST, PW), (1, 1, HEADS, DK, DV), (1, DEC_B, HIST, PW),
         (1, DEC_B, HEADS, DK, DV)]


def kernel(**inputs):
    import numpy as _np
    import concourse.bacc as _bacc
    from concourse import mybir as _mybir
    from concourse.bass_utils import run_bass_kernel_spmd as _run

    nc = _bacc.Bacc("TRN2", target_bir_lowering=False, num_devices=1)
    arrays, args = {}, {}
    for name in _INS:
        a = _np.ascontiguousarray(inputs[name])
        arrays[f"in_{name}"] = a
        args[name] = nc.dram_tensor(f"in_{name}", a.shape, _mybir.dt.from_np(a.dtype), kind="ExternalInput").ap()
    outs = [nc.dram_tensor(f"out_{i}", s, F32, kind="ExternalOutput").ap() for i, s in enumerate(_OUTS)]
    program(nc, args, outs)
    r = _run(nc, [arrays], core_ids=[0])
    return tuple(r.results[0][f"out_{i}"] for i in range(len(_OUTS)))
```

```python
from contextlib import ExitStack

import concourse.bass as bass
from concourse import mybir
from concourse.alu_op_type import AluOpType as ALU

F32 = mybir.dt.float32
F32R = mybir.dt.float32r
BF16 = mybir.dt.bfloat16
I32 = mybir.dt.int32
ACT = mybir.ActivationFunctionType
AX = mybir.AxisListType

P = 128
D = 1024
KC = D // P
SEQ = 1024
DEC_B, DEC_T = 8, 8
NS = DEC_B * DEC_T
N = SEQ + NS
TT = 9
ROWS = [P] * (TT - 1) + [NS]
BLK = [(0, 384), (384, 384), (768, 320)]
PW = 512
PG = 4
WINDOWS = (2, 4, 8, 16)
HIST = 15
U_P = 16
U_S = U_P + SEQ
SEG = HIST + DEC_T
U_W = U_S + DEC_B * SEG
HEADS = 4
DK, DV = 64, 128
LR = 16
NG, NE = 4, 16
DE = 512
EPS = 1e-6
GATE = 16.0
CLAMP = 80.0 * GATE
SB = 32

W = 160
W2 = W - P
assert 4 * W2 == P
PARTS = 5
ROUNDS = -(-N // W)


def program(nc, A, O):
    C_U, C_Q, C_K, C_V, C_G, C_L = 0, 512, 768, 1024, 1536, 2048
    w_in = A["w_in"].rearrange("l (k p) n -> p (l k) n", p=P)
    w_out = A["w_out"].rearrange("l (k p) n -> p (l k) n", p=P)
    x_rows = [A["x_prompt"][0, i * P:(i + 1) * P, :] for i in range(TT - 1)]
    x_rows.append(A["x_sample"].rearrange("a t d -> (a t) d"))
    h2_dram = nc.dram_tensor("h2_rows", [N, D], F32).ap()
    sums_dram = nc.dram_tensor("sums", [N, D], F32).ap()

    with ExitStack() as whole:
        def sb(name, shape, dt=F32, ctx=whole):
            return ctx.enter_context(nc.sbuf_tensor(name, shape, dt))

        def sem(name):
            return whole.enter_context(nc.semaphore(name))

        bank = [whole.enter_context(nc.psum_tensor(f"bank{i}", [P, 512], F32)) for i in range(8)]

        ident = sb("ident", [P, P])
        onesf = sb("onesf", [P, P])
        eps_c = sb("eps_c", [P, 1])

        rank_m = sb("rank_m", [P, NE * TT])
        table = sb("table", [P, NE, TT, PARTS], BF16)
        iota_w = sb("iota_w", [P, 2 * P])
        steps = sb("steps", [1, 1], I32)
        x1 = sb("x1", [P, TT, D])

        with ExitStack() as before_uT:
            halves = sb("halves", [P, 11 * 1024], F32R, ctx=before_uT)
        uT = sb("uT", [P, PG, U_W])
        gT = sb("gT", [P, HEADS, N])
        S0 = sb("S0", [P, DEC_B, 2, DV])
        Sp = sb("Sp", [P, 2, DV])
        ring = sb("ring", [P, 4, KC, 256])

        s_w = [sem(f"s_w{j}") for j in range(4)]

        b1_all(nc, A, O, S0, Sp, s_w, halves, sb, sem, bank, ident, onesf, eps_c, uT, gT, ring, x1, w_in, w_out, x_rows,
               (C_U, C_Q, C_K, C_V, C_G, C_L))

        wdn = sb("wdn", [P, 2, 2048])
        e_w = [sem(f"e_w{u}") for u in range(6)]

        b2_all(nc, A, O, S0, Sp, s_w, sb, sem, e_w, wdn, bank, ident, onesf, eps_c, uT, gT, ring, x1, x_rows, h2_dram,
               sums_dram, rank_m, table, iota_w, steps)
        b3_all(nc, A, sb, sem, e_w, ring, wdn, bank, ident, h2_dram, sums_dram, rank_m, table, iota_w, steps)
        b4_all(nc, A, O, sb, sem, eps_c, x1, sums_dram)


def b1_all(nc, A, O, S0, Sp, s_w, halves, sb, sem, bank, ident, onesf, eps_c, uT, gT, ring, x1, w_in, w_out, x_rows, cols):
    C_U, C_Q, C_K, C_V, C_G, C_L = cols
    c1 = ExitStack()
    POOL_AT = U_W - U_P
    scratch = x1[:, :, :].rearrange("p a b -> p (a b)")
    hT = sb("hT", [P, KC, N], ctx=c1)
    qT = sb("qT", [P, 2, N], ctx=c1)
    kT = sb("kT", [P, 2, N], ctx=c1)
    bT = scratch[:, 5120:5120 + 2 * N].rearrange("p (a t) -> p a t", a=2)
    v = sb("v", [P, TT, 512], ctx=c1)
    lr_or_decay = sb("lr_or_decay", [P, N], ctx=c1)
    lrT = lr_or_decay[0:LR, :]
    X_AT = (0, 1, 2, 5, 6)
    xn = x1[:, 3:5, :]
    ssq = sb("ssq", [P, TT], ctx=c1)
    rstd = sb("rstd", [P, 2 * TT], ctx=c1)
    warm = sb("warm", [P, 1], ctx=c1)
    g1b = sb("g1b", [P, D], ctx=c1)
    wlr = sb("wlr", [P, KC, LR], ctx=c1)
    wgk2 = sb("wgk2", [LR, 256], ctx=c1)
    bgk = sb("bgk", [P, 2], ctx=c1)
    pscale = sb("pscale", [P, PG], ctx=c1)
    gnorm = sb("gnorm", [P, 1], ctx=c1)
    wpool = sb("wpool", [P, PG, P], ctx=c1)
    tmpa = sb("tmpa", [P, N], ctx=c1)
    T1even = sb("T1", [P, 3, 2, P], ctx=c1)
    T1s = [T1even[:, :, :, :], lr_or_decay[:, 0:768].rearrange("p (w a t) -> p w a t", w=3, a=2)]
    T2s = [t.rearrange("p (a i t) -> p a i t", a=2, i=4) for t in (xn[:, 1, :], g1b[:, :])]
    Pm = scratch[:, 8320:8832].rearrange("p (h t) -> p h t", h=HEADS)
    khN = scratch[:, 8832:9088].rearrange("p (a d) -> p a d", a=2)
    o2 = scratch[:, 7296:7808]
    hist = o2[0:DEC_B * HIST, :]
    qz = xn[:, 0, :].rearrange("p (w h t) -> p w h t", w=2, h=HEADS)
    KM = xn[0:NS, :, :].rearrange("p a (b d) -> p (a b) d", d=256)
    rs = scratch[:, 7808:8320]
    rmid = sb("rmid", [P, 2, SEQ // SB], ctx=c1)
    mask_p = sb("mask_p", [P, P], ctx=c1)
    mask_s = sb("mask_s", [NS, NS], ctx=c1)
    bmask = sb("bmask", [NS, DEC_B], ctx=c1)
    resets = sb("resets", [P, NS], ctx=c1)
    onesN = sb("onesN", [P, P], ctx=c1)
    icnt = sb("icnt", [P, 16], ctx=c1)
    sdecs = sb("sdec", [P, 2, 2], ctx=c1)
    o_dec = sb("o_dec", [P, 2, DEC_B], ctx=c1)
    npS = tmpa[0:NS, 256:768]
    npP = scratch[0:HIST, 2 * POOL_AT:2 * POOL_AT + 512]
    wsum = [scratch[:, POOL_AT * j:POOL_AT * (j + 1)] for j in range(2)]
    edge = scratch[:, 9088:9088 + 96]

    s_const = sem("s_const")
    s_x = [sem(f"s_x{j}") for j in range(5)]
    s_g1 = sem("s_g1")
    s_ku = sem("s_ku")
    s_ssq, s_rt, s_rstd, s_xn = sem("s_ssq"), sem("s_rt"), sem("s_rstd"), sem("s_xn")
    s_tr = sem("s_tr")
    s_tra, s_trd = sem("s_tra"), sem("s_trd")
    s_wlr = sem("s_wlr")
    s_qh, s_ql, s_qu = sem("s_qh"), sem("s_ql"), sem("s_qu")
    s_vh, s_vl = sem("s_vh"), sem("s_vl")
    s_th, s_tl, s_tu = sem("s_th"), sem("s_tl"), sem("s_tu")
    s_um = sem("s_um")
    s_grp = sem("s_grp")
    s_eva, s_evd = sem("s_eva"), sem("s_evd")
    s_gc = sem("s_gc")
    s_hist, s_histev = sem("s_hist"), sem("s_histev")
    s_za, s_b = sem("s_za"), sem("s_b")
    s_d = sem("s_d")
    s_args, s_exp, s_kq, s_score = sem("s_args"), sem("s_exp"), sem("s_kq"), sem("s_score")
    s_khn, s_pm, s_o, s_sq, s_ms, s_rs, s_on, s_st = [sem(x) for x in (
        "s_khn", "s_pm", "s_o", "s_sq", "s_ms", "s_rs", "s_on", "s_st")]
    s_pool, s_pmix = sem("s_pool"), sem("s_pmix")
    s_np, s_npev, s_npo = sem("s_np"), sem("s_npev"), sem("s_npo")
    s_km, s_us = sem("s_km"), sem("s_us")
    s_s0, s_silu = sem("s_s0"), sem("s_silu")
    s_a = sem("s_a")

    groups = [(kind, m, b) for b in range(3) for kind, m in (("lr", 0), ("k", 0), ("k", 1))]
    groups += [("z", p, b) for p in range(2) for b in range(3)] + [("q", p, b) for b in range(3) for p in range(2)]
    groups += [("v", 0, t) for t in range(TT)]
    g_list = [("g", m, b) for m in range(4) for b in range(3)]
    between = [[[("u", c, b)] for b in range(3)] for c in range(4)]
    between += [[[g_list[2 * c]], [g_list[2 * c + 1]], [("mix", c, b) for b in range(3)]] for c in range(4)]
    between += [[[g_list[8]], [g_list[9]], g_list[10:12]]]
    groups += [g for chunk in between for part in chunk for g in part]
    index = {g: n for n, g in enumerate(groups)}
    ON_ACT = {"lr", "k", "q", "u", "mix"}
    unit = {"k": 0, "q": 1, "v": 2, "u": 4, "g": 6}

    def evacs(n, on_act):
        return sum((g[0] in ON_ACT) == on_act for g in groups[:n + 1])

    def out_sem(n):
        on_act = groups[n][0] in ON_ACT
        return (s_eva if on_act else s_evd), evacs(n, on_act)

    def acc(n):
        return bank[5 + n % 3]

    def pooled(m):
        return wsum[m % 2][:, 0:N]

    def q_weights(k, half):
        return halves[:, k * 512 + half * 256:k * 512 + (half + 1) * 256]

    def q_tokens(k, half, tn):
        return halves[:, 4096 + k * 768 + half * 384:4096 + k * 768 + half * 384 + tn]

    def v_weights(k, half):
        return halves[:, k * 1024 + half * 512:k * 1024 + (half + 1) * 512]

    def v_tokens(n, half):
        at = 8192 + (2048, 0, 1024)[n % 3] + 512 * half
        return halves[:, at:at + 512].rearrange("p (k t) -> p k t", k=4)

    def half_used(eng, n):
        if n % 2 == 0:
            eng.wait_ge(s_tu, n // 2 + 1)
        else:
            eng.wait_ge(s_grp, index[("v", 0, n // 2)] + 1)

    V_FREE = index[("q", 1, 2)] + 1

    def q_split(eng, b, split):
        t0, tn = BLK[b]
        for k in range(KC):
            if b >= 1 and k < KC - 1:
                eng.wait_ge(s_qu, (KC - 1) * (b - 1) + k + 1)
            elif b >= 1:
                eng.wait_ge(s_grp, index[("q", 1, b - 1)] + 1)
            split(k, hT[:, k, t0:t0 + tn], q_tokens(k, 0, tn), q_tokens(k, 1, tn))

    block = ExitStack()
    blk = block.enter_context(nc.Block())

    @blk.gpsimd
    def _(pool):
        nc.gpsimd.memset(ident[:], 0.0).then_inc(s_gc, 1)
        nc.gpsimd.memset(mask_p[:], 1.0).then_inc(s_gc, 1)
        nc.gpsimd.memset(mask_s[:], 1.0).then_inc(s_gc, 1)
        nc.gpsimd.memset(bmask[:], 1.0).then_inc(s_gc, 1)
        nc.gpsimd.memset(resets[:], 1.0).then_inc(s_gc, 1)
        nc.gpsimd.memset(onesf[:], 1.0).then_inc(s_gc, 1)
        nc.gpsimd.memset(onesN[:], 1.0 / DV).then_inc(s_gc, 1)
        nc.gpsimd.memset(eps_c[:], EPS).then_inc(s_gc, 1)
        nc.gpsimd.memset(Pm, 0.0).then_inc(s_gc, 1)
        nc.gpsimd.iota(icnt[:], [[1, 16]], base=1, channel_multiplier=0,
                       allow_small_or_imprecise_dtypes=True).then_inc(s_gc, 1)
        pool.wait_ge(s_gc, 10)
        nc.gpsimd.affine_select(out=ident[:], in_=ident[:], pattern=[[-1, P]], compare_op=ALU.not_equal, fill=1.0,
                                base=0, channel_multiplier=1).then_inc(s_gc, 1)
        nc.gpsimd.affine_select(out=mask_p[:], in_=mask_p[:], pattern=[[1, P]], compare_op=ALU.is_ge, fill=0.0,
                                base=0, channel_multiplier=-1).then_inc(s_gc, 1)
        nc.gpsimd.affine_select(out=mask_s[:], in_=mask_s[:], pattern=[[1, NS]], compare_op=ALU.is_ge, fill=0.0,
                                base=0, channel_multiplier=-1).then_inc(s_gc, 1)
        nc.gpsimd.affine_select(out=bmask[:], in_=bmask[:], pattern=[[-DEC_T, DEC_B]], compare_op=ALU.is_ge,
                                fill=0.0, base=0, channel_multiplier=1).then_inc(s_gc, 1)
        nc.gpsimd.memset(resets[:].rearrange("p (b t) -> p b t", t=DEC_T)[:, :, 0:1], 0.0).then_inc(s_gc, 1)
        pool.wait_ge(s_gc, 15)
        nc.gpsimd.affine_select(out=bmask[:], in_=bmask[:], pattern=[[DEC_T, DEC_B]], compare_op=ALU.is_ge,
                                fill=0.0, base=DEC_T - 1, channel_multiplier=-1).then_inc(s_gc, 1)
        nc.gpsimd.affine_select(out=mask_s[:].rearrange("s (b t) -> s b t", t=DEC_T),
                                in_=mask_s[:].rearrange("s (b t) -> s b t", t=DEC_T),
                                pattern=[[-DEC_T, DEC_B], [0, DEC_T]], compare_op=ALU.is_ge, fill=0.0, base=0,
                                channel_multiplier=1).then_inc(s_gc, 1)
        pool.wait_ge(s_grp, index[("v", 0, TT - 1)] + 1)
        nc.gpsimd.memset(uT[:, :, 0:U_P], 0.0).then_inc(s_um, 1)
    GC = 17

    @blk.sync
    def _(sp):
        def load_x(i):
            if i >= 5:
                sp.wait_ge(s_xn, i - 4)
            sp.dma_start(x1[0:ROWS[i], X_AT[i % 5], :], x_rows[i]).then_inc(s_x[i % 5], 16)

        def load_unit(n, src):
            sp.dma_start(ring[:, n % 4, :, :], src).then_inc(s_w[n % 4], 16)

        units = [C_K, C_Q, C_V, C_V + 256, C_U, C_U + 256, C_G, C_G + 256]
        load_x(0)
        sp.dma_start(g1b[:], A["norm1_g"].broadcast_to([P, D])).then_inc(s_g1, 16)
        load_x(1)
        load_x(2)
        sp.dma_start(wlr[:], w_in[:, :, C_L:C_L + LR]).then_inc(s_wlr, 16)
        load_unit(0, w_in[:, :, units[0]:units[0] + 256])
        for i in range(3, TT):
            load_x(i)
        with nc.allow_non_contiguous_dma(reason="small vectors, one value a partition"):
            sp.dma_start(bgk[:], A["b_gk"].rearrange("l (a p) -> p (l a)", p=P)).then_inc(s_const, 16)
            sp.dma_start(pscale[:], A["pool_scale"].rearrange("l (a p) -> p (l a)", p=P)).then_inc(s_const, 16)
            sp.dma_start(gnorm[:], A["gla_norm_g"].rearrange("l p -> p l")).then_inc(s_const, 16)
        sp.dma_start(wgk2[:], A["w_gk2"][0]).then_inc(s_const, 16)
        sp.dma_start(wpool[:], A["w_pool"][0].rearrange("g c d -> c g d")).then_inc(s_const, 16)
        sp.dma_start(hist, A["state_pool"][0].rearrange("b t c -> (b t) c")).then_inc(s_const, 16)
        for u in range(1, 4):
            load_unit(u, w_in[:, :, units[u]:units[u] + 256])
        for b in range(DEC_B):
            sp.dma_start(O[4][0, b, 0:HIST - DEC_T, :], A["state_pool"][0, b, DEC_T:HIST, :]).then_inc(s_npo, 16)
        last = [index[("k", 1, 2)], index[("q", 1, 2)], index[("v", 0, 8)], index[("v", 0, 8)],
                index[("u", 1, 2)], index[("u", 3, 2)], index[("g", 1, 2)], index[("g", 3, 2)]]
        for n in range(4, 12):
            sp.wait_ge(s_grp, last[n - 4] + 1)
            if n < 8:
                load_unit(n, w_in[:, :, units[n]:units[n] + 256])
            if n == 6:
                for a in range(2):
                    sp.dma_start(S0[64 * a:64 * a + 64, :, :, :],
                                 A["state_gla"][0].rearrange("b (p a) k v -> a k b p v", a=2)[a]).then_inc(s_s0, 16)
            if n >= 8:
                load_unit(n, w_out[:, :, (n - 8) * 256:(n - 7) * 256])
        sp.wait_ge(s_npev, 1)
        sp.dma_start(O[2][0, 0], npP).then_inc(s_npo, 16)
        for b in range(DEC_B):
            sp.dma_start(O[4][0, b, HIST - DEC_T:HIST, :], npS[b * DEC_T:(b + 1) * DEC_T, :]).then_inc(s_npo, 16)
        sp.wait_ge(s_npo, 16 * (2 * DEC_B + 1))

    @blk.tensor
    def _(pe):
        def turn(i):
            r = ROWS[i]
            pe.wait_ge(s_xn, i + 1)
            for h in range(2):
                if i >= 2:
                    pe.wait_ge(s_trd if h else s_tra, i - 1)
                for k in range(4):
                    t = nc.tensor.transpose(bank[2 * (i % 2) + h][:, k * P:k * P + r],
                                            xn[0:r, i % 2, (4 * h + k) * P:(4 * h + k + 1) * P], ident[0:r, 0:r])
                t.then_inc(s_tr, 1)

        def group(kind, m, b):
            n = index[(kind, m, b)]
            if n >= 3:
                s, c = out_sem(n - 3)
                pe.wait_ge(s, c)
            if kind in unit and kind not in "qv":
                u = unit[kind] + (0 if kind == "k" else m // 2)
                pe.wait_ge(s_w[u % 4], 16 * (u // 4 + 1))
            if kind == "lr":
                t0, tn = BLK[b]
                for k in range(KC):
                    mm = nc.tensor.matmul(acc(n)[0:LR, 0:tn], wlr[:, k, :], hT[:, k, t0:t0 + tn],
                                          start=k == 0, stop=k == KC - 1)
            elif kind == "z":
                t0, tn = BLK[b]
                mm = nc.tensor.matmul(acc(n)[:, 0:tn], wgk2[:, m * P:(m + 1) * P], lrT[:, t0:t0 + tn],
                                      start=True, stop=True)
            elif kind == "mix":
                t0, tn = BLK[b]
                mm = nc.tensor.matmul(acc(n)[:, 0:tn], wpool[:, m, :], pooled(m)[:, t0:t0 + tn],
                                      start=True, stop=True)
            elif kind == "q":
                tn = BLK[b][1]
                for k in range(KC):
                    pe.wait_ge(s_ql, KC * (b + 1) + k + 1)
                    whi, wlo = [q_weights(k, half)[:, m * P:(m + 1) * P] for half in range(2)]
                    out = acc(n)[:, 0:tn]
                    nc.tensor.matmul(out, whi, q_tokens(k, 0, tn), start=k == 0, stop=False)
                    nc.tensor.matmul(out, whi, q_tokens(k, 1, tn), start=False, stop=False)
                    mm = nc.tensor.matmul(out, wlo, q_tokens(k, 0, tn), start=False, stop=k == KC - 1)
                    if m == 1 and k < KC - 1:
                        mm.then_inc(s_qu, 1)
            elif kind == "v":
                r = ROWS[b]
                out = acc(n)[0:r, :]
                for k in range(KC):
                    pe.wait_ge(s_tl, 2 * b + k // 4 + 1)
                    if b == 0:
                        pe.wait_ge(s_vl, k + 1)
                    hi, lo = [v_tokens(2 * b + k // 4, half)[:, k % 4, 0:r] for half in range(2)]
                    nc.tensor.matmul(out, hi, v_weights(k, 0), start=k == 0, stop=False)
                    nc.tensor.matmul(out, hi, v_weights(k, 1), start=False, stop=False)
                    mm = nc.tensor.matmul(out, lo, v_weights(k, 0), start=False, stop=k == KC - 1)
                    if k == 3:
                        mm.then_inc(s_tu, 1)
            else:
                t0, tn = BLK[b]
                c0 = (m % 2) * P
                for k in range(KC):
                    mm = nc.tensor.matmul(acc(n)[:, 0:tn], ring[:, u % 4, k, c0:c0 + P], hT[:, k, t0:t0 + tn],
                                          start=k == 0, stop=k == KC - 1)
            mm.then_inc(s_grp, 1)

        pe.wait_ge(s_gc, GC)
        for i in range(3):
            turn(i)
        for b in range(3):
            if b < 2:
                turn(3 * b + 3)
            pe.wait_ge(s_tra, 3 * b + 3)
            pe.wait_ge(s_trd, 3 * b + 3)
            if b == 0:
                pe.wait_ge(s_wlr, 16)
            group("lr", 0, b)
            if b < 2:
                turn(3 * b + 4)
            group("k", 0, b)
            if b < 2:
                turn(3 * b + 5)
            group("k", 1, b)
        pe.wait_ge(s_const, 16 * 6)
        for m in range(PG):
            t = nc.tensor.transpose(bank[0][:, m * P:m * P + DEC_B * HIST], hist[:, m * P:(m + 1) * P],
                                    ident[0:DEC_B * HIST, 0:DEC_B * HIST])
        t.then_inc(s_hist, 1)
        pe.wait_ge(s_eva, evacs(index[("lr", 0, 2)], True))
        for m in range(2):
            for b in range(3):
                group("z", m, b)
        for b in range(3):
            for m in range(2):
                group("q", m, b)
        for t in range(TT):
            group("v", 0, t)

        def attend_scores(c):
            T1, T2 = T1s[c % 2], T2s[c % 2]
            n = ROWS[c]
            if c >= 1:
                pe.wait_ge(s_pm, c)
                pe.wait_ge(s_khn, c)
            else:
                pe.wait_ge(s_histev, 1)
            pe.wait_ge(s_kq, c + 1)
            for h in range(HEADS):
                p = h // 2
                if c < TT - 1:
                    for i in range(4):
                        m = SB * (i + 1)
                        nc.tensor.matmul(bank[0][0:m, h * P + SB * i:h * P + SB * (i + 1)], T2[:, p, i, 0:m],
                                         qz[:, 0, h, SB * i:SB * (i + 1)], start=True, stop=True)
                else:
                    nc.tensor.matmul(bank[0][0:n, h * P:h * P + n], T2[:, p, 0, 0:n], qz[:, 0, h, 0:n],
                                     start=True, stop=True)
            for p in range(2):
                t = nc.tensor.transpose(bank[1][0:n, p * P:(p + 1) * P], T1[:, 2, p, 0:n], ident[:])
            t.then_inc(s_score, 1)

        def attend_out(c):
            n = ROWS[c]
            if c == TT - 1:
                pe.wait_ge(s_s0, 32)
            pe.wait_ge(s_pm, c + 1)
            pe.wait_ge(s_khn, c + 1)
            if c >= 1:
                pe.wait_ge(s_st, c)
                pe.wait_ge(s_on, c)
            for h in range(HEADS):
                p = h // 2
                o = nc.tensor.matmul(bank[2][:, h * P:h * P + n], v[0:n, c, h * DV:(h + 1) * DV], Pm[0:n, h, 0:n],
                                     start=h == 0 or c < TT - 1, stop=c == 0, skip_group_check=c == TT - 1)
                if c < TT - 1:
                    if c > 0:
                        o = nc.tensor.matmul(bank[2][:, h * P:h * P + n], Sp[:, p, :], qz[:, 1, h, 0:n],
                                             start=False, stop=True)
            if c == TT - 1:
                for b in range(DEC_B):
                    t0 = b * DEC_T
                    for p in range(2):
                        o = nc.tensor.matmul(
                            bank[2][:, 2 * p * P:2 * (p + 1) * P].rearrange("v (a t) -> v a t", a=2)[:, :, t0:t0 + DEC_T],
                            S0[:, b, p, :], qz[:, 1, 2 * p:2 * p + 2, t0:t0 + DEC_T], start=False, stop=True,
                            skip_group_check=True)
            if c < TT - 1:
                for p in range(2):
                    o = nc.tensor.matmul(bank[3][:, p * 256:(p + 1) * 256], khN[:, p, :],
                                         v[:, c, p * 256:(p + 1) * 256], start=True, stop=True)
            o.then_inc(s_o, 1)

        def attend_norm(c):
            n = ROWS[c]
            pe.wait_ge(s_sq, c + 1)
            if c >= 1:
                pe.wait_ge(s_rs, c)
            nc.tensor.matmul(bank[4][:, :], onesN[:], o2, start=True,
                             stop=True).then_inc(s_ms, 1)

        def rows_of_state():
            pe.wait_ge(s_eva, evacs(index[("u", 3, 2)], True))
            pe.wait_ge(s_pm, 4)
            pe.wait_ge(s_khn, 4)
            for m in range(PG):
                nc.tensor.transpose(bank[0][0:HIST, m * P:(m + 1) * P], uT[:, m, U_S - HIST:U_S], ident[:])
                t = nc.tensor.transpose(bank[1][0:NS, m * P:(m + 1) * P], tmpa[:, m * NS:(m + 1) * NS], ident[:])
            t.then_inc(s_np, 1)

        def fill(c, part):
            for kind, m, b in between[c][part]:
                if kind == "mix" and b == 0:
                    pe.wait_ge(s_pool, m + 1)
                group(kind, m, b)

        for c in range(TT):
            if c == 4:
                rows_of_state()
            fill(c, 0)
            if c == 4:
                pe.wait_ge(s_npev, 1)
            attend_scores(c)
            fill(c, 1)
            attend_out(c)
            fill(c, 2)
            attend_norm(c)
        pe.wait_ge(s_km, 1)
        for b in range(DEC_B):
            if b >= 2:
                pe.wait_ge(s_us, b - 1)
            for p in range(2):
                t = nc.tensor.matmul(bank[[0, 3][b % 2]][:, p * 256:(p + 1) * 256], KM[:, b, p * P:(p + 1) * P],
                                     v[0:NS, TT - 1, p * 256:(p + 1) * 256], start=True, stop=True)
            t.then_inc(s_ku, 1)

    @blk.scalar
    def _(act):
        def square(i):
            r = ROWS[i]
            act.wait_ge(s_x[i % 5], 16 * (i // 5 + 1))
            nc.scalar.activation(tmpa[0:r, 0:D], x1[0:r, X_AT[i % 5], :], ACT.Square, scale=D ** -0.5,
                                 accum_out=ssq[0:r, i:i + 1]).then_inc(s_ssq, 1)
            act.wait_ge(s_ssq, i + 1)
            nc.scalar.activation(rstd[0:r, TT + i:TT + i + 1], ssq[0:r, i:i + 1], ACT.Sqrt,
                                 bias=eps_c[0:r, :]).then_inc(s_rt, 1)

        def turned(i):
            act.wait_ge(s_tr, 2 * i + 1)
            nc.scalar.copy(hT[:, 0:4, i * P:i * P + ROWS[i]],
                           bank[2 * (i % 2)][:, :].rearrange("p (k t) -> p k t", t=P)[:, :, 0:ROWS[i]]).then_inc(s_tra, 1)

        def evac(kind, m, b):
            n = index[(kind, m, b)]
            act.wait_ge(s_grp, n + 1)
            t0, tn = BLK[b]
            a = acc(n)
            if kind == "lr":
                nc.scalar.copy(lrT[:, t0:t0 + tn], a[0:LR, 0:tn]).then_inc(s_eva, 1)
            elif kind == "k":
                nc.scalar.copy(kT[:, m, t0:t0 + tn], a[:, 0:tn]).then_inc(s_eva, 1)
            elif kind == "q":
                nc.scalar.mul(qT[:, m, t0:t0 + tn], a[:, 0:tn], DK ** -0.5).then_inc(s_eva, 1)
            elif kind == "u":
                pn = min(tn, SEQ - t0)
                if pn == tn:
                    nc.scalar.copy(uT[:, m, U_P + t0:U_P + t0 + tn], a[:, 0:tn]).then_inc(s_eva, 1)
                else:
                    nc.scalar.copy(uT[:, m, U_P + t0:U_P + t0 + pn], a[:, 0:pn])
                    nc.scalar.copy(tmpa[:, m * NS:(m + 1) * NS], a[:, pn:tn])
                    nc.scalar.copy(uT[:, m, U_S:].rearrange("p (b t) -> p b t", t=SEG)[:, :, HIST:],
                                   a[:, pn:tn].rearrange("p (b t) -> p b t", t=DEC_T)).then_inc(s_eva, 1)
            elif kind == "mix":
                nc.scalar.activation(uT[:, m, t0:t0 + tn], a[:, 0:tn], ACT.Copy,
                                     scale=pscale[:, m:m + 1]).then_inc(s_eva, 1)

        act.wait_ge(s_gc, GC)
        nc.scalar.activation(warm[:], eps_c[:], ACT.Sqrt)
        for i in range(TT):
            square(i)
            if i >= 1:
                turned(i - 1)
            if i == 5:
                evac("lr", 0, 0)
                evac("k", 0, 0)
            elif i == 6:
                evac("k", 1, 0)
        turned(TT - 1)
        act.wait_ge(s_w[1], 16)
        for k in range(KC):
            nc.scalar.copy(q_weights(k, 0), ring[:, 1, k, :]).then_inc(s_qh, 1)

        def split_hi(k, src, hi, lo):
            nc.scalar.copy(hi, src).then_inc(s_qh, 1)

        act.wait_ge(s_trd, 3)
        act.wait_ge(s_tra, 3)
        q_split(act, 0, split_hi)
        for b in (1, 2):
            for kind, m in (("lr", 0), ("k", 0), ("k", 1)):
                evac(kind, m, b)
        def v_tile_hi(n):
            r, t0, k0 = ROWS[n // 2], n // 2 * P, n % 2 * 4
            if n >= 3:
                half_used(act, n - 3)
            elif n >= 1:
                act.wait_ge(s_grp, V_FREE)
            nc.scalar.copy(v_tokens(n, 0)[:, :, 0:r], hT[:, k0:k0 + 4, t0:t0 + r]).then_inc(s_th, 1)

        for m in range(2):
            act.wait_ge(s_evd, 3 * m + 3)
            if m:
                act.wait_ge(s_b, m)
            nc.scalar.activation(tmpa[:], bT[:, m, :], ACT.Abs).then_inc(s_a, 1)
            act.wait_ge(s_a, 2 * m + 1)
            nc.scalar.activation(tmpa[:], tmpa[:], ACT.Exp, scale=-1.0).then_inc(s_a, 1)
            act.wait_ge(s_a, 2 * m + 2)
            nc.scalar.activation(tmpa[:], tmpa[:], ACT.Ln, bias=1.0).then_inc(s_za, 1)
        act.wait_ge(s_trd, TT)
        act.wait_ge(s_tra, TT)
        evac("q", 0, 0)
        q_split(act, 1, split_hi)
        evac("q", 1, 0)
        evac("q", 0, 1)
        q_split(act, 2, split_hi)
        evac("q", 1, 1)
        evac("q", 0, 2)
        act.wait_ge(s_w[2], 16)
        act.wait_ge(s_w[3], 16)
        for k in range(KC):
            if k < 3:
                act.wait_ge(s_qu, (KC - 1) * 2 + 2 * k + 2)
            else:
                act.wait_ge(s_grp, V_FREE)
            nc.scalar.copy(v_weights(k, 0).rearrange("p (u n) -> p u n", u=2), ring[:, 2:4, k, :]).then_inc(s_vh, 1)
            if k == 0:
                v_tile_hi(0)
        evac("q", 1, 2)
        for n in range(1, 2 * TT):
            v_tile_hi(n)
        act.wait_ge(s_grp, index[("v", 0, TT - 1)] + 1)
        act.wait_ge(s_hist, 1)
        nc.scalar.copy(uT[:, :, U_S:].rearrange("p m (b t) -> p m b t", t=SEG)[:, 0:2, :, 0:HIST],
                       bank[0][:, :].rearrange("p (m x) -> p m x", m=PG)[:, 0:2, 0:DEC_B * HIST].rearrange(
                           "p m (b t) -> p m b t", t=HIST))
        nc.scalar.copy(uT[:, :, U_S:].rearrange("p m (b t) -> p m b t", t=SEG)[:, 2:4, :, 0:HIST],
                       bank[0][:, :].rearrange("p (m x) -> p m x", m=PG)[:, 2:4, 0:DEC_B * HIST].rearrange(
                           "p m (b t) -> p m b t", t=HIST)).then_inc(s_histev, 1)

        def exps(c):
            n = ROWS[c]
            T1, T2 = T1s[c % 2], T2s[c % 2]
            act.wait_ge(s_args, c + 1)
            if c < TT - 1:
                nc.scalar.activation(T1.rearrange("p a b t -> p (a b t)"),
                                     T1.rearrange("p a b t -> p (a b t)"), ACT.Exp, scale=1.0 / GATE)
                nc.scalar.activation(T2.rearrange("p a b t -> p (a b t)"),
                                     T2.rearrange("p a b t -> p (a b t)"), ACT.Exp,
                                     scale=1.0 / GATE).then_inc(s_exp, 1)
            else:
                nc.scalar.activation(T1[:, :, :, 0:n].rearrange("p a b t -> p (a b) t"),
                                     T1[:, :, :, 0:n].rearrange("p a b t -> p (a b) t"), ACT.Exp, scale=1.0 / GATE)
                nc.scalar.activation(T2[:, :, 0, 0:n], T2[:, :, 0, 0:n], ACT.Exp, scale=1.0 / GATE).then_inc(s_exp, 1)

        def keys_rows(c):
            n = ROWS[c]
            act.wait_ge(s_score, c + 1)
            nc.scalar.copy(khN[0:n, :, :], bank[1][0:n, 0:256].rearrange("p (a d) -> p a d", a=2)).then_inc(s_khn, 1)

        def squares(c):
            act.wait_ge(s_o, c + 1)
            nc.scalar.activation(o2 if ROWS[c] == P else o2.rearrange("p (h t) -> p h t", h=HEADS)[:, :, 0:NS],
                                 bank[2][:, :] if ROWS[c] == P else
                                 bank[2][:, :].rearrange("p (h t) -> p h t", h=HEADS)[:, :, 0:NS],
                                 ACT.Square).then_inc(s_sq, 1)

        def inv_root(c):
            act.wait_ge(s_ms, c + 1)
            if c >= 1:
                act.wait_ge(s_on, c)
            nc.scalar.activation(rs, bank[4][:, :], ACT.Ln, bias=eps_c[:]).then_inc(s_a, 1)
            act.wait_ge(s_a, 5 + c)
            nc.scalar.activation(rs, rs, ACT.Exp, scale=-0.5).then_inc(s_rs, 1)

        def fill(c, part):
            for g in between[c][part]:
                if g[0] in ON_ACT:
                    evac(*g)

        def silu(m):
            nc.scalar.activation(gT[:, m, :], gT[:, m, :], ACT.Silu).then_inc(s_silu, 1)

        exps(0)
        exps(1)
        for c in range(TT):
            if c == 4:
                act.wait_ge(s_np, 1)
                nc.scalar.copy(npP, bank[0][0:HIST, :])
                nc.scalar.copy(npS, bank[1][0:NS, :]).then_inc(s_npev, 1)
            fill(c, 0)
            keys_rows(c)
            if c == TT - 1:
                act.wait_ge(s_evd, out_sem(index[("g", 2, 2)])[1])
                for m in range(3):
                    silu(m)
            fill(c, 1)
            squares(c)
            fill(c, 2)
            inv_root(c)
            if c + 2 < TT:
                exps(c + 2)
        act.wait_ge(s_evd, evacs(len(groups) - 1, False))
        silu(3)

    @blk.vector
    def _(dve):
        chain = [0]

        def link(ins):
            chain[0] += 1
            ins.then_inc(s_d, 1)
            dve.wait_ge(s_d, chain[0])

        dve.wait_ge(s_gc, GC)
        link(nc.vector.reciprocal(icnt[:], icnt[:]))

        def turned(i):
            dve.wait_ge(s_tr, 2 * i + 2)
            nc.vector.tensor_copy(hT[:, 4:8, i * P:i * P + ROWS[i]],
                                  bank[2 * (i % 2) + 1][:, :].rearrange("p (k t) -> p k t", t=P)[:, :, 0:ROWS[i]]
                                  ).then_inc(s_trd, 1)

        for i in range(TT):
            r = ROWS[i]
            dve.wait_ge(s_rt, i + 1)
            link(nc.vector.reciprocal(rstd[0:r, i:i + 1], rstd[0:r, TT + i:TT + i + 1]))
            if i == 0:
                dve.wait_ge(s_g1, 16)
            if i >= 2:
                dve.wait_ge(s_tr, 2 * (i - 1))
            nc.vector.scalar_tensor_tensor(out=xn[0:r, i % 2, :], in0=x1[0:r, X_AT[i % 5], :],
                                           scalar=rstd[0:r, i:i + 1], in1=g1b[0:r, :], op0=ALU.mult,
                                           op1=ALU.mult).then_inc(s_xn, 1)
            if i >= 1:
                turned(i - 1)
        turned(TT - 1)
        dve.wait_ge(s_const, 16 * 6)

        def evac(kind, m, b):
            n = index[(kind, m, b)]
            dve.wait_ge(s_grp, n + 1)
            a = acc(n)
            if kind == "v":
                nc.vector.tensor_copy(v[0:ROWS[b], b, :], a[0:ROWS[b], :]).then_inc(s_evd, 1)
                return
            t0, tn = BLK[b]
            if kind == "z":
                nc.vector.tensor_scalar(bT[:, m, t0:t0 + tn], a[:, 0:tn], bgk[:, m:m + 1], None,
                                        ALU.add).then_inc(s_evd, 1)
            else:
                nc.vector.tensor_copy(gT[:, m, t0:t0 + tn], a[:, 0:tn]).then_inc(s_evd, 1)

        for k in range(KC):
            dve.wait_ge(s_qh, k + 1)
            nc.vector.tensor_tensor(q_weights(k, 1), ring[:, 1, k, :], q_weights(k, 0).bitcast(F32),
                                    ALU.subtract).then_inc(s_ql, 1)
        splits = [KC]

        def split_lo(k, src, hi, lo):
            splits[0] += 1
            dve.wait_ge(s_qh, splits[0])
            nc.vector.tensor_tensor(lo, src, hi.bitcast(F32), ALU.subtract).then_inc(s_ql, 1)

        dve.wait_ge(s_tra, 3)
        dve.wait_ge(s_trd, 3)
        q_split(dve, 0, split_lo)
        for m in range(2):
            for b in range(3):
                evac("z", m, b)
        for m in range(2):
            dve.wait_ge(s_za, m + 1)
            nc.vector.scalar_tensor_tensor(out=bT[:, m, :], in0=bT[:, m, :], scalar=0.0, in1=tmpa[:], op0=ALU.min,
                                           op1=ALU.subtract).then_inc(s_b, 1)
            dve.wait_ge(s_b, m + 1)
        dve.wait_ge(s_tra, TT)
        dve.wait_ge(s_trd, TT)
        q_split(dve, 1, split_lo)
        for c in range(TT):
            for m in range(2):
                n = ROWS[c]
                sl = bT[:, m, c * P:c * P + n]
                ch = nc.vector.tensor_tensor_scan(sl, onesf[:, 0:n] if n == P else resets[:], sl, 0.0,
                                                  ALU.mult, ALU.add)
        link(ch)
        link(nc.vector.tensor_copy(rmid[:, :, :],
                                   bT[:, :, 0:SEQ].rearrange("p a (i t) -> p a i t", t=SB)[:, :, :, SB // 2 - 1]))

        def args(c):
            n = ROWS[c]
            B = bT[:, :, c * P:c * P + n]
            T1, T2 = T1s[c % 2], T2s[c % 2]
            if c >= 2:
                dve.wait_ge(s_score, c - 1)
            if c < TT - 1:
                r = rmid[:, :, 4 * c:4 * c + 4]
                nc.vector.tensor_tensor(T1[:, 0, :, :].rearrange("p a (i t) -> p a i t", t=SB),
                                        B.rearrange("p a (i t) -> p a i t", t=SB),
                                        r.unsqueeze(3).broadcast_to([P, 2, 4, SB]), ALU.subtract)
                nc.vector.tensor_copy(T1[:, 1, :, :], B)
                nc.vector.tensor_tensor(T1[:, 2, :, :], B[:, :, P - 1:P].broadcast_to([P, 2, P]), B, ALU.subtract)
                for p in range(2):
                    link(nc.vector.tensor_tensor(T2[:, p, :, :], r[:, p, :].unsqueeze(2).broadcast_to([P, 4, P]),
                                                 B[:, p, :].unsqueeze(1).broadcast_to([P, 4, P]), ALU.subtract))
                nc.vector.tensor_scalar(T1[:, 0, :, :], T1[:, 0, :, :], CLAMP, -CLAMP, ALU.min, ALU.max)
                nc.vector.tensor_scalar(T2, T2, CLAMP, -CLAMP, ALU.min,
                                        ALU.max).then_inc(s_args, 1)
            else:
                nc.vector.tensor_scalar(T1[:, 0, :, 0:n], B, CLAMP, -CLAMP, ALU.min, ALU.max)
                nc.vector.tensor_copy(T1[:, 1, :, 0:n], B)
                for p in range(2):
                    bl = B[:, p, :].rearrange("p (b t) -> p b t", t=DEC_T)
                    nc.vector.tensor_tensor(T1[:, 2, p, 0:n].rearrange("p (b t) -> p b t", t=DEC_T),
                                            bl[:, :, DEC_T - 1:DEC_T].broadcast_to([P, DEC_B, DEC_T]), bl,
                                            ALU.subtract)
                nc.vector.tensor_scalar(T2[:, :, 0, 0:n], B, -1.0, CLAMP, ALU.mult, ALU.min).then_inc(s_args, 1)

        def decayed_k(c):
            n = ROWS[c]
            T1, T2 = T1s[c % 2], T2s[c % 2]
            dve.wait_ge(s_exp, c + 1)
            if c == 0:
                dve.wait_ge(s_eva, evacs(index[("q", 1, 2)], True))
            k = kT[:, :, c * P:c * P + n]
            if c < TT - 1:
                nc.vector.tensor_copy(sdecs[:, c % 2, :], T1[:, 1, :, P - 1])
            else:
                nc.vector.tensor_copy(o_dec[:], T1[:, 1, :, 0:n].rearrange("p a (b t) -> p a b t",
                                                                           t=DEC_T)[:, :, :, DEC_T - 1])
            nc.vector.tensor_tensor(T1[:, 2, :, 0:n], T1[:, 2, :, 0:n], k, ALU.mult)
            if c < TT - 1:
                for p in range(2):
                    nc.vector.tensor_tensor(T2[:, p, :, :], T2[:, p, :, :],
                                            k[:, p, :].unsqueeze(1).broadcast_to([P, 4, P]), ALU.mult)
            else:
                nc.vector.tensor_tensor(T2[:, :, 0, 0:n], T2[:, :, 0, 0:n], k, ALU.mult)

        def decayed_q(c):
            n = ROWS[c]
            T1 = T1s[c % 2]
            q = qT[:, :, c * P:c * P + n]
            if c >= 1:
                dve.wait_ge(s_o, c)
            for a in range(2):
                rows = slice(64 * a, 64 * a + 64)
                x = nc.vector.tensor_tensor(qz[rows, :, :, 0:n].rearrange("p w (b a) t -> p w b a t", a=2)[:, :, :, a, :],
                                            T1[rows, 0:2, :, 0:n],
                                            q[rows, :, :].unsqueeze(1).broadcast_to([64, 2, 2, n]), ALU.mult)
            x.then_inc(s_kq, 1)

        def mask_scores(c):
            n = ROWS[c]
            dve.wait_ge(s_score, c + 1)
            S = bank[0][:, :].rearrange("p (h t) -> p h t", h=HEADS)
            if c < TT - 1:
                for i in range(4):
                    m = SB * (i + 1)
                    t = slice(SB * i, SB * (i + 1))
                    x = nc.vector.tensor_tensor(Pm[0:m, :, t], S[0:m, :, t],
                                                mask_p[0:m, t].unsqueeze(1).broadcast_to([m, HEADS, SB]), ALU.mult)
            else:
                x = nc.vector.tensor_tensor(Pm[0:n, :, 0:n], S[0:n, :, 0:n],
                                            mask_s[:].unsqueeze(1).broadcast_to([n, HEADS, n]), ALU.mult)
            x.then_inc(s_pm, 1)

        def state(c):
            dve.wait_ge(s_o, c + 1)
            for h in range(HEADS):
                p, a = h // 2, 64 * (h % 2)
                add = bank[3][a:a + 64, p * 256 + 2 * a:p * 256 + 2 * a + DV]
                if c == 0:
                    x = nc.vector.tensor_copy(Sp[a:a + 64, p, :], add)
                else:
                    x = nc.vector.scalar_tensor_tensor(out=Sp[a:a + 64, p, :], in0=Sp[a:a + 64, p, :],
                                                       scalar=sdecs[a:a + 64, c % 2, p:p + 1], in1=add, op0=ALU.mult,
                                                       op1=ALU.add)
            x.then_inc(s_st, 1)

        def out_norm(c):
            n = ROWS[c]
            dve.wait_ge(s_rs, c + 1)
            O_, R_ = bank[2][:, :], rs
            dst = v[:, c, :] if c < TT - 1 else R_
            dst = dst.rearrange("p (h t) -> p h t", h=HEADS)[:, :, 0:n]
            nc.vector.scalar_tensor_tensor(out=dst, in0=O_.rearrange("p (h t) -> p h t", h=HEADS)[:, :, 0:n],
                                           scalar=gnorm[:], in1=R_.rearrange("p (h t) -> p h t", h=HEADS)[:, :, 0:n],
                                           op0=ALU.mult, op1=ALU.mult).then_inc(s_on, 1)

        def pool_group(m):
            w = WINDOWS[m]
            full = wsum[m % 2]
            dve.wait_ge(s_eva, evacs(index[("u", m, 2)], True))
            if m == 0:
                dve.wait_ge(s_histev, 1)
                dve.wait_ge(s_um, 1)
            if m >= 2:
                dve.wait_ge(s_grp, index[("mix", m - 2, 2)] + 1)
            link(nc.vector.tensor_tensor_scan(full, uT[:, m, U_P:U_W], uT[:, m, U_P - w:U_W - w], 0.0,
                                              ALU.add, ALU.subtract))
            cur = uT[:, m, U_P:U_P + 16]
            link(nc.vector.tensor_tensor(edge[:, 0:w], full[:, 0:w], icnt[:, 0:w], ALU.mult))
            link(nc.vector.scalar_tensor_tensor(out=edge[:, 32:32 + NS].rearrange("p (b t) -> p b t", t=DEC_T),
                                           in0=full[:, SEQ:].rearrange("p (b t) -> p b t", t=SEG)[:, :, HIST:],
                                           scalar=1.0 / w,
                                           in1=uT[:, m, U_S:].rearrange("p (b t) -> p b t", t=SEG)[:, :, HIST:],
                                           op0=ALU.mult, op1=ALU.subtract))
            nc.vector.scalar_tensor_tensor(out=full[:, w:SEQ], in0=full[:, w:SEQ], scalar=1.0 / w,
                                           in1=uT[:, m, U_P + w:U_S], op0=ALU.mult, op1=ALU.subtract)
            nc.vector.tensor_tensor(full[:, 0:w], edge[:, 0:w], cur[:, 0:w], ALU.subtract)
            nc.vector.tensor_copy(full[:, SEQ:SEQ + NS], edge[:, 32:32 + NS]).then_inc(s_pool, 1)

        def fill(c, part):
            for g in between[c][part]:
                if g[0] not in ON_ACT:
                    evac(*g)

        q_split(dve, 2, split_lo)
        dve.wait_ge(s_tr, 2 * TT)
        link(nc.vector.memset(qz[:, :, :, :], 0.0))

        def v_tile_lo(n):
            r, t0, k0 = ROWS[n // 2], n // 2 * P, n % 2 * 4
            dve.wait_ge(s_th, n + 1)
            nc.vector.tensor_tensor(v_tokens(n, 1)[:, :, 0:r], hT[:, k0:k0 + 4, t0:t0 + r],
                                    v_tokens(n, 0)[:, :, 0:r].bitcast(F32), ALU.subtract).then_inc(s_tl, 1)

        for k in range(KC):
            dve.wait_ge(s_vh, k + 1)
            nc.vector.tensor_tensor(v_weights(k, 1).rearrange("p (u n) -> p u n", u=2), ring[:, 2:4, k, :],
                                    v_weights(k, 0).bitcast(F32).rearrange("p (u n) -> p u n", u=2),
                                    ALU.subtract).then_inc(s_vl, 1)
            if k == 0:
                v_tile_lo(0)
        v_tile_lo(1)
        v_tile_lo(2)
        for t in range(TT):
            for n in (2 * t + 3, 2 * t + 4):
                if n < 2 * TT:
                    v_tile_lo(n)
            evac("v", 0, t)
            if t == 1:
                args(0)
                args(1)
        decayed_k(0)
        decayed_q(0)
        for c in range(TT - 1):
            fill(c, 0)
            mask_scores(c)
            decayed_k(c + 1)
            fill(c, 1)
            decayed_q(c + 1)
            state(c)
            fill(c, 2)
            if c + 2 < TT:
                args(c + 2)
            out_norm(c)
            if 3 <= c < 7:
                pool_group(c - 3)
        def gate(m):
            dve.wait_ge(s_silu, m + 1)
            nc.vector.tensor_tensor(gT[:, m, 0:SEQ].rearrange("p (c t) -> p c t", t=P),
                                    gT[:, m, 0:SEQ].rearrange("p (c t) -> p c t", t=P),
                                    v[:, 0:TT - 1, m * P:(m + 1) * P], ALU.mult)

        def state_add(b):
            dve.wait_ge(s_ku, b + 1)
            for a in range(2):
                src = bank[[0, 3][b % 2]][64 * a:64 * a + 64, :].rearrange("p (q x) -> p q x", q=2)[
                    :, :, a * DV:(a + 1) * DV]
                x = nc.vector.tensor_tensor(S0[64 * a:64 * a + 64, b, :, :], S0[64 * a:64 * a + 64, b, :, :], src,
                                            ALU.add)
            x.then_inc(s_us, 1)

        c = TT - 1
        fill(c, 0)
        mask_scores(c)
        dve.wait_ge(s_on, c)
        for m in range(3):
            gate(m)
        fill(c, 1)
        dve.wait_ge(s_o, TT)
        dve.wait_ge(s_khn, TT)
        nc.vector.tensor_tensor(KM, khN[0:NS, :, :].rearrange("p a d -> p (a d)").unsqueeze(1).broadcast_to(
            [NS, DEC_B, 256]), bmask[:].unsqueeze(2).broadcast_to([NS, DEC_B, 256]), ALU.mult).then_inc(s_km, 1)
        for p in range(2):
            link(nc.vector.tensor_tensor(S0[:, :, p, :], S0[:, :, p, :],
                                         o_dec[:, p, :].unsqueeze(2).broadcast_to([P, DEC_B, DV]), ALU.mult))
        fill(c, 2)
        for b in range(4):
            state_add(b)
        out_norm(c)
        gate(3)
        dve.wait_ge(s_on, TT)
        nc.vector.tensor_tensor(gT[:, :, SEQ:N], gT[:, :, SEQ:N], rs.rearrange("p (h t) -> p h t", t=P)[:, :, 0:NS],
                                ALU.mult)
        for b in range(4, DEC_B):
            state_add(b)

    block.close()
    c1.close()


def b2_all(nc, A, O, S0, Sp, s_w, sb, sem, e_w, wdn, bank, ident, onesf, eps_c, uT, gT, ring, x1, x_rows, h2_dram,
           sums_dram, rank_m, table, iota_w, steps):
    c2 = ExitStack()
    whi = sb("whi", [P, KC, 512], F32R, ctx=c2)
    wlo = sb("wlo", [P, KC, 512], F32R, ctx=c2)
    ahi = sb("ahi", [P, 2, KC, P], F32R, ctx=c2)
    alo = sb("alo", [P, 2, KC, P], F32R, ctx=c2)
    h2 = sb("h2", [P, 2, D], ctx=c2)
    h2T = sb("h2T", [P, 2, KC, P], ctx=c2)
    g2b = sb("g2b", [P, D], ctx=c2)
    wr = sb("wr", [P, KC, NG + NE], ctx=c2)
    rb = sb("rb", [P, NG + NE], ctx=c2)
    ssq = sb("ssq2", [P, TT], ctx=c2)
    root = sb("root2", [P, TT], ctx=c2)
    rstd = sb("rstd2", [P, TT], ctx=c2)
    L = sb("L", [P, TT, NG + NE], ctx=c2)
    before = sb("before", [P, P], BF16, ctx=c2)
    onesb = sb("onesb", [P, P], BF16, ctx=c2)
    first = sb("first", [P, 4], ctx=c2)
    M = sb("M", [P, TT, NE], ctx=c2)
    M1 = sb("M1", [P, TT, NE], ctx=c2)
    M2 = sb("M2", [P, TT, NE], ctx=c2)
    Mb = sb("Mb", [P, TT, NE], BF16, ctx=c2)
    Mp = sb("Mp", [P, TT + 1, NE], BF16, ctx=c2)
    t4 = sb("t4", [P, TT, NG], ctx=c2)
    ohg = sb("ohg", [P, TT, NG], ctx=c2)
    oh1 = sb("oh1", [P, TT, 4], ctx=c2)
    oh2 = sb("oh2", [P, TT, 4], ctx=c2)
    es = sb("es", [P, TT, 4], ctx=c2)
    pr = sb("pr", [P, TT, 4, 4], ctx=c2)
    rank = pr[:].rearrange("p t g j -> p t (g j)")
    w1 = sb("w1", [P, TT], ctx=c2)
    w2 = sb("w2", [P, TT], ctx=c2)
    s1 = sb("s1", [P, TT], ctx=c2)
    s2 = sb("s2", [P, TT], ctx=c2)
    gp = sb("gp", [P, TT], ctx=c2)
    mx = sb("mx", [P, TT], ctx=c2)
    full = sb("full", [P, NE], ctx=c2)
    mxc = sb("mxc", [P, 2], ctx=c2)
    rlim = sb("rlim", [P, 8], ctx=c2)

    r_c = sem("r_c")
    s_states = sem("s_states")
    r_y, r_x1, r_ssq, r_root, r_h2, r_tr, r_trev, r_lg, r_lgev = [sem(x) for x in (
        "r_y", "r_x1", "r_ssq", "r_root", "r_h2", "r_tr", "r_trev", "r_lg", "r_lgev")]
    r_hout = [sem(f"r_hout{j}") for j in range(2)]
    r_wh, r_wl, r_wu = sem("r_wh"), sem("r_wl"), sem("r_wu")
    r_xout = sem("r_xout")
    r_ah, r_al = sem("r_ah"), sem("r_al")
    r_gc, r_d, r_ex, r_exd, r_m, r_rk, r_hf = [sem(x) for x in ("r_gc", "r_d", "r_ex", "r_exd", "r_m", "r_rk", "r_hf")]
    r_xt = [sem(f"r_xt{i}") for i in range(TT)]
    block = ExitStack()
    blk = block.enter_context(nc.Block())
    GC = 12

    @blk.gpsimd
    def _(pool):
        nc.gpsimd.memset(before[:], 1.0).then_inc(r_gc, 1)
        nc.gpsimd.memset(onesb[:], 1.0).then_inc(r_gc, 1)
        nc.gpsimd.memset(L[:], 0.0).then_inc(r_gc, 1)
        nc.gpsimd.memset(rlim[:], 0.0).then_inc(r_gc, 1)
        nc.gpsimd.iota(first[:], [[-1, 4]], base=4, channel_multiplier=0,
                       allow_small_or_imprecise_dtypes=True).then_inc(r_gc, 1)
        nc.gpsimd.iota(table[:, :, :, 0], [[0, NE], [1, TT]], base=1, channel_multiplier=0,
                       allow_small_or_imprecise_dtypes=True).then_inc(r_gc, 1)
        nc.gpsimd.iota(iota_w[:, 0:P], [[1, P]], base=0, channel_multiplier=0,
                       allow_small_or_imprecise_dtypes=True).then_inc(r_gc, 1)
        nc.gpsimd.iota(iota_w[:, P:], [[0, P // W2], [1, W2]], base=P, channel_multiplier=0,
                       allow_small_or_imprecise_dtypes=True).then_inc(r_gc, 1)
        nc.gpsimd.iota(table[:, :, :, 1], [[0, NE], [0, TT]], base=0, channel_multiplier=1,
                       allow_small_or_imprecise_dtypes=True).then_inc(r_gc, 1)
        nc.gpsimd.memset(Mp[:], 0.0).then_inc(r_gc, 1)
        pool.wait_ge(r_gc, 10)
        nc.gpsimd.affine_select(out=before[:], in_=before[:], pattern=[[1, P]], compare_op=ALU.is_gt, fill=0.0,
                                base=0, channel_multiplier=-1).then_inc(r_gc, 1)
        nc.gpsimd.iota(rlim[:, 0:ROUNDS], [[W, ROUNDS]], base=0, channel_multiplier=0,
                       allow_small_or_imprecise_dtypes=True).then_inc(r_gc, 1)

    @blk.sync
    def _(sp):
        sp.dma_start(g2b[:], A["norm2_g"].broadcast_to([P, D])).then_inc(r_c, 16)
        with nc.allow_non_contiguous_dma(reason="router weights, 16 and 64 bytes a row"):
            sp.dma_start(wr[:, :, 0:NG], A["w_router_group"][0].rearrange("(k p) n -> p k n", p=P)).then_inc(r_c, 16)
            sp.dma_start(wr[:, :, NG:], A["w_router_expert"][0].rearrange("(k p) n -> p k n", p=P)).then_inc(r_c, 16)
        sp.dma_start(rb[:, 0:NG], A["b_router_group"].broadcast_to([P, NG])).then_inc(r_c, 16)
        sp.dma_start(rb[:, NG:], A["b_router_expert"].broadcast_to([P, NE])).then_inc(r_c, 16)
        for i in range(TT):
            sp.dma_start(x1[0:ROWS[i], i, :], x_rows[i]).then_inc(r_xt[i], 16)
        for a in range(2):
            sp.dma_start(O[3][0, 0].rearrange("(p a) k v -> a k p v", a=2)[a],
                         Sp[64 * a:64 * a + 64, :, :]).then_inc(s_states, 16)
            sp.dma_start(O[5][0].rearrange("b (p a) k v -> a k b p v", a=2)[a],
                         S0[64 * a:64 * a + 64, :, :, :]).then_inc(s_states, 16)
        for u in (4, 5):
            dst, src = expert_unit(A, ring, wdn, u, 0)
            sp.dma_start(dst, src).then_inc(e_w[u], 16)
        sp.wait_ge(r_wl, 2 * KC)
        for u in range(4):
            dst, src = expert_unit(A, ring, wdn, u, 0)
            sp.dma_start(dst, src).then_inc(e_w[u], 16)
        for i in range(TT):
            sp.wait_ge(r_h2, i + 1)
            sp.dma_start(h2_dram[i * P:i * P + ROWS[i], :], h2[0:ROWS[i], i % 2, :]).then_inc(r_hout[i % 2], 16)
            sp.dma_start(sums_dram[i * P:i * P + ROWS[i], :], x1[0:ROWS[i], i, :]).then_inc(r_xout, 16)
        for j in range(2):
            sp.wait_ge(r_hout[j], 16 * len(range(j, TT, 2)))
        sp.wait_ge(r_xout, 16 * TT)
        sp.wait_ge(s_states, 16 * 4)

    @blk.tensor
    def _(pe):
        def router(i):
            r = ROWS[i]
            pe.wait_ge(r_h2, i + 1)
            if i >= 1:
                pe.wait_ge(r_trev, 2 * i)
            for h in range(2):
                for k in range(4):
                    t = nc.tensor.transpose(bank[4 + h][:, k * P:k * P + r],
                                            h2[0:r, i % 2, (4 * h + k) * P:(4 * h + k + 1) * P], ident[0:r, 0:r])
                t.then_inc(r_tr, 1)
            if i == 0:
                return
            logits(i - 1)

        def logits(i):
            r = ROWS[i]
            pe.wait_ge(r_trev, 2 * (i + 1))
            if i >= 1:
                pe.wait_ge(r_lgev, i)
            else:
                pe.wait_ge(r_c, 16 * 5)
            for k in range(KC):
                m = nc.tensor.matmul(bank[6][0:r, 0:NG + NE], h2T[:, i % 2, k, 0:r], wr[:, k, :],
                                     start=k == 0, stop=k == KC - 1)
            m.then_inc(r_lg, 1)

        for n in range(2 * TT):
            h, i = n // TT, n % TT
            r, s = ROWS[i], n % 2
            if n >= 4:
                pe.wait_ge(r_x1, n - 3)
            pe.wait_ge(r_al, n + 1)
            out = bank[n % 4][0:r, :]
            for k in range(KC):
                if i == 0:
                    pe.wait_ge(r_wl, KC * h + k + 1)
                nc.tensor.matmul(out, ahi[:, s, k, 0:r], whi[:, k, :], start=k == 0, stop=False)
                nc.tensor.matmul(out, ahi[:, s, k, 0:r], wlo[:, k, :], start=False, stop=False)
                m = nc.tensor.matmul(out, alo[:, s, k, 0:r], whi[:, k, :], start=False, stop=k == KC - 1)
                if i == TT - 1 and k < KC - 1:
                    m.then_inc(r_wu, 1)
            m.then_inc(r_y, 1)
            if h == 1 and i >= 1:
                router(i - 1)
        router(TT - 1)
        logits(TT - 1)
        pe.wait_ge(r_m, 1)
        nc.tensor.matmul(bank[7][:, 0:TT * NE], onesb[:], Mp[:, 0:TT, :].rearrange("p t e -> p (t e)"),
                         start=True, stop=False)
        nc.tensor.matmul(bank[7][:, 0:TT * NE], before[:], Mb[:].rearrange("p t e -> p (t e)"), start=False, stop=True)
        nc.tensor.matmul(bank[6][:, 0:NE], onesb[:], Mp[:, TT, :], start=True, stop=True).then_inc(r_rk, 1)

    @blk.scalar
    def _(act):
        def transposed(i):
            r = ROWS[i]
            if i >= 2:
                act.wait_ge(r_lg, i - 1)
            for h in range(2):
                act.wait_ge(r_tr, 2 * i + h + 1)
                nc.scalar.copy(h2T[:, i % 2, 4 * h:4 * h + 4, 0:r],
                               bank[4 + h][:, :].rearrange("p (k t) -> p k t", t=P)[:, :, 0:r]).then_inc(r_trev, 1)

        def tile_hi(n):
            r, t0 = ROWS[n % TT], n % TT * P
            if n >= 2:
                act.wait_ge(r_y, n - 1)
            nc.scalar.copy(ahi[:, n % 2, 0:4, 0:r], uT[:, :, t0:t0 + r])
            nc.scalar.copy(ahi[:, n % 2, 4:8, 0:r], gT[:, :, t0:t0 + r]).then_inc(r_ah, 1)

        def weights_hi(h):
            for j in (2 * h, 2 * h + 1):
                act.wait_ge(s_w[j], 48)
            for k in range(KC):
                if h == 1 and k < KC - 1:
                    act.wait_ge(r_wu, k + 1)
                elif h == 1:
                    act.wait_ge(r_y, TT)
                nc.scalar.copy(whi[:, k, :].rearrange("p (u n) -> p u n", u=2),
                               ring[:, 2 * h:2 * h + 2, k, :]).then_inc(r_wh, 1)

        tile_hi(0)
        weights_hi(0)
        for n in range(1, TT + 1):
            tile_hi(n)
        weights_hi(1)
        for i in range(TT):
            r = ROWS[i]
            if i < TT - 1:
                tile_hi(TT + i + 1)
            act.wait_ge(r_x1, TT + i + 1)
            if i >= 2:
                act.wait_ge(r_tr, 2 * (i - 1))
                act.wait_ge(r_hout[i % 2], 16 * (i // 2))
            nc.scalar.activation(h2[0:r, i % 2, :], x1[0:r, i, :], ACT.Square, scale=D ** -0.5,
                                 accum_out=ssq[0:r, i:i + 1]).then_inc(r_ssq, 1)
            act.wait_ge(r_ssq, i + 1)
            nc.scalar.activation(root[0:r, i:i + 1], ssq[0:r, i:i + 1], ACT.Sqrt,
                                 bias=eps_c[0:r, :]).then_inc(r_root, 1)
            if i >= 1:
                transposed(i - 1)
        transposed(TT - 1)
        act.wait_ge(r_exd, 1)
        nc.scalar.activation(t4[:], t4[:], ACT.Exp).then_inc(r_ex, 1)
        act.wait_ge(r_exd, 2)
        nc.scalar.activation(s2[:], s2[:], ACT.Exp).then_inc(r_ex, 1)

    @blk.vector
    def _(dve):
        chain = [0]

        def link(ins):
            chain[0] += 1
            ins.then_inc(r_d, 1)
            dve.wait_ge(r_d, chain[0])

        def logit_out(i):
            r = ROWS[i]
            dve.wait_ge(r_lg, i + 1)
            nc.vector.tensor_tensor(L[0:r, i, :], bank[6][0:r, 0:NG + NE], rb[0:r, :], ALU.add).then_inc(r_lgev, 1)

        dve.wait_ge(r_gc, GC)
        def tile_lo(n):
            r, t0 = ROWS[n % TT], n % TT * P
            dve.wait_ge(r_ah, n + 1)
            nc.vector.tensor_tensor(alo[:, n % 2, 0:4, 0:r], uT[:, :, t0:t0 + r],
                                    ahi[:, n % 2, 0:4, 0:r].bitcast(F32), ALU.subtract)
            nc.vector.tensor_tensor(alo[:, n % 2, 4:8, 0:r], gT[:, :, t0:t0 + r],
                                    ahi[:, n % 2, 4:8, 0:r].bitcast(F32), ALU.subtract).then_inc(r_al, 1)

        def weights_lo(h):
            for k in range(KC):
                dve.wait_ge(r_wh, KC * h + k + 1)
                nc.vector.tensor_tensor(wlo[:, k, :].rearrange("p (u n) -> p u n", u=2),
                                        ring[:, 2 * h:2 * h + 2, k, :],
                                        whi[:, k, :].bitcast(F32).rearrange("p (u n) -> p u n", u=2),
                                        ALU.subtract).then_inc(r_wl, 1)

        def residual(n):
            h, i = n // TT, n % TT
            r = ROWS[i]
            dve.wait_ge(r_xt[i], 16)
            dve.wait_ge(r_y, n + 1)
            nc.vector.tensor_tensor(x1[0:r, i, h * 512:(h + 1) * 512], x1[0:r, i, h * 512:(h + 1) * 512],
                                    bank[n % 4][0:r, :], ALU.add).then_inc(r_x1, 1)

        tile_lo(0)
        weights_lo(0)
        for n in range(1, TT + 1):
            tile_lo(n)
            if n < TT:
                residual(n - 1)
        weights_lo(1)
        residual(TT - 1)
        for i in range(TT):
            r = ROWS[i]
            if i < TT - 1:
                tile_lo(TT + i + 1)
            residual(TT + i)
            dve.wait_ge(r_root, i + 1)
            link(nc.vector.reciprocal(rstd[0:r, i:i + 1], root[0:r, i:i + 1]))
            if i == 0:
                dve.wait_ge(r_c, 16 * 5)
            nc.vector.scalar_tensor_tensor(out=h2[0:r, i % 2, :], in0=x1[0:r, i, :], scalar=rstd[0:r, i:i + 1],
                                           in1=g2b[0:r, :], op0=ALU.mult, op1=ALU.mult).then_inc(r_h2, 1)
            if i >= 2:
                logit_out(i - 2)
        logit_out(TT - 2)
        logit_out(TT - 1)
        dve.wait_ge(r_lgev, TT)

        def b(ap, shape):
            return ap.unsqueeze(2).broadcast_to(shape)

        def pick(oh, vals, top):
            link(nc.vector.tensor_reduce(top[:], vals, axis=AX.X, op=ALU.max))
            link(nc.vector.tensor_tensor(oh[:], vals, b(top[:], [P, TT, 4]), ALU.is_equal))
            link(nc.vector.tensor_tensor(oh[:], oh[:], first[:].unsqueeze(1).broadcast_to([P, TT, 4]), ALU.mult))
            link(nc.vector.tensor_reduce(mx[:], oh[:], axis=AX.X, op=ALU.max))
            link(nc.vector.tensor_tensor(oh[:], oh[:], b(mx[:], [P, TT, 4]), ALU.is_equal))

        gl, el = L[:, :, 0:NG], L[:, :, NG:]
        pick(ohg, gl, s1)
        nc.vector.tensor_tensor(t4[:], gl, b(s1[:], [P, TT, NG]), ALU.subtract).then_inc(r_exd, 1)
        link(nc.vector.tensor_tensor(pr[:], el.rearrange("p t (g j) -> p t g j", g=NG),
                                     ohg[:].unsqueeze(3).broadcast_to([P, TT, NG, 4]), ALU.mult))
        link(nc.vector.tensor_reduce(es[:], pr[:].rearrange("p t g j -> p t j g"), axis=AX.X, op=ALU.add))
        pick(oh1, es[:], s1)
        link(nc.vector.scalar_tensor_tensor(out=es[:], in0=oh1[:], scalar=-3e38, in1=es[:], op0=ALU.mult, op1=ALU.add))
        pick(oh2, es[:], s2)
        nc.vector.tensor_tensor(s2[:], s2[:], s1[:], ALU.subtract).then_inc(r_exd, 1)
        for oh, m in ((oh1, M1), (oh2, M2)):
            link(nc.vector.tensor_tensor(m[:].rearrange("p t (g j) -> p t g j", g=NG),
                                         ohg[:].unsqueeze(3).broadcast_to([P, TT, NG, 4]),
                                         oh[:].unsqueeze(2).broadcast_to([P, TT, NG, 4]), ALU.mult))
        link(nc.vector.memset(M1[NS:P, TT - 1, :], 0.0))
        link(nc.vector.memset(M2[NS:P, TT - 1, :], 0.0))
        link(nc.vector.tensor_tensor(M[:], M1[:], M2[:], ALU.add))
        link(nc.vector.tensor_copy(Mb[:], M[:]))
        for t in range(TT):
            x = nc.vector.tensor_tensor(Mp[:, t + 1, :], Mp[:, t, :], Mb[:, t, :], ALU.add)
            if t < TT - 1:
                link(x)
        x.then_inc(r_m, 1)
        dve.wait_ge(r_ex, 2)
        link(nc.vector.tensor_reduce(gp[:], t4[:], axis=AX.X, op=ALU.add))
        link(nc.vector.tensor_scalar(s1[:], s2[:], 1.0, None, ALU.add))
        link(nc.vector.tensor_tensor(s1[:], s1[:], gp[:], ALU.mult))
        link(nc.vector.reciprocal(w1[:], s1[:]))
        link(nc.vector.tensor_tensor(w2[:], w1[:], s2[:], ALU.mult))
        for m, w in ((M1, w1), (M2, w2)):
            link(nc.vector.tensor_tensor(m[:], m[:], b(w[:], [P, TT, NE]), ALU.mult))
        rest = pr[:].rearrange("p t g j -> p (t g j)").rearrange("p (e t) -> p e t", e=NE)
        link(nc.vector.tensor_tensor(rest, M1[:].rearrange("p t e -> p e t"), M2[:].rearrange("p t e -> p e t"), ALU.add))
        for part in (2, 3, 4):
            link(nc.vector.tensor_copy(table[:, :, :, part], rest))
            if part < 4:
                link(nc.vector.tensor_tensor(rest, rest, table[:, :, :, part], ALU.subtract))
        dve.wait_ge(r_rk, 1)
        link(nc.vector.tensor_copy(rank.rearrange("p t e -> p (t e)"), bank[7][:, 0:TT * NE]))
        link(nc.vector.scalar_tensor_tensor(out=rank, in0=rank, scalar=1.0, in1=M[:], op0=ALU.add, op1=ALU.mult))
        link(nc.vector.tensor_scalar(rank_m[:].rearrange("p (e t) -> p t e", e=NE), rank, -1.0, None, ALU.add))
        link(nc.vector.tensor_reduce(mxc[:, 0:1], bank[6][:, 0:NE], axis=AX.X, op=ALU.max))
        link(nc.vector.tensor_scalar(rlim[:, 0:ROUNDS], rlim[:, 0:ROUNDS], mxc[:, 0:1], float(NE), ALU.is_lt, ALU.mult))
        link(nc.vector.tensor_reduce(mxc[:, 1:2], rlim[:, 0:ROUNDS], axis=AX.X, op=ALU.add))
        link(nc.vector.tensor_copy(steps[0:1, 0:1], mxc[0:1, 1:2]))

    block.close()
    c2.close()


def expert_unit(A, ring, wdn, u, e):
    if u < 4:
        w = (A["w_gate"], A["w_up"])[u % 2].rearrange("l e (k p) n -> (l e) p k n", p=P)
        return ring[:, u, :, :], w[e, :, :, (u // 2) * 256:(u // 2 + 1) * 256]
    w = A["w_down"].rearrange("l e (k p) n -> (l e) p k n", p=P)
    return wdn[:, u - 4, :].rearrange("p (k n) -> p k n", k=4), w[e, :, :, (u - 4) * 512:(u - 3) * 512]


def b3_all(nc, A, sb, sem, e_w, ring, wdn, bank, ident, h2_dram, sums_dram, rank_m, table, iota_w, steps):
    c3 = ExitStack()
    xg = sb("xg", [P, D], ctx=c3)
    xg2 = sb("xg2", [P, 2, P], ctx=c3)
    chunk = sb("chunk", [P, 2], ctx=c3)
    xT = sb("xT", [P, KC, W], ctx=c3)
    oh = sb("oh", [P, TT, 2 * P], BF16, ctx=c3)
    idx = sb("idx", [P, 3], I32, ctx=c3)
    far = sb("far", [P, 2], ctx=c3)
    facts = sb("facts", [P, TT, PARTS], BF16, ctx=c3)
    tok = sb("tok", [P, 2], ctx=c3)
    to = sb("to", [P, 2], ctx=c3)
    dest = sb("dest", [P, 3], I32, ctx=c3)
    dest_now = sb("dest_now", [P, 3], I32, ctx=c3)
    weight = sb("weight", [P, 2], ctx=c3)
    weight_now = sb("weight_now", [P, 2], ctx=c3)
    sg = sb("sg", [P, 2, W], ctx=c3)
    hold_at = sb("hold_at", [P, 1], ctx=c3)
    hid = sb("hid", [P, 4, W], ctx=c3)
    yT = sb("yT", [P, KC, P], ctx=c3)
    yT2 = sb("yT2", [P, KC, W2], ctx=c3)
    yr = sb("yr", [P, D], ctx=c3)
    yr2 = sb("yr2", [P, 2, P], ctx=c3)

    e_oh, e_ix, e_idx = sem("e_oh"), sem("e_ix"), sem("e_idx")
    e_free = sem("e_free")
    e_far, e_now = sem("e_far"), sem("e_now")
    e_hold = sem("e_hold")
    e_rk = sem("e_rk")
    e_chunk = sem("e_chunk")
    e_xg, e_xt, e_xe = sem("e_xg"), sem("e_xt"), sem("e_xe")
    e_gu, e_si, e_h = sem("e_gu"), sem("e_si"), sem("e_h")
    e_yt, e_ya, e_yd = sem("e_yt"), sem("e_ya"), sem("e_yd")
    e_yr, e_re, e_out = sem("e_yr"), sem("e_re"), sem("e_out")
    block = ExitStack()
    blk = block.enter_context(nc.Block())

    def count(eng):
        return eng.value_load(steps[0:1, 0:1], min_val=NE, max_val=NE * ROUNDS)

    @blk.sync
    def _(sp):
        n = count(sp)
        with sp.Fori(0, n - 1) as i:
            e = (i + 1) % NE
            for u in range(6):
                sp.wait_ge(e_gu if u < 4 else e_yt, i * 4 + (2 if u in (0, 1, 4) else 4))
                dst, src = expert_unit(A, ring, wdn, u, bass.ds(e, 1))
                sp.dma_start(dst, src.rearrange("o p k n -> p (o k) n")).then_inc(e_w[u], 16)

    @blk.gpsimd
    def _(pool):
        h2_parts = h2_dram.rearrange("t (c d) -> (t c) d", d=P)
        sums_parts = sums_dram.rearrange("t (c d) -> (t c) d", d=P)

        def gather():
            for j, (dst, src) in enumerate(((xg[:], h2_dram), (xg2[:, 0, :], h2_parts), (xg2[:, 1, :], h2_parts))):
                nc.gpsimd.indirect_dma_start(out=dst, out_offset=None, in_=src,
                                             in_offset=bass.IndirectOffsetOnAxis(ap=idx[:, j:j + 1], axis=0)
                                             ).then_inc(e_xg, 16)

        def scatter():
            for j, (src, dst, rows) in enumerate(((yr[:], sums_dram, N), (yr2[:, 0, :], sums_parts, N * KC),
                                                  (yr2[:, 1, :], sums_parts, N * KC))):
                nc.gpsimd.indirect_dma_start(out=dst, in_=src, in_offset=None, bounds_check=rows - 1,
                                             out_offset=bass.IndirectOffsetOnAxis(ap=dest_now[:, j:j + 1], axis=0),
                                             oob_is_err=False, compute_op=ALU.add).then_inc(e_out, 16)

        def hold():
            nc.gpsimd.tensor_tensor(hold_at[:], ident[:, 0:1], ident[:, 1:2], ALU.add).then_inc(e_hold, 1)

        n = count(pool)
        pool.sem_inc(e_free, 1)
        pool.sem_inc(e_hold, 1)
        for h in range(2):
            for k in range(4):
                nc.gpsimd.memset(chunk[k * W2:(k + 1) * W2, h:h + 1], float(4 * h + k)).then_inc(e_chunk, 1)
        pool.wait_ge(e_idx, 1)
        gather()
        with pool.Fori(0, n) as i:
            pool.wait_ge(e_hold, i * 2 + 1)
            pool.wait_ge(e_idx, i + 2)
            pool.wait_ge(e_xt, i * 3 + 3)
            hold()
            gather()
            pool.wait_ge(e_hold, i * 2 + 2)
            pool.wait_ge(e_re, i * 4 + 5)
            hold()
            scatter()
            pool.wait_ge(e_out, i * 48 + 48)
            pool.sem_inc(e_free, 1)
        pool.wait_ge(e_xg, n * 48 + 48)

    @blk.tensor
    def _(pe):
        def indices():
            for c in range(2):
                for t in range(TT):
                    x = nc.tensor.matmul(bank[7][:, PARTS * c:PARTS * (c + 1)], oh[:, t, c * P:(c + 1) * P],
                                         facts[:, t, :], start=t == 0, stop=t == TT - 1)
            x.then_inc(e_ix, 1)

        def rows_in():
            for h in range(2):
                for k in range(4):
                    x = nc.tensor.transpose(bank[4 + h][:, k * P:(k + 1) * P],
                                            xg[:, (4 * h + k) * P:(4 * h + k + 1) * P], ident[:])
                x.then_inc(e_xt, 1)
            for h in range(2):
                x = nc.tensor.transpose(bank[6][:, h * P:(h + 1) * P], xg2[:, h, :], ident[:])
            x.then_inc(e_xt, 1)

        def gate_up(f):
            c0 = (f % 2) * P
            for side in range(2):
                u = 2 * (f // 2) + side
                for k in range(KC):
                    x = nc.tensor.matmul(bank[f % 2][:, side * 256:side * 256 + W],
                                         ring[:, u, k, c0:c0 + P], xT[:, k, :],
                                         start=k == 0, stop=k == KC - 1)
            x.then_inc(e_gu, 1)

        def down(j, i):
            for q in range(2):
                d = 2 * j + q
                for k in range(4):
                    if j == 0 and q == 0 and k >= 2:
                        pe.wait_ge(e_h, i * 4 + k + 2)
                    x = nc.tensor.matmul(bank[2 + j % 2][:, q * 256:q * 256 + W],
                                         wdn[:, d // 4, k * 512 + (d % 4) * P:k * 512 + (d % 4 + 1) * P],
                                         hid[:, k, :], start=k == 0, stop=k == 3)
            x.then_inc(e_yt, 1)

        def rows_back(h):
            for k in range(4):
                x = nc.tensor.transpose(bank[4 + h][:, k * P:(k + 1) * P], yT[:, 4 * h + k, :], ident[:])
            x.then_inc(e_yr, 1)
            nc.tensor.transpose(bank[6][:, h * P:(h + 1) * P], yT2[:, 4 * h:4 * h + 4, :], ident[:]).then_inc(e_yr, 1)

        n = count(pe)
        pe.wait_ge(e_oh, 1)
        indices()
        pe.wait_ge(e_oh, 2)
        pe.wait_ge(e_idx, 1)
        indices()
        pe.wait_ge(e_xg, 48)
        rows_in()
        with pe.Fori(0, n) as i:
            pe.wait_ge(e_xe, i * 3 + 3)
            for f in range(4):
                pe.wait_ge(e_h, i * 4 + (1 if f < 2 else f))
                if f % 2 == 0:
                    pe.wait_ge(e_w[f], i * 16 + 16)
                    pe.wait_ge(e_w[f + 1], i * 16 + 16)
                gate_up(f)
            for j in range(4):
                pe.wait_ge(e_ya if j % 2 == 0 else e_yd, i * 2 + j // 2 + 1)
                if j % 2 == 0:
                    pe.wait_ge(e_w[4 + j // 2], i * 16 + 16)
                down(j, i)
                if j == 1:
                    pe.wait_ge(e_xg, i * 48 + 96)
                    pe.wait_ge(e_re, i * 4 + 1)
                    rows_in()
                elif j == 2:
                    pe.wait_ge(e_xe, i * 3 + 6)
                    pe.wait_ge(e_ya, i * 2 + 2)
                    pe.wait_ge(e_yd, i * 2 + 2)
                    rows_back(0)
            pe.wait_ge(e_oh, i + 3)
            pe.wait_ge(e_idx, i + 2)
            indices()
            pe.wait_ge(e_ya, i * 2 + 3)
            pe.wait_ge(e_yd, i * 2 + 3)
            pe.wait_ge(e_re, i * 4 + 3)
            rows_back(1)

    @blk.scalar
    def _(act):
        n = count(act)
        act.sem_inc(e_ya, 1)
        act.sem_inc(e_re, 1)
        with act.Fori(0, n) as i:
            for f in range(4):
                act.wait_ge(e_gu, i * 4 + f + 1)
                nc.scalar.activation(sg[:, f % 2, :], bank[f % 2][:, 0:W], ACT.Silu).then_inc(e_si, 1)
            for j in (0, 2):
                act.wait_ge(e_yt, i * 4 + j + 1)
                y = bank[2][:, :].rearrange("p (q t) -> p q t", q=2)
                nc.scalar.copy(yT[:, 2 * j:2 * j + 2, :], y[:, :, 0:P])
                nc.scalar.copy(yT2[:, 2 * j:2 * j + 2, :], y[:, :, P:W]).then_inc(e_ya, 1)
            act.wait_ge(e_free, i + 1)
            act.wait_ge(e_now, i * 2 + 2)
            for h in range(2):
                for c in range(2):
                    act.wait_ge(e_yr, i * 4 + 2 * h + c + 1)
                    if c == 0:
                        dst, src = yr[:, h * 512:(h + 1) * 512], bank[4 + h][:, :]
                    else:
                        dst, src = yr2[:, h, :], bank[6][:, h * P:(h + 1) * P]
                    nc.scalar.activation(dst, src, ACT.Copy, scale=weight_now[:, c:c + 1]).then_inc(e_re, 1)

    @blk.vector
    def _(dve):
        def onehot(e):
            nc.vector.tensor_copy(facts[:], table[:, bass.ds(e, 1), :, :].rearrange("p o t f -> p (o t) f"))
            nc.vector.tensor_tensor(oh[:], iota_w[:].unsqueeze(1).broadcast_to([P, TT, 2 * P]),
                                    rank_m[:, bass.ds(e * TT, TT)].unsqueeze(2).broadcast_to([P, TT, 2 * P]),
                                    ALU.is_equal).then_inc(e_oh, 1)

        def lower(e):
            nc.vector.tensor_scalar(rank_m[:, bass.ds(e * TT, TT)], rank_m[:, bass.ds(e * TT, TT)], float(-W), None,
                                    ALU.add).then_inc(e_rk, 1)

        def indices(s):
            sums = bank[7][:, 0:2 * PARTS].rearrange("p (c f) -> p c f", c=2)
            nc.vector.tensor_scalar(far[:], sums[:, :, 0], 0.0, float(4 * N), ALU.is_equal, ALU.mult)
            nc.vector.tensor_reduce(weight[:], sums[:, :, 2:], axis=AX.X, op=ALU.add)
            nc.vector.tensor_scalar(tok[:], sums[:, :, 0], float(P), None, ALU.mult).then_inc(e_far, 1)
            dve.wait_ge(e_far, s * 3 + 1)
            nc.vector.tensor_tensor(tok[:], tok[:], sums[:, :, 1], ALU.add).then_inc(e_far, 1)
            dve.wait_ge(e_far, s * 3 + 2)
            nc.vector.scalar_tensor_tensor(out=to[:], in0=tok[:], scalar=float(-P), in1=far[:], op0=ALU.add,
                                           op1=ALU.add)
            nc.vector.tensor_scalar(tok[:], tok[:], float(-P), 0.0, ALU.add, ALU.max).then_inc(e_far, 1)
            dve.wait_ge(e_far, s * 3 + 3)
            for where, out in ((to, dest), (tok, idx)):
                nc.vector.tensor_copy(out[:, 0:1], where[:, 0:1])
                x = nc.vector.scalar_tensor_tensor(out=out[:, 1:3], in0=where[:, 1:2].broadcast_to([P, 2]),
                                                   scalar=float(KC), in1=chunk[:], op0=ALU.mult, op1=ALU.add)
            x.then_inc(e_idx, 1)

        n = count(dve)
        dve.sem_inc(e_h, 1)
        dve.sem_inc(e_yd, 1)
        nc.vector.memset(bank[7][:, 0:2 * PARTS], 0.0)
        onehot(0)
        dve.wait_ge(e_oh, 1)
        lower(0)
        dve.wait_ge(e_ix, 1)
        dve.wait_ge(e_chunk, 8)
        indices(0)
        onehot(1)
        dve.wait_ge(e_oh, 2)
        lower(1)

        def x_out(base):
            for h in range(2):
                dve.wait_ge(e_xt, base + h + 1)
                nc.vector.tensor_copy(xT[:, 4 * h:4 * h + 4, 0:P],
                                      bank[4 + h][:, :].rearrange("p (k t) -> p k t", t=P)).then_inc(e_xe, 1)
            dve.wait_ge(e_xt, base + 3)
            nc.vector.tensor_copy(xT[:, :, P:W],
                                  bank[6][:, 0:KC * W2].rearrange("p (k t) -> p k t", t=W2)).then_inc(e_xe, 1)

        x_out(0)
        with dve.Fori(0, n) as i:
            dve.wait_ge(e_ix, i + 2)
            dve.wait_ge(e_rk, i + 2)
            onehot((i + 2) % NE)
            for f in range(4):
                dve.wait_ge(e_si, i * 4 + f + 1)
                nc.vector.tensor_tensor(hid[:, f, :], sg[:, f % 2, :], bank[f % 2][:, 256:256 + W],
                                        ALU.mult).then_inc(e_h, 1)
                if f == 0:
                    dve.wait_ge(e_xg, i * 48 + 48)
                    dve.wait_ge(e_free, i + 1)
                    dve.wait_ge(e_idx, i + 1)
                    nc.vector.tensor_copy(dest_now[:], dest[:]).then_inc(e_now, 1)
                    nc.vector.tensor_copy(weight_now[:], weight[:]).then_inc(e_now, 1)
                    dve.wait_ge(e_now, i * 2 + 2)
                    indices(i + 1)
                    dve.wait_ge(e_oh, i + 3)
                    lower((i + 2) % NE)
            for j in (1, 3):
                dve.wait_ge(e_yt, i * 4 + j + 1)
                y = bank[3][:, :].rearrange("p (q t) -> p q t", q=2)
                nc.vector.tensor_copy(yT[:, 2 * j:2 * j + 2, :], y[:, :, 0:P])
                nc.vector.tensor_copy(yT2[:, 2 * j:2 * j + 2, :], y[:, :, P:W]).then_inc(e_yd, 1)
                if j == 1:
                    x_out(i * 3 + 3)

    block.close()
    c3.close()


def b4_all(nc, A, O, sb, sem, eps_c, x2, sums_dram):
    c4 = ExitStack()
    B = 4
    ot = sb("ot", [P, B, D], ctx=c4)
    squares = sb("squares", [P, D], ctx=c4)
    gfb = sb("gfb", [P, D], ctx=c4)
    ssq = sb("ssq4", [P, TT], ctx=c4)
    root = sb("root4", [P, TT], ctx=c4)
    rstd = sb("rstd4", [P, TT], ctx=c4)
    f_g = sem("f_g")
    f_x = [sem(f"f_x{i}") for i in range(TT)]
    f_ssq, f_root, f_r, f_o = [sem(x) for x in ("f_ssq", "f_root", "f_r", "f_o")]
    f_out = [sem(f"f_out{j}") for j in range(B)]
    block = ExitStack()
    blk = block.enter_context(nc.Block())

    @blk.sync
    def _(sp):
        for i in range(TT):
            sp.dma_start(x2[0:ROWS[i], i, :], sums_dram[i * P:i * P + ROWS[i], :]).then_inc(f_x[i], 16)
            if i == 0:
                sp.dma_start(gfb[:], A["final_g"].rearrange("(o d) -> o d", o=1).broadcast_to([P, D])).then_inc(f_g, 16)
        for i in range(TT):
            sp.wait_ge(f_o, i + 1)
            dst = O[0][0, i * P:(i + 1) * P, :] if i < TT - 1 else O[1].rearrange("a t d -> (a t) d")
            sp.dma_start(dst, ot[0:ROWS[i], i % B, :]).then_inc(f_out[i % B], 16)
        for j in range(B):
            sp.wait_ge(f_out[j], 16 * len(range(j, TT, B)))

    @blk.vector
    def _(dve):
        dve.wait_ge(f_g, 16)
        for i in range(TT):
            r = ROWS[i]
            dve.wait_ge(f_root, i + 1)
            nc.vector.reciprocal(rstd[0:r, i:i + 1], root[0:r, i:i + 1]).then_inc(f_r, 1)
            dve.wait_ge(f_r, i + 1)
            if i >= B:
                dve.wait_ge(f_out[i % B], 16 * (i // B))
            nc.vector.scalar_tensor_tensor(out=ot[0:r, i % B, :], in0=x2[0:r, i, :], scalar=rstd[0:r, i:i + 1],
                                           in1=gfb[0:r, :], op0=ALU.mult, op1=ALU.mult).then_inc(f_o, 1)

    @blk.scalar
    def _(act):
        for i in range(TT):
            r = ROWS[i]
            act.wait_ge(f_x[i], 16)
            nc.scalar.activation(squares[0:r, :], x2[0:r, i, :], ACT.Square, scale=D ** -0.5,
                                 accum_out=ssq[0:r, i:i + 1]).then_inc(f_ssq, 1)
            act.wait_ge(f_ssq, i + 1)
            nc.scalar.activation(root[0:r, i:i + 1], ssq[0:r, i:i + 1], ACT.Sqrt,
                                 bias=eps_c[0:r, :]).then_inc(f_root, 1)

    block.close()
    c4.close()


_INS = ["x_prompt", "x_sample", "state_pool", "state_gla", "norm1_g", "w_in", "w_gk2", "b_gk", "w_pool", "pool_scale",
        "gla_norm_g", "w_out", "norm2_g", "w_router_group", "b_router_group", "w_router_expert", "b_router_expert",
        "w_gate", "w_up", "w_down", "final_g"]
_OUTS = [(1, SEQ, D), (DEC_B, DEC_T, D), (1, 1, HIST, PW), (1, 1, HEADS, DK, DV), (1, DEC_B, HIST, PW),
         (1, DEC_B, HEADS, DK, DV)]


def kernel(**inputs):
    import numpy as _np
    import concourse.bacc as _bacc
    from concourse import mybir as _mybir
    from concourse.bass_utils import run_bass_kernel_spmd as _run

    nc = _bacc.Bacc("TRN2", target_bir_lowering=False, num_devices=1)
    arrays, args = {}, {}
    for name in _INS:
        a = _np.ascontiguousarray(inputs[name])
        arrays[f"in_{name}"] = a
        args[name] = nc.dram_tensor(f"in_{name}", a.shape, _mybir.dt.from_np(a.dtype), kind="ExternalInput").ap()
    outs = [nc.dram_tensor(f"out_{i}", s, F32, kind="ExternalOutput").ap() for i, s in enumerate(_OUTS)]
    program(nc, args, outs)
    r = _run(nc, [arrays], core_ids=[0])
    return tuple(r.results[0][f"out_{i}"] for i in range(len(_OUTS)))
```
